# Optimizing a Trainium2 kernel written in Bass

```python
import jax, jax.numpy as jnp
from jax import lax
import numpy as np
import math

D_MODEL = 1024
BATCH = 1
SEQ = 256
DEPTH = 2

N_META = 16
DEEPNORM_ALPHA = (2 * DEPTH) ** 0.25
DEEPNORM_BETA = (8 * DEPTH) ** -0.25
LN_EPS = 1e-5
RG_WIDTH = 1344
RG_BLOCKS = 8
RG_BLOCK_W = RG_WIDTH // RG_BLOCKS
RG_CONV_W = 4
RG_C = 8.0
GLA_HEADS = 4
GLA_DK = D_MODEL // 2 // GLA_HEADS
GLA_DV = D_MODEL // GLA_HEADS
GLA_QK = GLA_HEADS * GLA_DK
GLA_VD = GLA_HEADS * GLA_DV
GLA_RANK = 16
GLA_TAU = 16.0
GLA_CHUNK = 64
GLA_PAD = (-N_META) % GLA_CHUNK
D_FF = 3584
N_EXPERTS = 8
TOP_K = 2
N_REC = (DEPTH + 1) // 2
N_GLA = DEPTH // 2


def _normalize(x):
    xf = x.astype(jnp.float32)
    mu = jnp.mean(xf, axis=-1, keepdims=True)
    xc = xf - mu
    var = jnp.mean(xc * xc, axis=-1, keepdims=True)
    return xc * lax.rsqrt(var + LN_EPS)

def layer_norm(x, g, b):
    return (_normalize(x) * g + b).astype(x.dtype)

def swiglu(h, w_in, w_out):
    gate, up = jnp.split(h @ w_in, 2, axis=-1)
    return (jax.nn.silu(gate) * up) @ w_out

def _linear_scan_combine(c1, c2):
    a1, b1 = c1
    a2, b2 = c2
    return a1 * a2, a2 * b1 + b2

def rglru_block(h, w_in, conv_w, conv_b, w_gates, b_gates, lam, w_out):
    Bsz, T, _ = h.shape
    proj = h @ w_in
    gate_branch, xr = jnp.split(proj, 2, axis=-1)
    xp = jnp.pad(xr, ((0, 0), (RG_CONV_W - 1, 0), (0, 0)))
    xc = conv_b
    for tap in range(RG_CONV_W):
        xc = xc + xp[:, tap:tap + T] * conv_w[tap]
    gates = jnp.einsum('btnc,gncd->gbtnd', xc.reshape(Bsz, T, RG_BLOCKS, RG_BLOCK_W), w_gates)
    gates = gates.reshape(2, Bsz, T, RG_WIDTH) + b_gates[:, None, None, :]
    gates = jax.nn.sigmoid(gates.astype(jnp.float32))
    r_t, i_t = gates[0], gates[1]
    log_a = -RG_C * r_t * jax.nn.softplus(-lam.astype(jnp.float32))
    a_t = jnp.exp(log_a)
    u_t = jnp.sqrt(-jnp.expm1(2.0 * log_a)) * (i_t * xc)
    _, hs = lax.associative_scan(_linear_scan_combine, (a_t, u_t), axis=1)
    y = hs * jax.nn.gelu(gate_branch.astype(jnp.float32))
    return (y @ w_out).astype(h.dtype)

def gla_block(h, w_in, w_gate_up, b_gate, norm_g, w_out):
    Bsz, T, _ = h.shape
    proj = h @ w_in
    q, k, v, r, z = jnp.split(
        proj, [GLA_QK, 2 * GLA_QK, 2 * GLA_QK + GLA_VD, 2 * GLA_QK + 2 * GLA_VD], axis=-1)
    log_g = jax.nn.log_sigmoid((z @ w_gate_up + b_gate).astype(jnp.float32)) / GLA_TAU
    L = T + GLA_PAD
    nc = L // GLA_CHUNK

    def to_chunks(t, d):
        t = jnp.pad(t, ((0, 0), (GLA_PAD, 0), (0, 0)))
        return t.reshape(Bsz, nc, GLA_CHUNK, GLA_HEADS, d).transpose(0, 3, 1, 2, 4)

    qc = to_chunks(q, GLA_DK) * (GLA_DK ** -0.5)
    kc = to_chunks(k, GLA_DK)
    vc = to_chunks(v, GLA_DV)
    gc = to_chunks(log_g, GLA_DK)
    b = jnp.cumsum(gc, axis=3)
    b_mid = b[:, :, :, GLA_CHUNK // 2 - 1:GLA_CHUNK // 2]
    b_last = b[:, :, :, -1:]
    scores = jnp.einsum('bhncd,bhnsd->bhncs', qc * jnp.exp(b - b_mid), kc * jnp.exp(b_mid - b))
    causal = jnp.tril(jnp.ones((GLA_CHUNK, GLA_CHUNK), dtype=bool))
    scores = jnp.where(causal, scores, 0.0)
    o_intra = jnp.einsum('bhncs,bhnse->bhnce', scores, vc)
    q_in = qc * jnp.exp(b)
    k_out = kc * jnp.exp(b_last - b)
    decay = jnp.exp(b_last[:, :, :, 0])

    def step(S, xs):
        qn, kn, vn, dn = xs
        o = jnp.einsum('bhcd,bhde->bhce', qn, S)
        S = dn[..., None] * S + jnp.einsum('bhcd,bhce->bhde', kn, vn)
        return S, o

    S0 = jnp.zeros((Bsz, GLA_HEADS, GLA_DK, GLA_DV), jnp.float32)
    xs = (jnp.moveaxis(q_in, 2, 0), jnp.moveaxis(k_out, 2, 0),
          jnp.moveaxis(vc, 2, 0), jnp.moveaxis(decay, 2, 0))
    _, o_inter = lax.scan(step, S0, xs)
    o = o_intra + jnp.moveaxis(o_inter, 0, 2)
    o = o.transpose(0, 2, 3, 1, 4).reshape(Bsz, L, GLA_HEADS, GLA_DV)[:, GLA_PAD:]
    o = _normalize(o) * norm_g
    o = o.reshape(Bsz, T, GLA_VD) * jax.nn.silu(r.astype(jnp.float32))
    return (o @ w_out).astype(h.dtype)

def moe_swiglu(h, router, w_in, w_out):
    Bsz, T, D = h.shape
    hf = h.reshape(Bsz * T, D)
    logits = (hf @ router).astype(jnp.float32)
    top_logit, top_idx = lax.top_k(logits, TOP_K)
    top_w = jax.nn.softmax(top_logit, axis=-1)
    gates = jnp.einsum('nk,nke->ne', top_w, jax.nn.one_hot(top_idx, N_EXPERTS, dtype=jnp.float32))
    y = jnp.zeros((Bsz * T, D), jnp.float32)
    for e in range(N_EXPERTS):
        y = y + gates[:, e:e + 1] * swiglu(hf, w_in[e], w_out[e])
    return y.reshape(Bsz, T, D).astype(h.dtype)

def first_inputs(seed: int = 0) -> dict:
    key = jax.random.key(seed)
    ks = jax.random.split(key, 24)
    f32 = jnp.float32

    def nrm(k, shape, fan_in, scale=1.0):
        return jax.random.normal(k, shape, f32) * (scale * fan_in ** -0.5)

    x = jax.random.normal(ks[0], (BATCH, SEQ, D_MODEL), f32)
    meta_tokens = jax.random.normal(ks[1], (N_META, D_MODEL), f32)
    ln_gain = 1.0 + 0.02 * jax.random.normal(ks[2], (DEPTH, 2, D_MODEL), f32)
    ln_bias = 0.02 * jax.random.normal(ks[3], (DEPTH, 2, D_MODEL), f32)
    rg_w_in = nrm(ks[4], (N_REC, D_MODEL, 2 * RG_WIDTH), D_MODEL)
    rg_conv_w = nrm(ks[5], (N_REC, RG_CONV_W, RG_WIDTH), RG_CONV_W)
    rg_conv_b = 0.02 * jax.random.normal(ks[6], (N_REC, RG_WIDTH), f32)
    rg_w_gates = nrm(ks[7], (N_REC, 2, RG_BLOCKS, RG_BLOCK_W, RG_BLOCK_W), RG_BLOCK_W)
    rg_b_gates = 0.02 * jax.random.normal(ks[8], (N_REC, 2, RG_WIDTH), f32)
    a_pow_c = jax.random.uniform(ks[9], (N_REC, RG_WIDTH), f32, minval=0.9, maxval=0.999)
    a_base = a_pow_c ** (1.0 / RG_C)
    rg_lambda = jnp.log(a_base) - jnp.log1p(-a_base)
    rg_w_out = nrm(ks[10], (N_REC, RG_WIDTH, D_MODEL), RG_WIDTH, DEEPNORM_BETA)
    gla_w_in = nrm(ks[11], (N_GLA, D_MODEL, 2 * GLA_QK + 2 * GLA_VD + GLA_RANK), D_MODEL)
    gla_w_gate_up = nrm(ks[12], (N_GLA, GLA_RANK, GLA_QK), GLA_RANK)
    gla_b_gate = 2.0 + 0.1 * jax.random.normal(ks[13], (N_GLA, GLA_QK), f32)
    gla_norm_g = 1.0 + 0.02 * jax.random.normal(ks[14], (N_GLA, GLA_HEADS, GLA_DV), f32)
    gla_w_out = nrm(ks[15], (N_GLA, GLA_VD, D_MODEL), GLA_VD, DEEPNORM_BETA)
    ffn_w_in = nrm(ks[16], (N_REC, D_MODEL, 2 * D_FF), D_MODEL)
    ffn_w_out = nrm(ks[17], (N_REC, D_FF, D_MODEL), D_FF, DEEPNORM_BETA)
    moe_router = nrm(ks[18], (N_GLA, D_MODEL, N_EXPERTS), D_MODEL)
    moe_w_in = nrm(ks[19], (N_GLA, N_EXPERTS, D_MODEL, 2 * D_FF), D_MODEL)
    moe_w_out = nrm(ks[20], (N_GLA, N_EXPERTS, D_FF, D_MODEL), D_FF, DEEPNORM_BETA)
    return {
        "x": x, "meta_tokens": meta_tokens, "ln_gain": ln_gain, "ln_bias": ln_bias,
        "rg_w_in": rg_w_in, "rg_conv_w": rg_conv_w, "rg_conv_b": rg_conv_b,
        "rg_w_gates": rg_w_gates, "rg_b_gates": rg_b_gates, "rg_lambda": rg_lambda,
        "rg_w_out": rg_w_out,
        "gla_w_in": gla_w_in, "gla_w_gate_up": gla_w_gate_up, "gla_b_gate": gla_b_gate,
        "gla_norm_g": gla_norm_g, "gla_w_out": gla_w_out,
        "ffn_w_in": ffn_w_in, "ffn_w_out": ffn_w_out,
        "moe_router": moe_router, "moe_w_in": moe_w_in, "moe_w_out": moe_w_out,
    }

def first_block(x, meta_tokens, ln_gain, ln_bias,
              rg_w_in, rg_conv_w, rg_conv_b, rg_w_gates, rg_b_gates, rg_lambda, rg_w_out,
              gla_w_in, gla_w_gate_up, gla_b_gate, gla_norm_g, gla_w_out,
              ffn_w_in, ffn_w_out, moe_router, moe_w_in, moe_w_out):
    Bsz = x.shape[0]
    meta = jnp.broadcast_to(meta_tokens.astype(x.dtype)[None], (Bsz, N_META, D_MODEL))
    h = jnp.concatenate([meta, x], axis=1)
    for i in range(DEPTH):
        j = i // 2
        if i % 2 == 0:
            mix = rglru_block(h, rg_w_in[j], rg_conv_w[j], rg_conv_b[j], rg_w_gates[j],
                              rg_b_gates[j], rg_lambda[j], rg_w_out[j])
        else:
            mix = gla_block(h, gla_w_in[j], gla_w_gate_up[j], gla_b_gate[j],
                            gla_norm_g[j], gla_w_out[j])
        h = layer_norm(DEEPNORM_ALPHA * h + mix, ln_gain[i, 0], ln_bias[i, 0])
        if i % 2 == 0:
            ff = swiglu(h, ffn_w_in[j], ffn_w_out[j]).astype(h.dtype)
        else:
            ff = moe_swiglu(h, moe_router[j], moe_w_in[j], moe_w_out[j])
        h = layer_norm(DEEPNORM_ALPHA * h + ff, ln_gain[i, 1], ln_bias[i, 1])
    return h[:, N_META:]


DEPTH_2 = 1

CHUNK = 64
Q_BLOCK = 128
EPS = 1e-6
MLA_HEADS = 8
MLA_NOPE = 64
MLA_ROPE = 32
MLA_QK = MLA_NOPE + MLA_ROPE
MLA_V = 64
MLA_Q_LORA = 384
MLA_KV_LORA = 256
ROPE_THETA = 10000.0
DIFF_HEADS = 4
DIFF_HEAD_DIM = 64
DIFF_V = 2 * DIFF_HEAD_DIM
REL_BUCKETS = 32
REL_MAX_DIST = 128
MIX_WIDTH = MLA_HEADS * MLA_V + DIFF_HEADS * DIFF_V
IN_WIDTHS = (MLA_Q_LORA, MLA_KV_LORA, MLA_ROPE,
             DIFF_HEADS * 2 * DIFF_HEAD_DIM, DIFF_HEADS * 2 * DIFF_HEAD_DIM, DIFF_HEADS * DIFF_V)
IN_WIDTH = sum(IN_WIDTHS)
IN_SPLITS = np.cumsum(IN_WIDTHS)[:-1].tolist()
N_GROUPS = 4
EXPERTS_PER_GROUP = 4
N_EXPERTS_2 = N_GROUPS * EXPERTS_PER_GROUP
D_EXPERT = 512


def _rms(x, g):
    xf = x.astype(jnp.float32)
    y = xf * lax.rsqrt(jnp.mean(xf * xf, axis=-1, keepdims=True) + EPS)
    return (y * g.astype(jnp.float32)).astype(x.dtype)

def _to_blocks(a):
    b, s = a.shape[0], a.shape[1]
    return jnp.moveaxis(a.reshape(b, s // Q_BLOCK, Q_BLOCK, *a.shape[2:]), 1, 0)

def _from_blocks(a):
    a = jnp.moveaxis(a, 0, 1)
    return a.reshape(a.shape[0], a.shape[1] * a.shape[2], *a.shape[3:])

def _rope(x, cos, sin):
    x1, x2 = jnp.split(x, 2, axis=-1)
    return jnp.concatenate([x1 * cos - x2 * sin, x2 * cos + x1 * sin], axis=-1)

def _rel_bucket(rel):
    nb = REL_BUCKETS // 2
    max_exact = nb // 2
    n = jnp.abs(rel)
    large = max_exact + (jnp.log(jnp.maximum(n, 1).astype(jnp.float32) / max_exact)
                         / math.log(REL_MAX_DIST / max_exact) * (nb - max_exact)).astype(jnp.int32)
    large = jnp.minimum(large, nb - 1)
    return jnp.where(rel > 0, nb, 0) + jnp.where(n < max_exact, n, large)

def _mla(c_q, c_kv, k_pe, positions, cq_g, w_uq, ckv_g, w_ukv, q_g, k_g):
    B, S, _ = c_q.shape
    q = (_rms(c_q, cq_g) @ w_uq).reshape(B, S, MLA_HEADS, MLA_QK)
    kv = (_rms(c_kv, ckv_g) @ w_ukv).reshape(B, S, MLA_HEADS, MLA_NOPE + MLA_V)
    k_nope, v = kv[..., :MLA_NOPE], kv[..., MLA_NOPE:]
    k = jnp.concatenate([k_nope, jnp.broadcast_to(k_pe[:, :, None, :], (B, S, MLA_HEADS, MLA_ROPE))], axis=-1)
    q, k = _rms(q, q_g), _rms(k, k_g)
    inv_freq = ROPE_THETA ** (-jnp.arange(0, MLA_ROPE // 2, dtype=jnp.float32) / (MLA_ROPE // 2))
    ang = positions.astype(jnp.float32)[..., None] * inv_freq
    cos = jnp.cos(ang)[:, :, None, :].astype(q.dtype)
    sin = jnp.sin(ang)[:, :, None, :].astype(q.dtype)
    q = jnp.concatenate([q[..., :MLA_NOPE], _rope(q[..., MLA_NOPE:], cos, sin)], axis=-1)
    k = jnp.concatenate([k[..., :MLA_NOPE], _rope(k[..., MLA_NOPE:], cos, sin)], axis=-1)
    scale = MLA_QK ** -0.5
    key_chunk = jnp.arange(S) // CHUNK
    q_chunks = key_chunk.reshape(S // Q_BLOCK, Q_BLOCK)

    def block(args):
        qb, qc = args
        s = jnp.einsum('bqhd,bkhd->bhqk', qb, k).astype(jnp.float32) * scale
        s = jnp.where(key_chunk[None, :] <= qc[:, None], s, -jnp.inf)
        p = jax.nn.softmax(s, axis=-1).astype(v.dtype)
        return jnp.einsum('bhqk,bkhe->bqhe', p, v)

    o = _from_blocks(lax.map(block, (_to_blocks(q), q_chunks)))
    return o.reshape(B, S, MLA_HEADS * MLA_V)

def _diff_attn(dq, dk, dv, positions, rel_bias, q_g, k_g, lq1, lk1, lq2, lk2, subln_g, lambda_init):
    B, S, _ = dq.shape
    q = _rms(dq.reshape(B, S, DIFF_HEADS, 2, DIFF_HEAD_DIM), q_g)
    k = _rms(dk.reshape(B, S, DIFF_HEADS, 2, DIFF_HEAD_DIM), k_g)
    v = dv.reshape(B, S, DIFF_HEADS, DIFF_V)
    lam = (jnp.exp(jnp.sum(lq1.astype(jnp.float32) * lk1.astype(jnp.float32)))
           - jnp.exp(jnp.sum(lq2.astype(jnp.float32) * lk2.astype(jnp.float32))) + lambda_init)
    scale = DIFF_HEAD_DIM ** -0.5
    key_chunk = jnp.arange(S) // CHUNK
    q_chunks = key_chunk.reshape(S // Q_BLOCK, Q_BLOCK)

    def block(args):
        qb, qpos, qc = args
        s = jnp.einsum('bqhmd,bkhmd->bhmqk', qb, k).astype(jnp.float32) * scale
        bucket = _rel_bucket(positions[:, None, :] - qpos[:, :, None])
        bias = jnp.moveaxis(rel_bias[bucket], -1, 1).astype(jnp.float32)
        s = jnp.where(key_chunk[None, :] <= qc[:, None], s + bias[:, :, None], -jnp.inf)
        p = jax.nn.softmax(s, axis=-1)
        a = (p[:, :, 0] - lam * p[:, :, 1]).astype(v.dtype)
        return jnp.einsum('bhqk,bkhe->bqhe', a, v)

    o = _from_blocks(lax.map(block, (_to_blocks(q), _to_blocks(positions), q_chunks)))
    o = _rms(o, subln_g) * (1.0 - lambda_init)
    return o.reshape(B, S, DIFF_HEADS * DIFF_V)

def _hmoe(h, w_rg, b_rg, w_re, b_re, w_gate, w_up, w_down):
    B, S, D = h.shape
    t = h.reshape(B * S, D)
    g_logits = (t @ w_rg + b_rg).astype(jnp.float32)
    g_idx = jnp.argmax(g_logits, axis=-1)
    g_w = jnp.take_along_axis(jax.nn.softmax(g_logits, axis=-1), g_idx[:, None], axis=-1)
    e_logits = (t @ w_re + b_re).astype(jnp.float32).reshape(-1, N_GROUPS, EXPERTS_PER_GROUP)
    e_sel = jnp.take_along_axis(e_logits, g_idx[:, None, None], axis=1)[:, 0]
    top_v, top_i = lax.top_k(e_sel, TOP_K)
    top_w = jax.nn.softmax(top_v, axis=-1) * g_w
    gate_in = jnp.sum(jax.nn.one_hot(top_i, EXPERTS_PER_GROUP, dtype=jnp.float32) * top_w[..., None], axis=1)
    gate = (jax.nn.one_hot(g_idx, N_GROUPS, dtype=jnp.float32)[:, :, None]
            * gate_in[:, None, :]).reshape(-1, N_EXPERTS_2).astype(h.dtype)
    y = jnp.zeros_like(t)
    for e in range(N_EXPERTS_2):
        he = jax.nn.silu(t @ w_gate[e]) * (t @ w_up[e])
        y = y + gate[:, e:e + 1] * (he @ w_down[e])
    return y.reshape(B, S, D)

def second_inputs(seed: int = 0) -> dict:
    key = jax.random.key(seed)
    ks = jax.random.split(key, 40)
    D, L, f32 = D_MODEL, DEPTH_2, jnp.float32

    def nrm(k, shape, fan_in, mult=1.0):
        return jax.random.normal(k, shape, f32) * (mult * fan_in ** -0.5)

    def gain(k, shape):
        return 1.0 + 0.05 * jax.random.normal(k, shape, f32)

    def small(k, shape, s):
        return s * jax.random.normal(k, shape, f32)

    offs = jax.random.randint(ks[2], (BATCH, 1), 0, 1024, dtype=jnp.int32)
    return {
        "x": jax.random.normal(ks[0], (BATCH, SEQ, D), f32),
        "c": jax.random.normal(ks[1], (BATCH, D), f32),
        "positions": (offs + jnp.arange(SEQ, dtype=jnp.int32)[None, :]).astype(jnp.int32),
        "rel_bias": small(ks[3], (REL_BUCKETS, DIFF_HEADS), 0.5),
        "w_ada": nrm(ks[4], (L, D, 6 * D), D, 0.5),
        "b_ada": small(ks[5], (L, 6 * D), 0.02),
        "norm1_g": gain(ks[6], (L, D)),
        "w_in": nrm(ks[7], (L, D, IN_WIDTH), D),
        "mla_cq_g": gain(ks[8], (L, MLA_Q_LORA)),
        "w_uq": nrm(ks[9], (L, MLA_Q_LORA, MLA_HEADS * MLA_QK), MLA_Q_LORA),
        "mla_ckv_g": gain(ks[10], (L, MLA_KV_LORA)),
        "w_ukv": nrm(ks[11], (L, MLA_KV_LORA, MLA_HEADS * (MLA_NOPE + MLA_V)), MLA_KV_LORA),
        "mla_q_g": gain(ks[12], (L, MLA_QK)),
        "mla_k_g": gain(ks[13], (L, MLA_QK)),
        "diff_q_g": gain(ks[14], (L, DIFF_HEAD_DIM)),
        "diff_k_g": gain(ks[15], (L, DIFF_HEAD_DIM)),
        "lambda_q1": small(ks[16], (L, DIFF_HEAD_DIM), 0.1),
        "lambda_k1": small(ks[17], (L, DIFF_HEAD_DIM), 0.1),
        "lambda_q2": small(ks[18], (L, DIFF_HEAD_DIM), 0.1),
        "lambda_k2": small(ks[19], (L, DIFF_HEAD_DIM), 0.1),
        "diff_subln_g": gain(ks[20], (L, DIFF_V)),
        "w_o": nrm(ks[21], (L, MIX_WIDTH, D), MIX_WIDTH),
        "norm2_g": gain(ks[22], (L, D)),
        "w_rg": nrm(ks[23], (L, D, N_GROUPS), D),
        "b_rg": small(ks[24], (L, N_GROUPS), 0.01),
        "w_re": nrm(ks[25], (L, D, N_EXPERTS_2), D),
        "b_re": small(ks[26], (L, N_EXPERTS_2), 0.01),
        "w_gate": nrm(ks[27], (L, N_EXPERTS_2, D, D_EXPERT), D),
        "w_up": nrm(ks[28], (L, N_EXPERTS_2, D, D_EXPERT), D),
        "w_down": nrm(ks[29], (L, N_EXPERTS_2, D_EXPERT, D), D_EXPERT),
    }

def second_block(x, c, positions, rel_bias, w_ada, b_ada, norm1_g, w_in, mla_cq_g, w_uq, mla_ckv_g, w_ukv,
              mla_q_g, mla_k_g, diff_q_g, diff_k_g, lambda_q1, lambda_k1, lambda_q2, lambda_k2,
              diff_subln_g, w_o, norm2_g, w_rg, b_rg, w_re, b_re, w_gate, w_up, w_down):
    for l in range(DEPTH_2):
        lambda_init = 0.8 - 0.6 * math.exp(-0.3 * l)
        mod = jnp.einsum('bd,de->be', jax.nn.silu(c), w_ada[l]) + b_ada[l]
        sh1, sc1, g1, sh2, sc2, g2 = [m[:, None, :] for m in jnp.split(mod, 6, axis=-1)]
        h = _rms(x, norm1_g[l]) * (1.0 + sc1) + sh1
        proj = h @ w_in[l]
        c_q, c_kv, k_pe, dq, dk, dv = jnp.split(proj, IN_SPLITS, axis=-1)
        o_mla = _mla(c_q, c_kv, k_pe, positions, mla_cq_g[l], w_uq[l], mla_ckv_g[l], w_ukv[l],
                     mla_q_g[l], mla_k_g[l])
        o_diff = _diff_attn(dq, dk, dv, positions, rel_bias, diff_q_g[l], diff_k_g[l], lambda_q1[l],
                            lambda_k1[l], lambda_q2[l], lambda_k2[l], diff_subln_g[l], lambda_init)
        x = x + g1 * (jnp.concatenate([o_mla, o_diff], axis=-1) @ w_o[l])
        h2 = _rms(x, norm2_g[l]) * (1.0 + sc2) + sh2
        x = x + g2 * _hmoe(h2, w_rg[l], b_rg[l], w_re[l], b_re[l], w_gate[l], w_up[l], w_down[l])
    return x


def setup_inputs(seed=0):
    out = dict(first_inputs(seed))
    for name, value in second_inputs(seed + 1).items():
        if name != "x":
            out[name + "_2"] = value
    return out


def reference(
    x, meta_tokens, ln_gain, ln_bias, rg_w_in, rg_conv_w, rg_conv_b, rg_w_gates, rg_b_gates,
    rg_lambda, rg_w_out, gla_w_in, gla_w_gate_up, gla_b_gate, gla_norm_g, gla_w_out, ffn_w_in,
    ffn_w_out, moe_router, moe_w_in, moe_w_out, c_2, positions_2, rel_bias_2, w_ada_2, b_ada_2,
    norm1_g_2, w_in_2, mla_cq_g_2, w_uq_2, mla_ckv_g_2, w_ukv_2, mla_q_g_2, mla_k_g_2,
    diff_q_g_2, diff_k_g_2, lambda_q1_2, lambda_k1_2, lambda_q2_2, lambda_k2_2, diff_subln_g_2,
    w_o_2, norm2_g_2, w_rg_2, b_rg_2, w_re_2, b_re_2, w_gate_2, w_up_2, w_down_2,
):
    x = first_block(
        x, meta_tokens, ln_gain, ln_bias, rg_w_in, rg_conv_w, rg_conv_b, rg_w_gates, rg_b_gates,
        rg_lambda, rg_w_out, gla_w_in, gla_w_gate_up, gla_b_gate, gla_norm_g, gla_w_out,
        ffn_w_in, ffn_w_out, moe_router, moe_w_in, moe_w_out,
    )
    return second_block(
        x, c_2, positions_2, rel_bias_2, w_ada_2, b_ada_2, norm1_g_2, w_in_2, mla_cq_g_2,
        w_uq_2, mla_ckv_g_2, w_ukv_2, mla_q_g_2, mla_k_g_2, diff_q_g_2, diff_k_g_2, lambda_q1_2,
        lambda_k1_2, lambda_q2_2, lambda_k2_2, diff_subln_g_2, w_o_2, norm2_g_2, w_rg_2, b_rg_2,
        w_re_2, b_re_2, w_gate_2, w_up_2, w_down_2,
    )


_drawn_inputs = setup_inputs


def setup_inputs(seed=0):
    import zlib

    import numpy as np

    out = dict(_drawn_inputs(seed))
    spreads = {}
    factors = {'rg_b_gates': 8.0,
     'gla_b_gate': 3.771,
     'gla_norm_g': 8.0,
     'b_ada_2': 2.726,
     'norm1_g_2': 6.603,
     'mla_cq_g_2': 8.0,
     'mla_ckv_g_2': 8.0,
     'mla_q_g_2': 8.0,
     'mla_k_g_2': 8.0,
     'diff_q_g_2': 8.0,
     'diff_k_g_2': 8.0,
     'lambda_q1_2': 8.0,
     'lambda_k1_2': 7.549,
     'lambda_q2_2': 8.0,
     'lambda_k2_2': 5.703,
     'diff_subln_g_2': 4.345,
     'norm2_g_2': 2.77,
     'b_rg_2': 7.099,
     'b_re_2': 8.0}
    for name, (base, spread) in spreads.items():
        noise = np.random.default_rng([zlib.crc32(name.encode()), seed]).standard_normal(out[name].shape)
        drawn = base * np.exp(spread * noise) if base else spread * noise
        out[name] = __import__('jax').numpy.asarray(drawn.astype(out[name].dtype))
    for name, factor in factors.items():
        out[name] = (out[name] * factor).astype(out[name].dtype)
    return out
```

```python
from contextlib import ExitStack
import math

import numpy as np
import concourse.bass as bass
from concourse import mybir

F32 = mybir.dt.float32
F32R = mybir.dt.float32r
I32 = mybir.dt.int32
U32 = mybir.dt.uint32
ALU = mybir.AluOpType
ACT = mybir.ActivationFunctionType
AX = mybir.AxisListType

ALPHA = (2 * 2) ** 0.25
LN_EPS = 1e-5
RMS_EPS = 1e-6
T = 272
CW = 2048
NRAW, NSPL = 3, 3
LAMBDA_INIT = 0.8 - 0.6 * math.exp(-0.3 * 0)
STEPS = [(-90, 14), (-63, 13), (-45, 12), (-31, 11), (-22, 10), (-15, 9), (-11, 8), (-7, 7), (-6, 6), (-5, 5),
         (-4, 4), (-3, 3), (-2, 2), (-1, 1), (0, 0), (1, 17), (2, 18), (3, 19), (4, 20), (5, 21), (6, 22), (7, 23),
         (8, 24), (12, 25), (16, 26), (23, 27), (32, 28), (46, 29), (64, 30), (91, 31)]
TILES = [(2, 16, 0), (0, 128, 16), (1, 128, 144)]
XTILES = [(0, 128, 16), (1, 128, 144)]
QTILES = [(0, 128, 0), (1, 128, 128)]
C_ID, C_CM, C_SM, C_AM, C_IO, C_IF, C_END = 0, 128, 256, 528, 912, 928, 944


def const_table():
    c = np.zeros((128, C_END), np.float32)
    c[:, C_ID:C_ID + 128] = np.eye(128, dtype=np.float32)
    s, q = np.arange(128)[:, None], np.arange(128)[None, :]
    c[:, C_CM:C_CM + 128] = (s <= q) & (s // 64 == q // 64)
    m = np.ones(T, np.float32)
    m[[0, 16, 80, 144, 208]] = 0.0
    c[:, C_SM:C_SM + T] = m
    c[:64, C_AM + 64:C_AM + 128] = -1e30
    c[:64, C_AM + 128 + 192:C_AM + 384] = -1e30
    c[:, C_IO:C_IO + 16] = np.arange(16, dtype=np.float32)
    c[:, C_IF:C_IF + 16] = np.float32(10000.0) ** (-np.arange(16, dtype=np.float32) / np.float32(16))
    return c


class Queue:

    def __init__(self, sem):
        self.sem, self.n, self.items, self.seen = sem, 0, [], {}

    def wait(self, *toks):
        for tok in toks:
            if tok is None:
                continue
            sem, v = tok
            if self.seen.get(sem.name, 0) < v:
                self.seen[sem.name] = v
                self.items.append((None, sem, v))

    def run(self, f, *toks):
        self.wait(*toks)
        self.items.append((f, None, 0))

    def do(self, f, *toks):
        self.wait(*toks)
        self.n += 1
        self.items.append((f, self.sem, 1))
        return (self.sem, self.n)

    def seq(self, f, *toks):
        return self.do(f, self.last, *toks)

    def dma(self, f, sem, count, *toks):
        self.wait(*toks)
        count[0] += 16
        self.items.append((f, sem, 16))
        return (sem, count[0])

    @property
    def last(self):
        return (self.sem, self.n) if self.n else None

    def emit(self, eng):
        for f, sem, v in self.items:
            if f is None:
                eng.wait_ge(sem, v)
            elif sem is None:
                f(eng)
            else:
                f(eng).then_inc(sem, v)


class Program:
    def __init__(self, nc, d, out, dumps=None):
        self.nc, self.d, self.out, self.dumps = nc, d, out, dumps
        self.ctx = ExitStack()
        self.T = Queue(self.sem("s_pe"))
        self.V = Queue(self.sem("s_dve"))
        self.A = Queue(self.sem("s_act"))
        self.G = Queue(self.sem("s_pool"))
        self.S = Queue(self.sem("s_sp"))
        self.nsem = 0
        self.phase_ctx = None
        self.pending_out = []

    def sem(self, name):
        return self.ctx.enter_context(self.nc.semaphore(name))

    def sb(self, name, shape, dt=F32):
        return self.ctx.enter_context(self.nc.sbuf_tensor(name, shape, dt))

    def ph(self, name, shape, dt=F32):
        return self.phase_ctx.enter_context(self.nc.sbuf_tensor(name, shape, dt))

    def phase(self):
        if self.phase_ctx is not None:
            self.phase_ctx.close()
            lasts = [q.last for q in (self.T, self.V, self.A, self.G)]
            for q in (self.T, self.V, self.A, self.G):
                q.wait(*lasts, *self.loads)
        self.loads = []
        self.phase_ctx = ExitStack()

    def rest(self, name, shape, dt=F32):
        return self.ctx.enter_context(self.nc.sbuf_tensor(name, shape, dt))

    def load(self, q, dst, src, *toks):
        self.nsem += 1
        sem = self.sem(f"s_ld{self.nsem}")
        tok = q.dma(lambda e: e.dma_start(dst, src), sem, [0], *toks)
        self.loads.append(tok)
        return tok

    def dump(self, name, ap, *toks):
        if self.dumps is not None:
            o = self.nc.dram_tensor("dbg_" + name, ap.shape, F32, kind="ExternalOutput").ap()
            self.dumps.append("dbg_" + name)
            t = self.load(self.S, o, ap, *toks)
            for q in (self.T, self.V, self.A, self.G):
                q.wait(t)

    def banks_init(self):
        self.ps = [self.ctx.enter_context(self.nc.psum_tensor(f"ps{i}", [128, 512], F32)) for i in range(8)]
        self.bank_free = [[] for _ in range(8)]
        self.bank_at = 0

    def take(self):
        i = self.bank_at
        while self.bank_free[i] is None:
            i = (i + 1) % 8
        self.bank_at = (i + 1) % 8
        self.T.wait(*self.bank_free[i])
        self.bank_free[i] = None
        return i

    def free(self, i, *toks):
        self.bank_free[i] = list(toks)

    def stream_init(self):
        self.raw = self.sb("raw", [128, NRAW, CW], F32)
        self.whi = self.sb("whi", [128, NSPL, CW], F32R)
        self.wlo = self.sb("wlo", [128, NSPL, CW], F32R)
        self.s_raw = [self.sem(f"s_raw{i}") for i in range(NRAW)]
        self.n_raw = [[0] for _ in range(NRAW)]
        self.chunks = []
        self.at = 0
        self.n_loaded = 0
        self.n_split = 0
        self.spl_next = 0
        self.raw_free = [None] * NRAW
        self.spl_free = [None] * NSPL
        self.raw_busy = [False] * NRAW
        self.spl_busy = [False] * NSPL

    def chunk(self, key, rows, n, pieces, split=True, zero=False):
        self.chunks.append(dict(key=key, rows=rows, n=n, pieces=pieces, split=split, zero=zero))

    def pump(self):
        go = True
        while go:
            go = False
            i = self.n_loaded
            if i < len(self.chunks) and not self.raw_busy[i % NRAW]:
                c, k = self.chunks[i], i % NRAW
                self.raw_busy[k] = True
                slot = self.raw[0:c["rows"], k, 0:c["n"]]
                before = [self.raw_free[k]]
                if c["zero"]:
                    before = [self.G.do(lambda e, s=slot: e.memset(s, 0.0), *before)]
                for dst, src in c["pieces"](slot):
                    tok = self.S.dma(lambda e, a=dst, b=src: e.dma_start(a, b), self.s_raw[k], self.n_raw[k], *before)
                c["raw"], c["in"], c["k"] = slot, tok, k
                self.n_loaded += 1
                go = True
            i = self.n_split
            if i < self.n_loaded:
                c = self.chunks[i]
                if not c["split"]:
                    self.n_split += 1
                    go = True
                    continue
                s = self.spl_next
                if not self.spl_busy[s]:
                    self.spl_busy[s] = True
                    self.spl_next = (s + 1) % NSPL
                    hi = self.whi[0:c["rows"], s, 0:c["n"]]
                    lo = self.wlo[0:c["rows"], s, 0:c["n"]]
                    t1 = self.A.do(lambda e, h=hi, r=c["raw"]: e.activation(h, r, ACT.Copy), c["in"], self.spl_free[s])
                    t2 = self.V.do(lambda e, l=lo, h=hi, r=c["raw"]:
                                   e.tensor_tensor(l, r, h.bitcast(F32), ALU.subtract), t1, self.spl_free[s])
                    c["hi"], c["lo"], c["s"], c["ready"] = hi, lo, s, t2
                    self.raw_free[c["k"]] = t2
                    self.raw_busy[c["k"]] = False
                    self.n_split += 1
                    go = True

    def next(self, key):
        c = self.chunks[self.at]
        assert c["key"] == key, (c["key"], key)
        self.at += 1
        self.pump()
        self.T.wait(c["ready"] if c["split"] else c["in"])
        return c

    def done(self, c, tok):
        if c["split"]:
            self.spl_free[c["s"]] = tok
            self.spl_busy[c["s"]] = False
        else:
            self.raw_free[c["k"]] = tok
            self.raw_busy[c["k"]] = False
        self.pump()

    def mm3(self, out, lh, ll, rh, rl, start, stop, mark=False):
        self.T.run(lambda e: e.matmul(out, lh, rh, start=start, stop=False))
        self.T.run(lambda e: e.matmul(out, lh, rl, start=False, stop=False))
        f = lambda e: e.matmul(out, ll, rh, start=False, stop=stop)
        if stop or mark:
            return self.T.do(f)
        self.T.run(f)

    def mm(self, out, l, r, start, stop, *toks):
        f = lambda e: e.matmul(out, l, r, start=start, stop=stop)
        if stop:
            return self.T.do(f, *toks)
        self.T.run(f, *toks)

    def split(self, hi, lo, src, *toks):
        t1 = self.A.do(lambda e: e.activation(hi, src, ACT.Copy), *toks)
        t2 = self.V.do(lambda e: e.tensor_tensor(lo, src, hi.bitcast(F32), ALU.subtract), t1)
        return t2

    def make_T(self, src, tiles, nk, hi, lo, *toks):
        idn = self.cst
        tok = None
        c0 = min(c for _, _, c in tiles)
        c1 = max(c + n for _, n, c in tiles)
        for k in range(nk):
            b = self.take()
            for t, n, c in tiles:
                a = src(t, k)
                f = lambda e, o=self.ps[b][:, c:c + n], a=a, n=n: e.transpose(o, a, idn[0:n, C_ID:C_ID + n])
                tt = self.T.do(f, *toks)
            tok = self.split(hi[:, k, c0:c1], lo[:, k, c0:c1], self.ps[b][:, c0:c1], tt)
            self.free(b, tok)
        return tok

    def rsqrt(self, y, x, tmp, *toks):
        V = self.V
        V.seq(lambda e: e.tensor_scalar(y.bitcast(I32), x.bitcast(I32), 1, None, ALU.logical_shift_right), *toks)
        V.seq(lambda e: e.tensor_scalar(y.bitcast(I32), y.bitcast(I32), -1.0, 1597463007.0, ALU.mult, ALU.add))
        V.seq(lambda e: e.tensor_scalar(x, x, 0.5, None, ALU.mult))
        for _ in range(4):
            V.seq(lambda e: e.tensor_tensor(tmp, y, y, ALU.mult))
            V.seq(lambda e: e.tensor_tensor(tmp, tmp, x, ALU.mult))
            t = V.seq(lambda e: e.scalar_tensor_tensor(y, tmp, 1.5, y, ALU.subtract, ALU.mult))
        return t

    def layer_norm(self, tiles, src, gi, *toks):
        V, h = self.V, self.h
        i, j = gi
        tg = self.load(self.G, self.lng[:, :], self.d["ln_gain"][i, j:j + 1, :].partition_broadcast(128), self.ln_free)
        tb = self.load(self.G, self.lnb[:, :], self.d["ln_bias"][i, j:j + 1, :].partition_broadcast(128), self.ln_free)
        st, mv, rs, tmp = self.st, self.mv, self.rs, self.rtmp
        V.seq(lambda e: e.memset(mv[:, :, :], 1.0))
        read = None
        for t, n, _ in tiles:
            for q in range(2):
                a = h[0:n, t, q * 512:(q + 1) * 512]
                read = V.do(lambda e, a=a, s=src(t, q): e.scalar_tensor_tensor(a, a, ALPHA, s, ALU.mult, ALU.add), *toks)
        self.ln_read = read
        for t, n, _ in tiles:
            for q in range(2):
                V.seq(lambda e, a=h[0:n, t, q * 512:(q + 1) * 512], o=st[0:n, t, q, :]: e.bn_stats(o, a))
        for t, n, _ in tiles:
            V.seq(lambda e, o=mv[0:n, t, :], a=st[0:n, t, :, :]: e.bn_aggr(o, a))
        V.seq(lambda e: e.tensor_scalar(rs[:, 0, 0:3], mv[:, :, 1], LN_EPS, None, ALU.add))
        self.rsqrt(rs[:, 1, 0:3], rs[:, 0, 0:3], tmp[:, 0:3])
        for t, n, _ in tiles:
            a = h[0:n, t, :]
            V.seq(lambda e, a=a, n=n, t=t: e.tensor_scalar(a, a, mv[0:n, t, 0:1], rs[0:n, 1, t:t + 1],
                                                            ALU.subtract, ALU.mult))
            V.seq(lambda e, a=a, n=n: e.tensor_tensor(a, a, self.lng[0:n, :], ALU.mult), tg)
            self.ln_free = V.seq(lambda e, a=a, n=n: e.tensor_tensor(a, a, self.lnb[0:n, :], ALU.add), tb)
        return self.ln_free

    def plan_ffn(self, key, wg, wu, wd, F):
        for j in range(F // 256):
            for nm, w in (("g", wg), ("u", wu)):
                self.chunk((key, nm, j), 128, CW, lambda s, w=w, j=j: [
                    (s.rearrange("p (k n) -> p k n", k=8),
                     w[:, 256 * j:256 * j + 256].rearrange("(k p) n -> p k n", p=128))])
        for j in range(F // 256):
            self.chunk((key, "d", j), 128, CW, lambda s, j=j: [
                (s.rearrange("p (i n) -> p i n", i=2),
                 wd[256 * j:256 * j + 256, :].rearrange("(i p) n -> p i n", p=128))])

    def ffn(self, key, F, tiles, c0, n, xh, xl, ah, al, tx):
        V, A, T_ = self.V, self.A, self.T
        self.T.wait(tx)
        ta = None
        for j in range(F // 256):
            bs = {}
            for nm in "gu":
                c = self.next((key, nm, j))
                wh = c["hi"].rearrange("p (k n) -> p k n", k=8)
                wl = c["lo"].rearrange("p (k n) -> p k n", k=8)
                for i in range(2):
                    b = self.take()
                    for k in range(8):
                        tok = self.mm3(self.ps[b][:, 0:n], wh[:, k, i * 128:i * 128 + 128], wl[:, k, i * 128:i * 128 + 128],
                                       xh[:, k, c0:c0 + n], xl[:, k, c0:c0 + n], k == 0, k == 7)
                    bs[nm, i] = (b, tok)
                self.done(c, tok)
            for i in range(2):
                f = 2 * j + i
                bg, tg = bs["g", i]
                bu, tu = bs["u", i]
                z = self.sg_at
                self.sg_at = (z + 1) % 4
                g = self.sg[:, z, 0:n]
                t1 = A.do(lambda e, g=g, b=bg: e.activation(g, self.ps[b][:, 0:n], ACT.Silu), tg, self.sg_free[z])
                self.free(bg, t1)
                t2 = V.do(lambda e, g=g, b=bu: e.tensor_tensor(g, g, self.ps[b][:, 0:n], ALU.mult), t1, tu)
                self.free(bu, t2)
                ta = self.split(ah[:, f, 0:n], al[:, f, 0:n], g, t2, self.act_free)
                self.sg_free[z] = ta
        acc = {(t, q): self.take() for t, _, _ in tiles for q in range(2)}
        self.T.wait(ta)
        nf = F // 128
        for j in range(F // 256):
            c = self.next((key, "d", j))
            wh = c["hi"].rearrange("p (i n) -> p i n", i=2)
            wl = c["lo"].rearrange("p (i n) -> p i n", i=2)
            for i in range(2):
                f = 2 * j + i
                for t, nt, cc in tiles:
                    for q in range(2):
                        o = self.ps[acc[t, q]][0:nt, :]
                        a = slice(cc - c0, cc - c0 + nt)
                        tok = self.mm3(o, ah[:, f, a], al[:, f, a], wh[:, i, q * 512:q * 512 + 512],
                                       wl[:, i, q * 512:q * 512 + 512], f == 0, f == nf - 1,
                                       mark=(i == 1 and t == tiles[-1][0] and q == 1))
            self.done(c, tok)
        self.act_free = tok
        return acc, tok


def build(nc, d, out, dumps=None):
    P = Program(nc, d, out, dumps)
    T_, V, A, G, S = P.T, P.V, P.A, P.G, P.S
    P.loads = []
    P.banks_init()
    ps = P.ps
    P.cst = cst = P.sb("cst", [128, C_END])
    P.xh = xh = P.sb("xh", [128, 8, T], F32R)
    P.xl = xl = P.sb("xl", [128, 8, T], F32R)
    P.h = h = P.sb("h", [128, 3, 1024])
    lnt = P.sb("lnt", [128, 2048])
    P.lng, P.lnb = lnt[:, 0:1024], lnt[:, 1024:2048]
    P.st = P.sb("st", [128, 8, 2, 6])
    P.mv = P.sb("mv", [128, 3, 2])
    P.rs = P.sb("rs", [128, 2, 32])
    P.rtmp = P.sb("rtmp", [128, 32])
    rwr = P.sb("rwr", [128, 8, 32])
    rwh = P.sb("rwh", [128, 8, 32], F32R)
    rwl = P.sb("rwl", [128, 8, 32], F32R)
    gates = P.sb("gates", [128, 2, 16])
    gw = P.sb("gw", [128, 2, 64])
    gi = P.sb("gi", [128, 2, 8], U32)
    P.ln_free = None
    P.act_free = None
    P.stream_init()

    w_rg, w_ro = d["rg_w_in"][0], d["rg_w_out"][0]

    def plan_rg(key, off):
        for j in range(6):
            P.chunk((key, j), 128, 8 * 224, lambda s, j=j: [
                (s.rearrange("p (k n) -> p k n", k=8),
                 w_rg[:, off + 224 * j:off + 224 * j + 224].rearrange("(k p) n -> p k n", p=128))])

    plan_rg("xr", 1344)
    wgt = d["rg_w_gates"][0]
    for j in range(4):
        def pieces(s, j=j):
            v = s.rearrange("p (g k n) -> p g k n", g=2, k=3)
            a, b = wgt[:, 2 * j].rearrange("g c n -> c g n"), wgt[:, 2 * j + 1].rearrange("g c n -> c g n")
            return [(v[0:112, :, 0, 0:168], a[0:112]), (v[0:56, :, 1, 0:168], a[112:168]),
                    (v[56:112, :, 1, 168:336], b[0:56]), (v[0:112, :, 2, 168:336], b[56:168])]
        P.chunk(("gt", j), 112, 2 * 3 * 336, pieces, zero=True)
    plan_rg("gb", 0)
    for j in range(6):
        P.chunk(("ro", j), 112, CW, lambda s, j=j: [
            (s.rearrange("p (i n) -> p i n", i=2),
             w_ro[224 * j:224 * j + 224, :].rearrange("(i p) n -> p i n", p=112))])
    P.plan_ffn("ffn", d["ffn_w_in"][0][:, 0:3584], d["ffn_w_in"][0][:, 3584:7168], d["ffn_w_out"][0], 3584)
    w_gl = d["gla_w_in"][0]
    P.chunk("gz", 128, 128, lambda s: [(s.rearrange("p (k n) -> p k n", k=8),
                                        w_gl[:, 3072:3088].rearrange("(k p) n -> p k n", p=128))])

    def plan_cols(key, w, off, m, wd=256):
        for j in range(m):
            P.chunk((key, j), 128, 8 * wd, lambda s, j=j: [
                (s.rearrange("p (k n) -> p k n", k=8),
                 w[:, off + wd * j:off + wd * j + wd].rearrange("(k p) n -> p k n", p=128))])

    def plan_rows(key, w, m):
        for j in range(m):
            P.chunk((key, j), 128, CW, lambda s, j=j: [
                (s.rearrange("p (i n) -> p i n", i=2),
                 w[256 * j:256 * j + 256, :].rearrange("(i p) n -> p i n", p=128))])

    plan_cols("gk", w_gl, 512, 2)
    plan_cols("gq", w_gl, 0, 2)
    plan_cols("gv", w_gl, 1024, 4)
    plan_cols("gr", w_gl, 2048, 4)
    plan_rows("go", d["gla_w_out"][0], 4)
    for e in range(8):
        P.plan_ffn(("m1", e), d["moe_w_in"][0, e][:, 0:3584], d["moe_w_in"][0, e][:, 3584:7168], d["moe_w_out"][0, e], 3584)
    w_ada = d["w_ada_2"][0]
    for j in range(24):
        P.chunk(("ada", j), 128, CW, lambda s, j=j: [
            (s.rearrange("p (k n) -> p k n", k=8),
             w_ada[:, 256 * j:256 * j + 256].rearrange("(k p) n -> p k n", p=128))], split=False)
    w_i2 = d["w_in_2"][0]
    plan_cols("wi", w_i2, 0, 8)
    P.chunk(("wi", 8), 128, 8 * 160, lambda s: [(s.rearrange("p (k n) -> p k n", k=8),
                                                 w_i2[:, 2048:2208].rearrange("(k p) n -> p k n", p=128))])
    for j in range(2):
        P.chunk(("uq", j), 128, 3 * 384, lambda s, j=j: [
            (s.rearrange("p (k n) -> p k n", k=3),
             d["w_uq_2"][0][:, 384 * j:384 * j + 384].rearrange("(k p) n -> p k n", p=128))])
    P.chunk("ukv", 128, 2 * 1024, lambda s: [(s.rearrange("p (k n) -> p k n", k=2),
                                              d["w_ukv_2"][0].rearrange("(k p) n -> p k n", p=128))])
    plan_rows("wo", d["w_o_2"][0], 4)
    for e in range(16):
        P.plan_ffn(("m2", e), d["w_gate_2"][0, e], d["w_up_2"][0, e], d["w_down_2"][0, e], 512)

    P.phase()
    t_c = P.load(S, cst[:, :], d["consts"])
    t_h = [P.load(S, h[0:16, 2, :], d["meta_tokens"]), P.load(S, h[:, 0, :], d["x"][0, 0:128]),
           P.load(S, h[:, 1, :], d["x"][0, 128:256])]
    vec = P.ph("vec", [8, 1344])
    t_v = [P.load(S, vec[0:4, :], d["rg_conv_w"][0]), P.load(S, vec[4:5, :], d["rg_conv_b"]),
           P.load(S, vec[5:7, :], d["rg_b_gates"][0]), P.load(S, vec[7:8, :], d["rg_lambda"])]
    vT = P.ph("vT", [112, 12, 8])
    sp = P.ph("sp", [112, 6, 12])
    X1 = P.ph("X1", [112, 12, 275])
    X2 = P.ph("X2", [112, 12, T])
    xch = P.ph("xch", [112, 12, T], F32R)
    xcl = P.ph("xcl", [112, 12, T], F32R)
    R = P.ph("R", [112, 12, T])
    I = P.ph("I", [112, 12, T])

    P.pump()
    t_x = P.make_T(lambda t, k: h[0:(16 if t == 2 else 128), t, 128 * k:128 * k + 128], TILES, 8, xh, xl, t_c, *t_h)
    b = P.take()
    for c in range(12):
        tok = T_.do(lambda e, c=c, b=b: e.transpose(ps[b][0:112, 8 * c:8 * c + 8], vec[:, 112 * c:112 * c + 112],
                                                    cst[0:8, C_ID:C_ID + 8]), *t_v, t_c)
    tv = V.do(lambda e, b=b: e.tensor_copy(vT[:, :, :], ps[b][0:112, 0:96].rearrange("p (c n) -> p c n", n=8)), tok)
    P.free(b, tv)
    lam = vT[:, :, 7]
    ex = A.do(lambda e: e.activation(sp[:, 0, :], lam, ACT.Abs), tv)
    ex = A.seq(lambda e: e.activation(sp[:, 0, :], sp[:, 0, :], ACT.Exp, scale=-1.0))
    V.seq(lambda e: e.tensor_scalar(sp[:, 1, :], sp[:, 0, :], 2.0, None, ALU.add), ex)
    V.seq(lambda e: e.reciprocal(sp[:, 1, :], sp[:, 1, :]))
    V.seq(lambda e: e.tensor_tensor(sp[:, 1, :], sp[:, 1, :], sp[:, 0, :], ALU.mult))
    V.seq(lambda e: e.tensor_tensor(sp[:, 2, :], sp[:, 1, :], sp[:, 1, :], ALU.mult))
    V.seq(lambda e: e.memset(sp[:, 3, :], 1.0 / 17.0))
    for m in (15, 13, 11, 9, 7, 5, 3, 1):
        V.seq(lambda e: e.tensor_tensor(sp[:, 3, :], sp[:, 3, :], sp[:, 2, :], ALU.mult))
        V.seq(lambda e, m=m: e.tensor_scalar(sp[:, 3, :], sp[:, 3, :], 1.0 / m, None, ALU.add))
    V.seq(lambda e: e.tensor_tensor(sp[:, 3, :], sp[:, 3, :], sp[:, 1, :], ALU.mult))
    V.seq(lambda e: e.tensor_scalar(sp[:, 4, :], lam, -1.0, 0.0, ALU.mult, ALU.max))
    V.seq(lambda e: e.scalar_tensor_tensor(sp[:, 5, :], sp[:, 3, :], 2.0, sp[:, 4, :], ALU.mult, ALU.add))
    t_sp = V.seq(lambda e: e.tensor_scalar(sp[:, 5, :], sp[:, 5, :], 4.0, None, ALU.mult))
    V.seq(lambda e: e.memset(X1[:, :, 0:3], 0.0))

    def rg_in(key, j, evac):
        c = P.next((key, j))
        wh = c["hi"].rearrange("p (k n) -> p k n", k=8)
        wl = c["lo"].rearrange("p (k n) -> p k n", k=8)
        for i in range(2):
            b = P.take()
            for k in range(8):
                tok = P.mm3(ps[b][0:112, 0:T], wh[:, k, 112 * i:112 * i + 112], wl[:, k, 112 * i:112 * i + 112],
                            xh[:, k, :], xl[:, k, :], k == 0, k == 7)
            if i == 1:
                P.done(c, tok)
            P.free(b, evac(2 * j + i, ps[b][0:112, 0:T], tok))

    t_xc = {}

    def conv(m, pt, tok):
        te = A.do(lambda e: e.activation(X1[:, m, 3:275], pt, ACT.Copy), tok)
        V.seq(lambda e: e.tensor_scalar(X2[:, m, :], X1[:, m, 0:T], vT[:, m, 0:1], vT[:, m, 4:5], ALU.mult, ALU.add), te)
        for q in range(1, 4):
            t = V.seq(lambda e, q=q: e.scalar_tensor_tensor(X2[:, m, :], X1[:, m, q:q + T], vT[:, m, q:q + 1],
                                                            X2[:, m, :], ALU.mult, ALU.add))
        t_xc[m] = P.split(xch[:, m, :], xcl[:, m, :], X2[:, m, :], t)
        return te

    T_.wait(t_x)
    for j in range(6):
        rg_in("xr", j, conv)
    Qt = X1[:, :, 0:T]
    t_gate = None
    for j in range(4):
        c = P.next(("gt", j))
        wh = c["hi"].rearrange("p (g k n) -> p g k n", g=2, k=3)
        wl = c["lo"].rearrange("p (g k n) -> p g k n", g=2, k=3)
        T_.wait(t_xc[3 * j + 2])
        tt = []
        for mt in range(3):
            for g in range(2):
                b = P.take()
                kts = ([0, 1], [0, 1, 2], [1, 2])[mt]
                for kt in kts:
                    tok = P.mm3(ps[b][0:112, 0:T], wh[:, g, kt, 112 * mt:112 * mt + 112], wl[:, g, kt, 112 * mt:112 * mt + 112],
                                xch[:, 3 * j + kt, :], xcl[:, 3 * j + kt, :], kt == kts[0], kt == kts[-1])
                m = 3 * j + mt
                dst = (R, I)[g][:, m, :]
                t = A.do(lambda e, dst=dst, b=b, g=g, m=m: e.activation(dst, ps[b][0:112, 0:T], ACT.Sigmoid,
                                                                        bias=vT[:, m, 5 + g:6 + g]), tok)
                P.free(b, t)
            tt.append(A.seq(lambda e, m=m: e.activation(R[:, m, :], R[:, m, :], ACT.Tanh, scale=sp[:, 5, m:m + 1]), t_sp))
        P.done(c, tok)
        z = slice(3 * j, 3 * j + 3)
        V.seq(lambda e, z=z: e.tensor_scalar(Qt[:, z, :], R[:, z, :], 1.0, None, ALU.add), *tt)
        V.seq(lambda e, z=z: e.reciprocal(Qt[:, z, :], Qt[:, z, :]))
        V.seq(lambda e, z=z: e.tensor_tensor(I[:, z, :], I[:, z, :], X2[:, z, :], ALU.mult))
        V.seq(lambda e, z=z: e.tensor_scalar(X2[:, z, :], R[:, z, :], -1.0, 1.0, ALU.mult, ALU.add))
        V.seq(lambda e, z=z: e.tensor_tensor(X2[:, z, :], X2[:, z, :], Qt[:, z, :], ALU.mult))
        t_gate = V.seq(lambda e, z=z: e.tensor_tensor(I[:, z, :], I[:, z, :], Qt[:, z, :], ALU.mult))
    ts = A.do(lambda e: e.activation(R[:, :, :], R[:, :, :], ACT.Sqrt), t_gate)
    for m in range(12):
        V.seq(lambda e, m=m: e.scalar_tensor_tensor(I[:, m, :], R[:, m, :], 2.0, I[:, m, :], ALU.mult, ALU.mult), ts)
        t_hs = V.seq(lambda e, m=m: e.tensor_tensor_scan(Qt[:, m, :], X2[:, m, :], I[:, m, :], 0.0, ALU.mult, ALU.add))
    t_y = {}

    def gbr(m, pt, tok):
        te = A.do(lambda e: e.activation(R[:, m, :], pt, ACT.Gelu_apprx_tanh), tok, t_hs)
        t = V.seq(lambda e: e.tensor_tensor(I[:, m, :], R[:, m, :], Qt[:, m, :], ALU.mult), te)
        t_y[m] = P.split(xch[:, m, :], xcl[:, m, :], I[:, m, :], t)
        return te

    for j in range(6):
        rg_in("gb", j, gbr)
    acc = {(t, q): P.take() for t, _, _ in TILES for q in range(2)}
    for j in range(6):
        c = P.next(("ro", j))
        wh = c["hi"].rearrange("p (i n) -> p i n", i=2)
        wl = c["lo"].rearrange("p (i n) -> p i n", i=2)
        for i in range(2):
            m = 2 * j + i
            T_.wait(t_y[m])
            for t, n, cc in TILES:
                for q in range(2):
                    tok = P.mm3(ps[acc[t, q]][0:n, :], xch[:, m, cc:cc + n], xcl[:, m, cc:cc + n],
                                wh[:, i, 512 * q:512 * q + 512], wl[:, i, 512 * q:512 * q + 512], m == 0, m == 11,
                                mark=(i == 1 and t == TILES[-1][0] and q == 1))
        P.done(c, tok)

    def end_block(acc, tiles, gi, tok):
        t = P.layer_norm(tiles, lambda t, q: ps[acc[t, q]][0:(16 if t == 2 else 128), :], gi, tok)
        for b in acc.values():
            P.free(b, P.ln_read)
        return t

    t_ln = end_block(acc, TILES, (0, 0), tok)
    P.dump("h0", h[:, 0:2, :], t_ln)
    src_h = lambda t, k: h[0:(16 if t == 2 else 128), t, 128 * k:128 * k + 128]
    t_x = P.make_T(src_h, TILES, 8, xh, xl, t_ln)

    def ffn_tiles(nf=28):
        P.sg = P.ph(f"sg{P.nsem}", [128, 4, T])
        P.sg_at, P.sg_free = 0, [None] * 4
        ah = P.ph(f"ah{P.nsem}", [128, nf, T], F32R)
        al = P.ph(f"al{P.nsem}", [128, nf, T], F32R)
        return ah, al

    P.phase()
    ah, al = ffn_tiles()
    acc, tok = P.ffn("ffn", 3584, TILES, 0, T, xh, xl, ah, al, t_x)
    t_ln = end_block(acc, TILES, (0, 1), tok)
    P.dump("h1", h[:, 0:2, :], t_ln)
    t_x = P.make_T(src_h, TILES, 8, xh, xl, t_ln)

    P.phase()
    wgu = P.ph("wgu", [16, 512])
    bgr = P.ph("bgr", [4, 128])
    ngb = P.ph("ngb", [128, 1024])
    t_wgu = P.load(G, wgu[:, :], d["gla_w_gate_up"][0], *[q.last for q in (T_, V, A)])
    t_bgr = P.load(G, bgr[:, :], d["gla_b_gate"][0].rearrange("(a n) -> a n", a=4))
    t_ngb = P.load(G, ngb[:, :], d["gla_norm_g"][0].rearrange("(a h) n -> a (h n)", a=1).partition_broadcast(128))
    bgT = P.ph("bgT", [128, 4])
    zT = P.ph("zT", [16, T])
    lg = P.ph("lg", [128, 4, T])
    bb = P.ph("bb", [128, 4, T])
    E1 = P.ph("E1", [128, 4, T])
    E2 = P.ph("E2", [128, 4, T])
    E3 = P.ph("E3", [128, 4, T])
    E4 = P.ph("E4", [128, 4, T])
    kot = P.ph("kot", [128, 3, 512])
    vt = P.ph("vt", [128, 3, 1024])
    rt = P.ph("rt", [128, 2, 1024])
    Sst = P.ph("Sst", [128, 5, 1024])
    sc = P.ph("sc", [128, 2, 512])
    og = rt
    mv8 = P.ph("mv8", [128, 8, 2])

    t_zero = V.do(lambda e: e.memset(sc[:, :, :], 0.0))
    b = P.take()
    tok = T_.do(lambda e, b=b: e.transpose(ps[b][:, 0:4], bgr[:, :], cst[0:4, C_ID:C_ID + 4]), t_bgr)
    t_bg = V.do(lambda e, b=b: e.tensor_copy(bgT[:, :], ps[b][:, 0:4]), tok)
    P.free(b, t_bg)
    T_.wait(t_x)
    c = P.next("gz")
    wh, wl = (c[s].rearrange("p (k n) -> p k n", k=8) for s in ("hi", "lo"))
    b = P.take()
    for k in range(8):
        tok = P.mm3(ps[b][0:16, 0:T], wh[:, k, :], wl[:, k, :], xh[:, k, :], xl[:, k, :], k == 0, k == 7)
    P.done(c, tok)
    t_z = A.do(lambda e, b=b: e.activation(zT[:, :], ps[b][0:16, 0:T], ACT.Copy), tok)
    P.free(b, t_z)
    for hh in range(4):
        b = P.take()
        tok = P.mm(ps[b][:, 0:T], wgu[:, 128 * hh:128 * hh + 128], zT[:, :], True, True, t_z, t_wgu)
        t = V.do(lambda e, b=b, hh=hh: e.tensor_scalar(lg[:, hh, :], ps[b][:, 0:T], bgT[:, hh:hh + 1], None, ALU.add),
                 tok, t_bg)
        P.free(b, t)
    fl = lambda a: a[:, :, :].rearrange("p h n -> p (h n)")
    A.do(lambda e: e.activation(fl(E1), fl(lg), ACT.Abs), t)
    A.seq(lambda e: e.activation(fl(E1), fl(E1), ACT.Exp, scale=-1.0))
    ta = A.seq(lambda e: e.activation(fl(E1), fl(E1), ACT.Ln, bias=1.0))
    V.seq(lambda e: e.scalar_tensor_tensor(fl(lg), fl(lg), 0.0, fl(E1), ALU.min, ALU.subtract), ta)
    for hh in range(4):
        t_b = V.seq(lambda e, hh=hh: e.tensor_tensor_scan(bb[:, hh, :], cst[:, C_SM:C_SM + T], lg[:, hh, :], 0.0,
                                                          ALU.mult, ALU.add))
    dec = lg
    for hh in range(4):
        bx = bb[:, hh, 16:272].rearrange("p (c s) -> p c s", s=64)
        dx = dec[:, hh, 16:272].rearrange("p (c s) -> p c s", s=64)
        V.do(lambda e, bx=bx, dx=dx: e.tensor_tensor(dx, bx, bx[:, :, 31:32].to_broadcast([128, 4, 64]), ALU.subtract), t_b)
        V.do(lambda e, hh=hh: e.tensor_copy(dec[:, hh, 0:16], bb[:, hh, 0:16]))
    t_d = V.last
    A.do(lambda e: e.activation(fl(E1), fl(dec), ACT.Exp, scale=1.0 / 16), t_d)
    te2 = A.do(lambda e: e.activation(fl(E2), fl(dec), ACT.Exp, scale=-1.0 / 16))
    te3 = A.do(lambda e: e.activation(fl(E3), fl(bb), ACT.Exp, scale=1.0 / 16))
    for hh in range(4):
        bx = bb[:, hh, 16:272].rearrange("p (c s) -> p c s", s=64)
        dx = dec[:, hh, 16:272].rearrange("p (c s) -> p c s", s=64)
        V.do(lambda e, bx=bx, dx=dx: e.tensor_tensor(dx, bx[:, :, 63:64].to_broadcast([128, 4, 64]), bx, ALU.subtract), te3)
        t_d = V.do(lambda e, hh=hh: e.tensor_tensor(dec[:, hh, 0:16], bb[:, hh, 15:16].to_broadcast([128, 16]),
                                                    bb[:, hh, 0:16], ALU.subtract))
    te4 = A.do(lambda e: e.activation(fl(E4), fl(dec), ACT.Exp, scale=1.0 / 16), t_d)
    tdc = V.do(lambda e: e.tensor_copy(gw[:, 0, 0:16].rearrange("p (h c) -> p h c", h=4),
                                       E3[:, :, 16:272].rearrange("p h (c s) -> p h c s", s=64)[:, :, :, 63]), te3)
    decs = gw[:, 0, 0:16].rearrange("p (h c) -> p h c", h=4)

    def chan(key, j, evac):
        c = P.next((key, j))
        wh, wl = (c[s].rearrange("p (k n) -> p k n", k=8) for s in ("hi", "lo"))
        for i in range(2):
            b = P.take()
            for k in range(8):
                tok = P.mm3(ps[b][:, 0:T], wh[:, k, 128 * i:128 * i + 128], wl[:, k, 128 * i:128 * i + 128],
                            xh[:, k, :], xl[:, k, :], k == 0, k == 7)
            if i == 1:
                P.done(c, tok)
            P.free(b, evac(2 * j + i, ps[b][:, 0:T], tok))

    def ev_k(m, pt, tok):
        V.do(lambda e: e.tensor_tensor(E2[:, m, :], pt, E2[:, m, :], ALU.mult), tok, te2)
        return V.do(lambda e: e.tensor_tensor(E4[:, m, :], pt, E4[:, m, :], ALU.mult), te4)

    def ev_q(m, pt, tok):
        s = 128.0 ** -0.5
        V.do(lambda e: e.scalar_tensor_tensor(E1[:, m, :], pt, s, E1[:, m, :], ALU.mult, ALU.mult), tok)
        return V.do(lambda e: e.scalar_tensor_tensor(E3[:, m, :], pt, s, E3[:, m, :], ALU.mult, ALU.mult), tdc)

    for j in range(2):
        chan("gk", j, ev_k)
    t_k = V.last
    for j in range(2):
        chan("gq", j, ev_q)
    t_q = V.last
    for t, n, cc in TILES:
        b = P.take()
        for hh in range(4):
            tok = T_.do(lambda e, b=b, n=n, cc=cc, hh=hh: e.transpose(ps[b][0:n, 128 * hh:128 * hh + 128], E4[:, hh, cc:cc + n],
                                                                      cst[:, C_ID:C_ID + 128]), t_k)
        t_ko = A.do(lambda e, b=b, n=n, t=t: e.activation(kot[0:n, t, :], ps[b][0:n, :], ACT.Copy), tok)
        P.free(b, t_ko)
    for t, n, cc in XTILES:
        b = P.take()
        for hh in range(4):
            tok = P.mm(ps[b][:, 128 * hh:128 * hh + 128], E2[:, hh, cc:cc + 128], E1[:, hh, cc:cc + 128], True, True, t_q)
        for hh in range(4):
            t_s = V.do(lambda e, b=b, t=t, hh=hh: e.copy_predicated(sc[:, t, 128 * hh:128 * hh + 128],
                                                                    cst[:, C_CM:C_CM + 128].bitcast(U32),
                                                                    ps[b][:, 128 * hh:128 * hh + 128]), tok, t_zero)
        P.free(b, t_s)

    def tokm(key, j, tiles, evac):
        c = P.next((key, j))
        n = c["n"] // 8
        wh, wl = (c[s].rearrange("p (k n) -> p k n", k=8) for s in ("hi", "lo"))
        for t, nt, cc in tiles:
            b = P.take()
            for k in range(8):
                tok = P.mm3(ps[b][0:nt, 0:n], xh[:, k, cc:cc + nt], xl[:, k, cc:cc + nt], wh[:, k, :], wl[:, k, :],
                            k == 0, k == 7)
            if t == tiles[-1][0]:
                P.done(c, tok)
            P.free(b, evac(t, nt, j, ps[b][0:nt, 0:n], tok))

    for j in range(4):
        tokm("gv", j, TILES, lambda t, n, j, pt, tok: A.do(
            lambda e: e.activation(vt[0:n, t, 256 * j:256 * j + 256], pt, ACT.Copy), tok))
    t_vt = A.last
    for j in range(4):
        tokm("gr", j, XTILES, lambda t, n, j, pt, tok: A.do(
            lambda e: e.activation(rt[0:n, t, 256 * j:256 * j + 256], pt, ACT.Silu), tok))
    t_rt = A.last
    t_S = None
    for ch in range(4):
        t, p0, n = ((2, 0, 16), (0, 0, 64), (0, 64, 64), (1, 0, 64))[ch]
        for pr in range(2):
            b = P.take()
            for hh in (2 * pr, 2 * pr + 1):
                tok = P.mm(ps[b][:, 256 * (hh % 2):256 * (hh % 2) + 256], kot[p0:p0 + n, t, 128 * hh:128 * hh + 128],
                           vt[p0:p0 + n, t, 256 * hh:256 * hh + 256], True, True, t_vt, t_ko)
            for hh in (2 * pr, 2 * pr + 1):
                o, a = Sst[:, ch + 1, 256 * hh:256 * hh + 256], ps[b][:, 256 * (hh % 2):256 * (hh % 2) + 256]
                if ch == 0:
                    t_S = V.do(lambda e, o=o, a=a: e.tensor_copy(o, a), tok)
                else:
                    t_S = V.seq(lambda e, o=o, a=a, hh=hh, ch=ch: e.scalar_tensor_tensor(
                        o, Sst[:, ch, 256 * hh:256 * hh + 256], decs[:, hh, ch - 1:ch], a, ALU.mult, ALU.add), tok, tdc)
            P.free(b, t_S)
    ob = {}
    for t, n, cc in XTILES:
        for pr in range(2):
            b = ob[t, pr] = P.take()
            for hh in (2 * pr, 2 * pr + 1):
                o = slice(256 * (hh % 2), 256 * (hh % 2) + 256)
                P.mm(ps[b][:, o], sc[:, t, 128 * hh:128 * hh + 128], vt[:, t, 256 * hh:256 * hh + 256], True, False, t_s, t_S)
                for u in range(2):
                    tok = P.mm(ps[b][64 * u:64 * u + 64, o], E3[:, hh, cc + 64 * u:cc + 64 * u + 64],
                               Sst[:, 1 + 2 * t + u, 256 * hh:256 * hh + 256], False, True)
            for hh in (2 * pr, 2 * pr + 1):
                V.do(lambda e, b=b, t=t, hh=hh: e.bn_stats(P.st[:, 4 * t + hh, 0, :], ps[b][:, 256 * (hh % 2):256 * (hh % 2) + 256]), tok)
                V.seq(lambda e, t=t, hh=hh: e.bn_aggr(mv8[:, 4 * t + hh, :], P.st[:, 4 * t + hh, 0:1, :]))
    V.seq(lambda e: e.tensor_scalar(P.rs[:, 0, 0:8], mv8[:, :, 1], LN_EPS, None, ALU.add))
    P.rsqrt(P.rs[:, 1, 0:8], P.rs[:, 0, 0:8], P.rtmp[:, 0:8])
    V.seq(lambda e: e.tensor_tensor(rt[:, 0, :], rt[:, 0, :], ngb[:, :], ALU.mult), t_rt, t_ngb)
    V.seq(lambda e: e.tensor_tensor(rt[:, 1, :], rt[:, 1, :], ngb[:, :], ALU.mult))
    on = vt
    t_vt2 = T_.last
    for t in range(2):
        for hh in range(4):
            b = ob[t, hh // 2]
            k = 4 * t + hh
            z = V.seq(lambda e, b=b, t=t, hh=hh, k=k: e.tensor_scalar(
                on[:, t, 256 * hh:256 * hh + 256], ps[b][:, 256 * (hh % 2):256 * (hh % 2) + 256],
                mv8[:, k, 0:1], P.rs[:, 1, k:k + 1], ALU.subtract, ALU.mult), t_vt2)
            if hh % 2:
                P.free(b, z)
        t_og = V.seq(lambda e, t=t: e.tensor_tensor(on[:, t, :], on[:, t, :], rt[:, t, :], ALU.mult))
    t_x = P.make_T(lambda t, k: on[:, t, 128 * k:128 * k + 128], XTILES, 8, xh, xl, t_og)

    def rows_out(key, tiles, tx):
        T_.wait(tx)
        acc = {(t, q): P.take() for t, _, _ in tiles for q in range(2)}
        for j in range(4):
            c = P.next((key, j))
            wh, wl = (c[s].rearrange("p (i n) -> p i n", i=2) for s in ("hi", "lo"))
            for i in range(2):
                k = 2 * j + i
                for t, n, cc in tiles:
                    for q in range(2):
                        tok = P.mm3(ps[acc[t, q]][:, :], xh[:, k, cc:cc + n], xl[:, k, cc:cc + n],
                                    wh[:, i, 512 * q:512 * q + 512], wl[:, i, 512 * q:512 * q + 512], k == 0, k == 7,
                                    mark=(i == 1 and t == tiles[-1][0] and q == 1))
            P.done(c, tok)
        return acc, tok

    acc, tok = rows_out("go", XTILES, t_x)
    t_ln = end_block(acc, XTILES, (1, 0), tok)
    P.dump("h2", h[:, 0:2, :], t_ln)
    t_x = P.make_T(src_h, QTILES, 8, xh, xl, t_ln)

    def router(srcs, n):
        tl = []
        o = 0
        for s, m in srcs:
            tl.append(P.load(G, rwr[:, :, o:o + m], s.rearrange("(k p) n -> p k n", p=128)))
            o += m
        tw = P.split(rwh[:, :, 0:n], rwl[:, :, 0:n], rwr[:, :, 0:n], *tl)
        bs = []
        T_.wait(tw, t_x)
        for t, _, cc in QTILES:
            b = P.take()
            for k in range(8):
                tok = P.mm3(ps[b][:, 0:n], xh[:, k, cc:cc + 128], xl[:, k, cc:cc + 128], rwh[:, k, 0:n], rwl[:, k, 0:n],
                            k == 0, k == 7)
            bs.append((b, tok))
        return bs

    def top2(t, lo, n, ready):
        L = gw[:, t, lo:lo + n]
        m8 = gw[:, t, 40:48]
        w = gw[:, t, 48:56]
        V.seq(lambda e: e.max(m8, L), ready)
        t1 = V.seq(lambda e: e.max_index(gi[:, t, :], m8, L))
        V.seq(lambda e: e.tensor_copy(w[:, 0:2], gi[:, t, 0:2]))
        td = V.seq(lambda e: e.tensor_tensor(w[:, 2:3], m8[:, 1:2], m8[:, 0:1], ALU.subtract))
        te = A.do(lambda e: e.activation(w[:, 3:4], w[:, 2:3], ACT.Exp), td)
        V.seq(lambda e: e.tensor_scalar(w[:, 4:5], w[:, 3:4], 1.0, None, ALU.add), te)
        V.seq(lambda e: e.reciprocal(w[:, 4:5], w[:, 4:5]))
        return w

    def top2_gates(t, n, w):
        io = cst[:, C_IO:C_IO + n]
        V.seq(lambda e: e.tensor_tensor(w[:, 5:6], w[:, 3:4], w[:, 4:5], ALU.mult))
        V.seq(lambda e: e.tensor_scalar(gates[:, t, 0:n], io, w[:, 0:1], w[:, 4:5], ALU.is_equal, ALU.mult))
        V.seq(lambda e: e.tensor_scalar(gw[:, t, 0:n], io, w[:, 1:2], w[:, 5:6], ALU.is_equal, ALU.mult))
        return V.seq(lambda e: e.tensor_tensor(gates[:, t, 0:n], gates[:, t, 0:n], gw[:, t, 0:n], ALU.add))

    P.phase()
    ah, al = ffn_tiles()
    y = P.ph("y", [128, 2, 1024])
    for t, (b, tok) in enumerate(router([(d["moe_router"][0], 8)], 8)):
        tc = V.seq(lambda e, t=t, b=b: e.tensor_copy(gw[:, t, 0:8], ps[b][:, 0:8]), tok)
        P.free(b, tc)
        w = top2(t, 0, 8, tc)
        t_g = top2_gates(t, 8, w)

    def experts(key, ne, F):
        for e_ in range(ne):
            acc, tok = P.ffn((key, e_), F, QTILES, 0, 256, xh, xl, ah, al, t_x)
            for (t, q), b in acc.items():
                o = y[:, t, 512 * q:512 * q + 512]
                gcol = gates[:, t, e_:e_ + 1]
                if e_ == 0:
                    z = V.do(lambda e, o=o, b=b, g=gcol: e.tensor_scalar(o, ps[b][:, :], g, None, ALU.mult), tok, t_g)
                else:
                    z = V.seq(lambda e, o=o, b=b, g=gcol: e.scalar_tensor_tensor(o, ps[b][:, :], g, o, ALU.mult, ALU.add), tok)
                P.free(b, z)
        return z

    t_y = experts("m1", 8, 3584)
    P.dump("ff1", y[:, :, :], t_y)
    t_ln = P.layer_norm(QTILES, lambda t, q: y[:, t, 512 * q:512 * q + 512], (1, 1), t_y)
    P.dump("h3", h[:, 0:2, :], t_ln)

    P.phase()
    every = [q.last for q in (T_, V, A)]
    mod = P.rest("mod", [128, 4, 1024])
    hn = P.rest("hn", [128, 2, 1024])
    bcast = lambda nm: d[nm].partition_broadcast(128)
    mod2 = P.ph("mod2", [128, 2, 1024])
    t_n1 = P.load(G, P.lng, bcast("norm1_g_2"), *every)
    crow = P.ph("crow", [8, 128])
    bada = P.ph("bada", [1, 6144])
    ccol = P.ph("ccol", [128, 8])
    cbc = P.ph("cbc", [128, 8, 128])
    ones = P.ph("ones", [1, 128])
    t_cr = P.load(G, crow[:, :], d["c_2"][0].rearrange("(k p) -> k p", p=128))
    t_ba = P.load(G, bada[:, :], d["b_ada_2"])
    V.do(lambda e: e.memset(ones[:, :], 1.0))
    t_on = V.do(lambda e: e.memset(cbc[:, :, :], 0.0))
    b = P.take()
    tok = T_.do(lambda e, b=b: e.transpose(ps[b][:, 0:8], crow[:, :], cst[0:8, C_ID:C_ID + 8]), t_cr)
    tcc = A.do(lambda e, b=b: e.activation(ccol[:, :], ps[b][:, 0:8], ACT.Silu), tok)
    P.free(b, tcc)
    t_cb = V.seq(lambda e: e.tensor_tensor(cbc[:, :, :], cbc[:, :, :], ccol[:, :].unsqueeze(2).to_broadcast([128, 8, 128]), ALU.add), tcc)
    T_.wait(t_cb, t_on, t_ba)
    for j in range(24):
        c = P.next(("ada", j))
        w = c["raw"].rearrange("p (k n) -> p k n", k=8)
        b = P.take()
        for k in range(8):
            P.mm(ps[b][:, 0:256], cbc[:, k, :], w[:, k, :], k == 0, False)
        tok = P.mm(ps[b][:, 0:256], ones[:, :], bada[:, 256 * j:256 * j + 256], False, True)
        P.done(c, tok)
        part, q = j // 4, j % 4
        dst = mod2[:, part, 256 * q:256 * q + 256] if part < 2 else mod[:, part - 2, 256 * q:256 * q + 256]
        t_md = A.do(lambda e, b=b, dst=dst, part=part: e.activation(dst, ps[b][:, 0:256], ACT.Copy,
                                                                    bias=1.0 if part in (1, 4) else 0.0), tok)
        P.free(b, t_md)

    def rms_w(dst, src, G_, n, sq, *toks):
        V.seq(lambda e: e.tensor_tensor(sq, src, src, ALU.mult), *toks)
        four = len(src.shape) == 4
        fold = (lambda a: a.rearrange("p (t h) -> p t h", t=2)) if four else (lambda a: a)
        V.seq(lambda e: e.tensor_reduce(fold(P.rs[:, 0, 0:G_]), sq, AX.X, ALU.add))
        V.seq(lambda e: e.tensor_scalar(P.rs[:, 0, 0:G_], P.rs[:, 0, 0:G_], 1.0 / n, RMS_EPS, ALU.mult, ALU.add))
        P.rsqrt(P.rs[:, 1, 0:G_], P.rs[:, 0, 0:G_], P.rtmp[:, 0:G_])
        r = fold(P.rs[:, 1, 0:G_])
        return V.seq(lambda e: e.tensor_tensor(dst, src, r.unsqueeze(len(r.shape)).to_broadcast(list(src.shape)), ALU.mult))

    def modulate(gain, scale, shift, tg, tm):
        rms_w(hn[:, :, :], h[:, 0:2, :], 2, 1024, hn[:, :, :])
        V.seq(lambda e: e.tensor_tensor(gain, gain, scale, ALU.mult), tg, tm)
        for t in range(2):
            V.seq(lambda e, t=t: e.tensor_tensor(hn[:, t, :], hn[:, t, :], gain, ALU.mult))
            z = V.seq(lambda e, t=t: e.tensor_tensor(hn[:, t, :], hn[:, t, :], shift, ALU.add))
        return z

    t_hn = modulate(P.lng, mod2[:, 1, :], mod2[:, 0, :], t_n1, t_md)
    P.dump("hh", hn[:, :, :], t_hn)
    src_n = lambda t, k: hn[:, t, 128 * k:128 * k + 128]
    t_x = P.make_T(src_n, QTILES, 8, xh, xl, t_hn)

    P.phase()
    every = [q.last for q in (T_, V, A)]
    small =P.ph("small", [128, 1344])
    t_sm = []
    off = {}
    o = 0
    for nm, n in (("mla_cq_g_2", 384), ("mla_ckv_g_2", 256), ("mla_q_g_2", 96), ("mla_k_g_2", 96), ("diff_q_g_2", 64),
                  ("diff_k_g_2", 64), ("diff_subln_g_2", 128), ("lambda_q1_2", 64), ("lambda_k1_2", 64),
                  ("lambda_q2_2", 64), ("lambda_k2_2", 64)):
        off[nm] = (o, n)
        t_sm.append(P.load(G, small[:, o:o + n], bcast(nm)))
        o += n
    sm = lambda nm: small[:, off[nm][0]:off[nm][0] + off[nm][1]]
    pj = P.ph("pj", [128, 2, 2208])
    T_.wait(t_x)
    for j in range(9):
        tokm("wi", j, QTILES, lambda t, n, j, pt, tok: A.do(
            lambda e: e.activation(pj[:, t, 256 * j:256 * j + (256 if j < 8 else 160)], pt, ACT.Copy), tok))
    t_pj = A.last
    P.dump("proj", pj[:, :, :], t_pj)
    pi = P.ph("pi", [128, 2], I32)
    t_pi0 = P.load(G, pi[:, 0:1], d["positions_2"][0, 0:128].rearrange("(p a) -> p a", a=1), *every)
    t_pi = P.load(G, pi[:, 1:2], d["positions_2"][0, 128:256].rearrange("(p a) -> p a", a=1))
    V.wait(t_pi0)
    pkb = P.ph("pkb", [128, 256], I32)
    t_pk = P.load(G, pkb[:, :], bcast("positions_2"), *every)
    ang = P.ph("ang", [128, 4, 2, 16])
    pf = P.ph("pf", [128, 2])
    V.seq(lambda e: e.tensor_copy(pf[:, :], pi[:, :]), t_pi)
    for t in range(2):
        V.seq(lambda e, t=t: e.tensor_scalar(ang[:, 0, t, :], cst[:, C_IF:C_IF + 16], pf[:, t:t + 1], None, ALU.mult))
    a0, a1, a2, a3 = (ang[:, i, :, :] for i in range(4))
    MAGIC = 12582912.0
    V.seq(lambda e: e.tensor_scalar(a1, a0, 1.0 / (2 * math.pi), MAGIC, ALU.mult, ALU.add))
    V.seq(lambda e: e.tensor_scalar(a1, a1, MAGIC, None, ALU.subtract))
    c1 = 6.28125
    c2 = float(np.float32(2 * math.pi - c1).view(np.uint32) & np.uint32(0xFFFFF000))
    c2 = float((np.array(2 * math.pi - c1, np.float32).view(np.uint32) & np.uint32(0xFFFFF000)).view(np.float32))
    c3 = 2 * math.pi - c1 - c2
    for cc in (c1, c2, c3):
        V.seq(lambda e, cc=cc: e.scalar_tensor_tensor(a0, a1, -cc, a0, ALU.mult, ALU.add))
    PI = 3.1415925
    V.seq(lambda e: e.tensor_scalar(a0, a0, PI, -PI, ALU.min, ALU.max))
    V.seq(lambda e: e.tensor_scalar(a1, a0, math.pi / 2, -2 * math.pi, ALU.is_gt, ALU.mult))
    V.seq(lambda e: e.scalar_tensor_tensor(a1, a0, math.pi / 2, a1, ALU.add, ALU.add))
    t_an = V.seq(lambda e: e.tensor_scalar(a1, a1, PI, -PI, ALU.min, ALU.max))
    A.do(lambda e: e.activation(a2, a0, ACT.Sin), t_an)
    t_cs = A.do(lambda e: e.activation(a3, a1, ACT.Sin))
    SIN, COS = a2, a3

    bias = lnt[:, 0:1536].rearrange("p (h n) -> p h n", h=4)
    rel = lnt[:, 1536:1920]
    stp = P.ph("stp", [128, 384])
    rb = P.ph("rb", [128, 128])
    dl = P.ph("dl", [128, 30, 4])
    i2 = h[:, 2, 512:1024].bitcast(I32).rearrange("p (a n) -> p a n", a=2)
    j2 = P.ph("j2", [128, 2, 2], I32)
    f2 = h[:, 2, 0:512].rearrange("p (a n) -> p a n", a=2)
    g2f = P.ph("g2f", [128, 2, 2])
    t_rb = P.load(G, rb[:, :], d["rel_bias_2"].rearrange("(a b) h -> a (b h)", a=1).partition_broadcast(128), *every)
    for dst, src, tk in ((i2, pkb, t_pk), (j2, pi, t_pi)):
        V.seq(lambda e, dst=dst, src=src: e.tensor_scalar(dst[:, 0, :], src[:, :], 12, None, ALU.arith_shift_right), tk)
        V.seq(lambda e, dst=dst, src=src: e.tensor_scalar(dst[:, 1, :], src[:, :], 4095, None, ALU.bitwise_and))
    V.seq(lambda e: e.tensor_copy(f2[:, :, :], i2[:, :, :]))
    V.seq(lambda e: e.tensor_copy(g2f[:, :, :], j2[:, :, :]))
    for t in range(2):
        n, o = (128, 0) if t == 0 else (256, 128)
        V.seq(lambda e, t=t, n=n: e.tensor_scalar(stp[:, 0:n], f2[:, 0, 0:n], g2f[:, 0, t:t + 1], 4096.0, ALU.subtract, ALU.mult))
        V.seq(lambda e, t=t, n=n, o=o: e.tensor_scalar(rel[:, o:o + n], f2[:, 1, 0:n], g2f[:, 1, t:t + 1], None, ALU.subtract))
        V.seq(lambda e, n=n, o=o: e.tensor_tensor(rel[:, o:o + n], rel[:, o:o + n], stp[:, 0:n], ALU.add))
    prev = 15
    for i, (th, bk) in enumerate(STEPS):
        V.do(lambda e, i=i, bk=bk, prev=prev: e.tensor_tensor(dl[:, i, :], rb[:, 4 * bk:4 * bk + 4], rb[:, 4 * prev:4 * prev + 4],
                                                              ALU.subtract), t_rb)
        prev = bk
    t_dl = V.last
    for hh in range(4):
        G.seq(lambda e, hh=hh: e.tensor_scalar(bias[:, hh, :], cst[:, C_AM:C_AM + 384], rb[:, 60 + hh:61 + hh], None, ALU.add),
              t_dl, t_rb)
        for i, (th, bk) in enumerate(STEPS):
            G.seq(lambda e, hh=hh, i=i, th=th: e.tensor_scalar(stp[:, :], rel[:, :], float(th), dl[:, i, hh:hh + 1],
                                                               ALU.is_ge, ALU.mult))
            t_bias = G.seq(lambda e, hh=hh: e.tensor_tensor(bias[:, hh, :], bias[:, hh, :], stp[:, :], ALU.add))
    lw = P.ph("lw", [128, 64])
    l2 = P.ph("l2", [128, 4])
    for i in range(2):
        V.seq(lambda e, i=i: e.tensor_tensor(lw[:, :], sm(f"lambda_q{i + 1}_2"), sm(f"lambda_k{i + 1}_2"), ALU.mult), *t_sm)
        tl = V.seq(lambda e, i=i: e.tensor_reduce(l2[:, i:i + 1], lw[:, :], AX.X, ALU.add))
    tl = A.do(lambda e: e.activation(l2[:, 0:2], l2[:, 0:2], ACT.Exp), tl)
    V.seq(lambda e: e.tensor_tensor(l2[:, 2:3], l2[:, 1:2], l2[:, 0:1], ALU.subtract), tl)
    V.seq(lambda e: e.tensor_scalar(l2[:, 2:3], l2[:, 2:3], -LAMBDA_INIT, None, ALU.add))
    nlam = l2[:, 2:3]

    sq = P.ph("sq", [128, 2, 768])
    qq = P.ph("qq", [128, 2, 768])
    kk = P.ph("kk", [128, 2, 768])
    vv = P.ph("vv", [128, 2, 512])

    def lat(o, n, g):
        a = pj[:, :, o:o + n]
        rms_w(a, a, 2, n, sq[:, :, 0:n], t_pj)
        for t in range(2):
            z = V.seq(lambda e, t=t: e.tensor_tensor(pj[:, t, o:o + n], pj[:, t, o:o + n], sm(g), ALU.mult))
        return z

    t1 = lat(0, 384, "mla_cq_g_2")
    t_x = P.make_T(lambda t, k: pj[:, t, 128 * k:128 * k + 128], QTILES, 3, xh, xl, t1)
    T_.wait(t_x)
    for j in range(2):
        c = P.next(("uq", j))
        wh, wl = (c[s].rearrange("p (k n) -> p k n", k=3) for s in ("hi", "lo"))
        for t, _, cc in QTILES:
            b = P.take()
            for k in range(3):
                tok = P.mm3(ps[b][:, 0:384], xh[:, k, cc:cc + 128], xl[:, k, cc:cc + 128], wh[:, k, :], wl[:, k, :], k == 0, k == 2)
            if t == 1:
                P.done(c, tok)
            t_qq = A.do(lambda e, b=b, t=t, j=j: e.activation(qq[:, t, 384 * j:384 * j + 384], ps[b][:, 0:384], ACT.Copy), tok)
            P.free(b, t_qq)
    t1 = lat(384, 256, "mla_ckv_g_2")
    t_x = P.make_T(lambda t, k: pj[:, t, 384 + 128 * k:512 + 128 * k], QTILES, 2, xh, xl, t1, T_.last)
    c = P.next("ukv")
    wh, wl = (c[s].rearrange("p (k n) -> p k n", k=2) for s in ("hi", "lo"))
    T_.wait(t_x)
    k4 = [kk[:, t, :].rearrange("p (h n) -> p h n", n=96) for t in range(2)]
    v4 = [vv[:, t, :].rearrange("p (h n) -> p h n", n=64) for t in range(2)]
    for t, _, cc in QTILES:
        for q in range(2):
            b = P.take()
            for k in range(2):
                tok = P.mm3(ps[b][:, :], xh[:, k, cc:cc + 128], xl[:, k, cc:cc + 128], wh[:, k, 512 * q:512 * q + 512],
                            wl[:, k, 512 * q:512 * q + 512], k == 0, k == 1)
            if t == 1 and q == 1:
                P.done(c, tok)
            pv = ps[b][:, :].rearrange("p (h n) -> p h n", n=128)
            A.do(lambda e, pv=pv, t=t, q=q: e.activation(k4[t][:, 4 * q:4 * q + 4, 0:64], pv[:, :, 0:64], ACT.Copy), tok)
            t_kv = A.do(lambda e, pv=pv, t=t, q=q: e.activation(v4[t][:, 4 * q:4 * q + 4, :], pv[:, :, 64:128], ACT.Copy))
            P.free(b, t_kv)
        t_kv = A.do(lambda e, t=t: e.activation(k4[t][:, :, 64:96], pj[:, t, 640:672].unsqueeze(1).to_broadcast([128, 8, 32]),
                                                ACT.Copy), t_pj)

    def head_norm(buf, G_, n, g, tok):
        a = buf.rearrange("p t (h n) -> p t h n", n=n)
        s = sq[:, :, 0:G_ * n // 2].rearrange("p t (h n) -> p t h n", n=n)
        rms_w(a, a, G_, n, s, tok)
        return V.seq(lambda e: e.tensor_tensor(a, a, sm(g).unsqueeze(1).unsqueeze(1).to_broadcast(list(a.shape)), ALU.mult))

    def rope(buf):
        v = buf.rearrange("p t (h n) -> p t h n", n=96)
        x1, x2 = v[:, :, :, 64:80], v[:, :, :, 80:96]
        s = sq[:, :, 0:512].rearrange("p t (i h n) -> p t i h n", i=4, n=16)
        for t in range(2):
            cb, sb_ = (a[:, t, :].unsqueeze(1).to_broadcast([128, 8, 16]) for a in (COS, SIN))
            for i, (x, f) in enumerate(((x1, cb), (x2, sb_), (x2, cb), (x1, sb_))):
                V.seq(lambda e, i=i, x=x, f=f, t=t: e.tensor_tensor(s[:, t, i], x[:, t], f, ALU.mult), t_cs)
            V.seq(lambda e, t=t: e.tensor_tensor(x1[:, t], s[:, t, 0], s[:, t, 1], ALU.subtract))
            z = V.seq(lambda e, t=t: e.tensor_tensor(x2[:, t], s[:, t, 2], s[:, t, 3], ALU.add))
        return z

    head_norm(qq[:, :, :], 16, 96, "mla_q_g_2", t_qq)
    t_q = rope(qq[:, :, :])
    head_norm(kk[:, :, :], 16, 96, "mla_k_g_2", t_kv)
    t_k = rope(kk[:, :, :])
    dq, dk, dv = pj[:, :, 672:1184], pj[:, :, 1184:1696], pj[:, :, 1696:2208]
    t_dq = head_norm(dq, 16, 64, "diff_q_g_2", t_pj)
    t_dk = head_norm(dk, 16, 64, "diff_k_g_2", t_pj)

    P.o2 = o2 = hn
    qT = P.ph("qT", [128, 2, 256])
    kT = P.ph("kT", [128, 2, 256])
    Sx = P.ph("Sx", [128, 2, 2, 384])
    Pt = P.ph("Pt", [128, 2, 3, 128])
    ss = P.ph("ss", [128, 2, 16])
    qk_free, S_free, Pt_free = [None, None], [None, None], [None, None]

    def to_heads(i, n, qsrc, ksrc, tq):
        b = P.take()
        for t in range(2):
            T_.do(lambda e, b=b, t=t: e.transpose(ps[b][0:n, 128 * t:128 * t + 128], qsrc(t), cst[:, C_ID:C_ID + 128]), *tq)
            tok = T_.do(lambda e, b=b, t=t: e.transpose(ps[b][0:n, 256 + 128 * t:384 + 128 * t], ksrc(t), cst[:, C_ID:C_ID + 128]))
        A.do(lambda e, b=b: e.activation(qT[0:n, i, :], ps[b][0:n, 0:256], ACT.Copy), tok, qk_free[i])
        z = A.do(lambda e, b=b: e.activation(kT[0:n, i, :], ps[b][0:n, 256:512], ACT.Copy))
        P.free(b, z)
        return z

    def scores(i, u, p0, n, scale, bm, tz, tb):
        b = P.take()
        P.mm(ps[b][:, 0:128], qT[p0:p0 + n, i, 0:128], kT[p0:p0 + n, i, 0:128], True, True, tz)
        tok = P.mm(ps[b][:, 128:384], qT[p0:p0 + n, i, 128:256], kT[p0:p0 + n, i, 0:256], True, True)
        qk_free[i] = tok
        x = Sx[:, i, u, :]
        t1 = V.do(lambda e, b=b: e.scalar_tensor_tensor(x, ps[b][:, 0:384], scale, bm, ALU.mult, ALU.add), tok, tb, S_free[i])
        P.free(b, t1)
        V.seq(lambda e: e.tensor_reduce(ss[:, u, 0:1], x[:, 0:128], AX.X, ALU.max, negate=True))
        t2 = V.seq(lambda e: e.tensor_reduce(ss[:, u, 1:2], x[:, 128:384], AX.X, ALU.max, negate=True))
        A.do(lambda e: e.activation(x[:, 0:128], x[:, 0:128], ACT.Exp, bias=ss[:, u, 0:1], accum_out=ss[:, u, 2:3]), t2)
        t3 = A.do(lambda e: e.activation(x[:, 128:384], x[:, 128:384], ACT.Exp, bias=ss[:, u, 1:2], accum_out=ss[:, u, 3:4]))
        return V.seq(lambda e: e.reciprocal(ss[:, u, 4:6], ss[:, u, 2:4]), t3)

    def probs_T(i, tp):
        b = P.take()
        for m in range(3):
            tok = T_.do(lambda e, b=b, m=m: e.transpose(ps[b][:, 128 * m:128 * m + 128], Sx[:, i, 0, 128 * m:128 * m + 128],
                                                        cst[:, C_ID:C_ID + 128]), tp)
        S_free[i] = tok
        z = A.do(lambda e, b=b: e.activation(Pt[:, i, :, :].rearrange("p m q -> p (m q)"), ps[b][:, 0:384], ACT.Copy), tok, Pt_free[i])
        P.free(b, z)
        return z

    obk = [P.take(), P.take()]

    def values(i, cols, vsrc, tz):
        P.mm(ps[obk[0]][:, cols], Pt[:, i, 0, :], vsrc(0), True, True, tz)
        P.mm(ps[obk[1]][:, cols], Pt[:, i, 1, :], vsrc(0), True, False)
        Pt_free[i] = P.mm(ps[obk[1]][:, cols], Pt[:, i, 2, :], vsrc(1), False, True)
        return Pt_free[i]

    am = cst[:, C_AM:C_AM + 384]
    for hh in range(8):
        i = hh % 2
        tz = to_heads(i, 96, lambda t, hh=hh: qq[:, t, 96 * hh:96 * hh + 96],
                      lambda t, hh=hh: kk[:, t, 96 * hh:96 * hh + 96], (t_q, t_k))
        tr = scores(i, 0, 0, 96, 96.0 ** -0.5, am, tz, None)
        x = Sx[:, i, 0, :]
        V.seq(lambda e, x=x: e.tensor_scalar(x[:, 0:128], x[:, 0:128], ss[:, 0, 4:5], None, ALU.mult))
        tp = V.seq(lambda e, x=x: e.tensor_scalar(x[:, 128:384], x[:, 128:384], ss[:, 0, 5:6], None, ALU.mult))
        tz = probs_T(i, tp)
        tok = values(i, slice(64 * hh, 64 * hh + 64), lambda t, hh=hh: v4[t][:, hh, :], tz)
    for t in range(2):
        z = A.do(lambda e, t=t, b=obk[t]: e.activation(o2[:, t, 0:512], ps[b][:, :], ACT.Copy), tok)
        P.free(obk[t], z)
    P.dump("omla", o2[:, :, 0:512], z)
    obk = [P.take(), P.take()]
    for hh in range(4):
        i = hh % 2
        tz = to_heads(i, 128, lambda t, hh=hh: dq[:, t, 128 * hh:128 * hh + 128], lambda t, hh=hh: dk[:, t, 128 * hh:128 * hh + 128],
                      (t_dq, t_dk))
        scores(i, 0, 0, 64, 0.125, bias[:, hh, :], tz, t_bias)
        scores(i, 1, 64, 64, 0.125, bias[:, hh, :], tz, t_bias)
        V.seq(lambda e: e.tensor_scalar(ss[:, 1, 4:6], ss[:, 1, 4:6], nlam, None, ALU.mult))
        for t, (a, z) in enumerate(((0, 128), (128, 384))):
            V.seq(lambda e, i=i, t=t, a=a, z=z: e.tensor_scalar(Sx[:, i, 1, a:z], Sx[:, i, 1, a:z], ss[:, 1, 4 + t:5 + t], None, ALU.mult))
            tp = V.seq(lambda e, i=i, t=t, a=a, z=z: e.scalar_tensor_tensor(Sx[:, i, 0, a:z], Sx[:, i, 0, a:z], ss[:, 0, 4 + t:5 + t],
                                                                            Sx[:, i, 1, a:z], ALU.mult, ALU.add))
        tz = probs_T(i, tp)
        tok = values(i, slice(128 * hh, 128 * hh + 128), lambda t, hh=hh: dv[:, t, 128 * hh:128 * hh + 128], tz)
    for t in range(2):
        z = A.do(lambda e, t=t, b=obk[t]: e.activation(o2[:, t, 512:1024], ps[b][:, :], ACT.Copy), tok)
        P.free(obk[t], z)
    od = sq[:, :, 0:512].rearrange("p t (h n) -> p t h n", n=128)
    od2 = qq[:, :, 0:512].rearrange("p t (h n) -> p t h n", n=128)
    V.seq(lambda e: e.tensor_copy(sq[:, :, 0:512], o2[:, :, 512:1024]), z)
    rms_w(od, od, 8, 128, od2)
    V.seq(lambda e: e.tensor_tensor(od, od, sm("diff_subln_g_2").unsqueeze(1).unsqueeze(1).to_broadcast(list(od.shape)), ALU.mult))
    t_o = V.seq(lambda e: e.tensor_scalar(o2[:, :, 512:1024], sq[:, :, 0:512], 1.0 - LAMBDA_INIT, None, ALU.mult))
    P.dump("odiff", o2[:, :, 512:1024], t_o)
    t_x = P.make_T(lambda t, k: o2[:, t, 128 * k:128 * k + 128], QTILES, 8, xh, xl, t_o)
    acc, tok = rows_out("wo", QTILES, t_x)
    for (t, q), b in acc.items():
        a = slice(512 * q, 512 * q + 512)
        z = V.do(lambda e, t=t, a=a, b=b: e.tensor_tensor(hn[:, t, a], ps[b][:, :], mod[:, 0, a], ALU.mult), tok)
        P.free(b, z)
        t_h = V.seq(lambda e, t=t, a=a: e.tensor_tensor(h[:, t, a], h[:, t, a], hn[:, t, a], ALU.add))
    P.dump("x1", h[:, 0:2, :], t_h)
    t_n2 = P.load(G, P.lng, bcast("norm2_g_2"), V.last)
    t_hn = modulate(P.lng, mod[:, 2, :], mod[:, 1, :], t_n2, t_md)
    P.dump("hh2", hn[:, :, :], t_hn)
    t_x = P.make_T(src_n, QTILES, 8, xh, xl, t_hn)

    P.phase()
    ah, al = ffn_tiles(4)
    y = P.ph("y2", [128, 2, 1024])
    br = P.ph("br", [128, 20])
    big = P.ph("big", [128, 2, 24])
    gm = P.ph("gm", [128, 2, 16], I32)
    t_br = [P.load(G, br[:, 0:4], bcast("b_rg_2"), *[q.last for q in (T_, V, A)]), P.load(G, br[:, 4:20], bcast("b_re_2"))]
    V.seq(lambda e: e.memset(big[:, :, :], -3.0e38))
    for t, (b, tok) in enumerate(router([(d["w_rg_2"][0], 4), (d["w_re_2"][0], 16)], 20)):
        gl, el = gw[:, t, 0:4], gw[:, t, 4:20]
        z = V.seq(lambda e, t=t, b=b: e.tensor_tensor(gw[:, t, 0:20], ps[b][:, 0:20], br[:, :], ALU.add), tok, *t_br)
        P.free(b, z)
        m8, w = gw[:, t, 40:48], gw[:, t, 48:64]
        V.seq(lambda e, t=t, gl=gl: e.tensor_copy(big[:, t, 16:20], gl))
        V.seq(lambda e, t=t, m8=m8: e.max(m8, big[:, t, 16:24]))
        V.seq(lambda e, t=t, m8=m8: e.max_index(gi[:, t, :], m8, big[:, t, 16:24]))
        V.seq(lambda e, t=t, w=w: e.tensor_copy(w[:, 8:9], gi[:, t, 0:1]))
        z = V.seq(lambda e, w=w, m8=m8: e.tensor_scalar(w[:, 9:10], m8[:, 0:1], -1.0, None, ALU.mult))
        z = A.do(lambda e, w=w, gl=gl: e.activation(w[:, 10:14], gl, ACT.Exp, bias=w[:, 9:10], accum_out=w[:, 14:15]), z)
        V.seq(lambda e, w=w: e.reciprocal(w[:, 15:16], w[:, 14:15]), z)
        io = cst[:, C_IO:C_IO + 4].unsqueeze(2).to_broadcast([128, 4, 4])
        V.seq(lambda e, t=t, io=io, w=w: e.tensor_scalar(gm[:, t, :].rearrange("p (g n) -> p g n", n=4), io, w[:, 8:9], None, ALU.is_equal))
        z = V.seq(lambda e, t=t, el=el: e.copy_predicated(big[:, t, 0:16], gm[:, t, :], el))
        z = V.seq(lambda e, t=t: e.tensor_copy(gw[:, t, 20:36], big[:, t, 0:16]))
        w = top2(t, 20, 16, z)
        V.seq(lambda e, t=t, w=w: e.tensor_tensor(w[:, 4:5], w[:, 4:5], gw[:, t, 63:64], ALU.mult))
        t_g = top2_gates(t, 16, w)
    t_y = experts("m2", 16, 512)
    P.dump("y2", y[:, :, :], t_y)
    for t in range(2):
        V.seq(lambda e, t=t: e.tensor_tensor(y[:, t, :], y[:, t, :], mod[:, 3, :], ALU.mult))
        z = V.seq(lambda e, t=t: e.tensor_tensor(h[:, t, :], h[:, t, :], y[:, t, :], ALU.add))
        P.pending_out.append(P.load(S, out[0, 128 * t:128 * t + 128, :], h[:, t, :], z))
    S.wait(*P.loads)
    P.phase_ctx.close()
    assert P.at == len(P.chunks)

    with P.ctx:
        block = P.ctx.enter_context(nc.Block())

        @block.sync
        def _(eng):
            S.emit(eng)

        @block.tensor
        def _(eng):
            T_.emit(eng)

        @block.vector
        def _(eng):
            V.emit(eng)

        @block.scalar
        def _(eng):
            A.emit(eng)

        @block.gpsimd
        def _(eng):
            G.emit(eng)


NAMES = ["x", "meta_tokens", "ln_gain", "ln_bias", "rg_w_in", "rg_conv_w", "rg_conv_b", "rg_w_gates", "rg_b_gates",
         "rg_lambda", "rg_w_out", "gla_w_in", "gla_w_gate_up", "gla_b_gate", "gla_norm_g", "gla_w_out", "ffn_w_in",
         "ffn_w_out", "moe_router", "moe_w_in", "moe_w_out", "c_2", "positions_2", "rel_bias_2", "w_ada_2", "b_ada_2",
         "norm1_g_2", "w_in_2", "mla_cq_g_2", "w_uq_2", "mla_ckv_g_2", "w_ukv_2", "mla_q_g_2", "mla_k_g_2",
         "diff_q_g_2", "diff_k_g_2", "lambda_q1_2", "lambda_k1_2", "lambda_q2_2", "lambda_k2_2", "diff_subln_g_2",
         "w_o_2", "norm2_g_2", "w_rg_2", "b_rg_2", "w_re_2", "b_re_2", "w_gate_2", "w_up_2", "w_down_2"]


def program(nc, inputs, dumps=None):
    arrays, d = {}, {}
    for name in NAMES:
        arrays["in_" + name] = np.ascontiguousarray(inputs[name])
    arrays["in_consts"] = const_table()
    for name in NAMES + ["consts"]:
        a = arrays["in_" + name]
        d[name] = nc.dram_tensor("in_" + name, a.shape, mybir.dt.from_np(a.dtype), kind="ExternalInput").ap()
    out = nc.dram_tensor("out_0", (1, 256, 1024), F32, kind="ExternalOutput").ap()
    build(nc, d, out, dumps)
    return arrays


def kernel(**inputs):
    import concourse.bacc as bacc
    from concourse.bass_utils import run_bass_kernel_spmd as run

    nc = bacc.Bacc("TRN2", target_bir_lowering=False, num_devices=1)
    arrays = program(nc, inputs)
    r = run(nc, [arrays], core_ids=[0])
    return r.results[0]["out_0"]
```

```python
from contextlib import ExitStack
import math

import numpy as np
import concourse.bass as bass
from concourse import mybir

F32 = mybir.dt.float32
F32R = mybir.dt.float32r
I32 = mybir.dt.int32
U32 = mybir.dt.uint32
ALU = mybir.AluOpType
ACT = mybir.ActivationFunctionType
AX = mybir.AxisListType

ALPHA = (2 * 2) ** 0.25
LN_EPS = 1e-5
RMS_EPS = 1e-6
T = 272
CW = 2048
NRAW, NSPL = 4, 3
LAMBDA_INIT = 0.8 - 0.6 * math.exp(-0.3 * 0)
STEPS = [(-90, 14), (-63, 13), (-45, 12), (-31, 11), (-22, 10), (-15, 9), (-11, 8), (-7, 7), (-6, 6), (-5, 5),
         (-4, 4), (-3, 3), (-2, 2), (-1, 1), (0, 0), (1, 17), (2, 18), (3, 19), (4, 20), (5, 21), (6, 22), (7, 23),
         (8, 24), (12, 25), (16, 26), (23, 27), (32, 28), (46, 29), (64, 30), (91, 31)]
TILES = [(2, 16, 0), (0, 128, 16), (1, 128, 144)]
XTILES = [(0, 128, 16), (1, 128, 144)]
QTILES = [(0, 128, 0), (1, 128, 128)]
C_ID, C_CM, C_SM, C_AM, C_IF, C_UP, C_IO, C_END = 0, 128, 256, 528, 912, 928, 1056, 1312


def const_table():
    c = np.zeros((128, C_END), np.float32)
    c[:, C_ID:C_ID + 128] = np.eye(128, dtype=np.float32)
    s, q = np.arange(128)[:, None], np.arange(128)[None, :]
    c[:, C_CM:C_CM + 128] = (s <= q) & (s // 64 == q // 64)
    m = np.ones(T, np.float32)
    m[[0, 16, 80, 144, 208]] = 0.0
    c[:, C_SM:C_SM + T] = m
    c[:64, C_AM + 64:C_AM + 128] = -1e30
    c[:64, C_AM + 128 + 192:C_AM + 384] = -1e30
    c[:, C_UP:C_UP + 128] = s < q
    c[:, C_IO:C_IO + 256] = np.arange(256, dtype=np.float32)
    c[:, C_IF:C_IF + 16] = np.float32(10000.0) ** (-np.arange(16, dtype=np.float32) / np.float32(16))
    return c


class Queue:

    def __init__(self, sem):
        self.sem, self.n, self.items, self.seen = sem, 0, [], {}

    def wait(self, *toks):
        for tok in toks:
            if tok is None:
                continue
            sem, v = tok
            if self.seen.get(sem.name, 0) < v:
                self.seen[sem.name] = v
                self.items.append((None, sem, v))

    def run(self, f, *toks):
        self.wait(*toks)
        self.items.append((f, None, 0))

    def do(self, f, *toks):
        self.wait(*toks)
        self.n += 1
        self.items.append((f, self.sem, 1))
        return (self.sem, self.n)

    def seq(self, f, *toks):
        return self.do(f, self.last, *toks)

    def dma(self, f, sem, count, *toks):
        self.wait(*toks)
        count[0] += 16
        self.items.append((f, sem, 16))
        return (sem, count[0])

    @property
    def last(self):
        return (self.sem, self.n) if self.n else None

    def begin_if(self, flag, sem):
        self.items.append(("if", flag, 0))
        self.outer = (self.sem, self.n, dict(self.seen))
        self.sem, self.n = sem, 0

    def end_if(self):
        self.items.append(("end", None, 0))
        self.sem, self.n, self.seen = self.outer

    def emit(self, eng):
        guard = None
        for f, sem, v in self.items:
            if f is None:
                eng.wait_ge(sem, v)
            elif f == "if":
                guard = eng.If(eng.value_load(sem, min_val=0, max_val=1) != 0)
                guard.__enter__()
            elif f == "end":
                guard.__exit__(None, None, None)
            elif sem is None:
                f(eng)
            else:
                f(eng).then_inc(sem, v)


class Program:
    def __init__(self, nc, d, out, dumps=None):
        self.nc, self.d, self.out, self.dumps = nc, d, out, dumps
        self.ctx = ExitStack()
        self.T = Queue(self.sem("s_pe"))
        self.V = Queue(self.sem("s_dve"))
        self.A = Queue(self.sem("s_act"))
        self.G = Queue(self.sem("s_pool"))
        self.S = Queue(self.sem("s_sp"))
        self.nsem = 0
        self.n_phase = 0
        self.phase_ctx = None
        self.pending_out = []

    def sem(self, name):
        return self.ctx.enter_context(self.nc.semaphore(name))

    def sb(self, name, shape, dt=F32):
        return self.ctx.enter_context(self.nc.sbuf_tensor(name, shape, dt))

    def ph(self, name, shape, dt=F32):
        return self.phase_ctx.enter_context(self.nc.sbuf_tensor(f"{name}_{self.n_phase}", shape, dt))

    def phase(self):
        if self.phase_ctx is not None:
            self.phase_ctx.close()
            lasts = [q.last for q in (self.T, self.V, self.A, self.G)]
            for q in (self.T, self.V, self.A, self.G):
                q.wait(*lasts, *self.loads)
        self.loads = []
        self.n_phase += 1
        self.phase_ctx = ExitStack()

    def rest(self, name, shape, dt=F32):
        return self.ctx.enter_context(self.nc.sbuf_tensor(name, shape, dt))

    def load(self, q, dst, src, *toks):
        self.nsem += 1
        sem = self.sem(f"s_ld{self.nsem}")
        tok = q.dma(lambda e: e.dma_start(dst, src), sem, [0], *toks)
        self.loads.append(tok)
        return tok

    def dump(self, name, ap, *toks):
        if self.dumps is not None:
            o = self.nc.dram_tensor("dbg_" + name, ap.shape, F32, kind="ExternalOutput").ap()
            self.dumps.append("dbg_" + name)
            t = self.load(self.S, o, ap, *toks)
            for q in (self.T, self.V, self.A, self.G):
                q.wait(t)

    def banks_init(self):
        self.ps = [self.ctx.enter_context(self.nc.psum_tensor(f"ps{i}", [128, 512], F32)) for i in range(8)]
        self.bank_free = [[] for _ in range(8)]
        self.bank_at = 0

    def take(self):
        i = self.bank_at
        while self.bank_free[i] is None:
            i = (i + 1) % 8
        self.bank_at = (i + 1) % 8
        self.T.wait(*self.bank_free[i])
        self.bank_free[i] = None
        return i

    def free(self, i, *toks):
        self.bank_free[i] = list(toks)

    def stream_init(self):
        self.raw = self.sb("raw", [128, NRAW, CW], F32)
        self.whi = self.sb("whi", [128, NSPL, CW], F32R)
        self.wlo = self.sb("wlo", [128, NSPL, CW], F32R)
        self.s_raw = [self.sem(f"s_raw{i}") for i in range(NRAW)]
        self.n_raw = [[0] for _ in range(NRAW)]
        self.chunks = []
        self.at = 0
        self.n_loaded = 0
        self.n_split = 0
        self.spl_next = 0
        self.raw_free = [None] * NRAW
        self.spl_free = [None] * NSPL
        self.raw_busy = [False] * NRAW
        self.spl_busy = [False] * NSPL
        self.fence = 0

    def chunk(self, key, rows, n, pieces, split=True, zero=False):
        self.chunks.append(dict(key=key, rows=rows, n=n, pieces=pieces, split=split, zero=zero))

    def pump(self):
        go = True
        while go:
            go = False
            i = self.n_loaded
            if i < self.fence and not self.raw_busy[i % NRAW]:
                c, k = self.chunks[i], i % NRAW
                self.raw_busy[k] = True
                slot = self.raw[0:c["rows"], k, 0:c["n"]]
                before = [self.raw_free[k]]
                if c["zero"]:
                    before = [self.G.do(lambda e, s=slot: e.memset(s, 0.0), *before)]
                for dst, src in c["pieces"](slot):
                    tok = self.S.dma(lambda e, a=dst, b=src: e.dma_start(a, b), self.s_raw[k], self.n_raw[k], *before)
                c["raw"], c["in"], c["k"] = slot, tok, k
                self.n_loaded += 1
                go = True
            i = self.n_split
            if i < self.n_loaded:
                c = self.chunks[i]
                if not c["split"]:
                    self.n_split += 1
                    go = True
                    continue
                s = self.spl_next
                if not self.spl_busy[s]:
                    self.spl_busy[s] = True
                    self.spl_next = (s + 1) % NSPL
                    hi = self.whi[0:c["rows"], s, 0:c["n"]]
                    lo = self.wlo[0:c["rows"], s, 0:c["n"]]
                    t1 = self.A.do(lambda e, h=hi, r=c["raw"]: e.activation(h, r, ACT.Copy), c["in"], self.spl_free[s])
                    t2 = self.V.do(lambda e, l=lo, h=hi, r=c["raw"]:
                                   e.tensor_tensor(l, r, h.bitcast(F32), ALU.subtract), t1, self.spl_free[s])
                    c["hi"], c["lo"], c["s"], c["ready"] = hi, lo, s, t2
                    self.raw_free[c["k"]] = t2
                    self.raw_busy[c["k"]] = False
                    self.n_split += 1
                    go = True

    def next(self, key):
        c = self.chunks[self.at]
        assert c["key"] == key, (c["key"], key)
        self.at += 1
        self.pump()
        self.T.wait(c["ready"] if c["split"] else c["in"])
        return c

    def done(self, c, tok):
        if c["split"]:
            self.spl_free[c["s"]] = tok
            self.spl_busy[c["s"]] = False
        else:
            self.raw_free[c["k"]] = tok
            self.raw_busy[c["k"]] = False
        self.pump()

    def begin_if(self, name, flag, chunks, *toks):
        qs = (self.T, self.V, self.A, self.G, self.S)
        lasts = [q.last for q in qs]
        for q in qs:
            q.wait(*lasts, *toks)
            q.begin_if(flag, self.sem(f"s_{name}_{q.sem.name}"))
        assert not any(self.raw_busy) and not any(self.spl_busy) and None not in self.bank_free
        self.kept = (self.chunks, self.at, self.n_loaded, self.n_split, self.spl_next, self.s_raw, self.n_raw,
                     list(self.raw_free), list(self.spl_free), list(self.bank_free), self.bank_at, self.fence)
        self.chunks, self.at, self.n_loaded, self.n_split, self.fence = chunks, 0, 0, 0, len(chunks)
        self.s_raw = [self.sem(f"s_{name}_raw{i}") for i in range(NRAW)]
        self.n_raw = [[0] for _ in range(NRAW)]
        self.raw_free, self.spl_free, self.bank_free = [None] * NRAW, [None] * NSPL, [[] for _ in range(8)]

    def end_if(self):
        qs = (self.T, self.V, self.A, self.G, self.S)
        assert self.at == len(self.chunks)
        lasts = [q.last for q in qs]
        for q in qs:
            q.wait(*lasts)
            q.end_if()
        (self.chunks, self.at, self.n_loaded, self.n_split, self.spl_next, self.s_raw, self.n_raw,
         self.raw_free, self.spl_free, self.bank_free, self.bank_at, self.fence) = self.kept

    def mm3(self, out, lh, ll, rh, rl, start, stop, mark=False):
        self.T.run(lambda e: e.matmul(out, lh, rh, start=start, stop=False))
        self.T.run(lambda e: e.matmul(out, lh, rl, start=False, stop=False))
        f = lambda e: e.matmul(out, ll, rh, start=False, stop=stop)
        if stop or mark:
            return self.T.do(f)
        self.T.run(f)

    def mm(self, out, l, r, start, stop, *toks):
        f = lambda e: e.matmul(out, l, r, start=start, stop=stop)
        if stop:
            return self.T.do(f, *toks)
        self.T.run(f, *toks)

    def split(self, hi, lo, src, *toks):
        t1 = self.A.do(lambda e: e.activation(hi, src, ACT.Copy), *toks)
        t2 = self.V.do(lambda e: e.tensor_tensor(lo, src, hi.bitcast(F32), ALU.subtract), t1)
        return t2

    def make_T(self, src, tiles, nk, hi, lo, *toks):
        idn = self.cst
        tok = None
        c0 = min(c for _, _, c in tiles)
        c1 = max(c + n for _, n, c in tiles)
        for k in range(nk):
            b = self.take()
            for t, n, c in tiles:
                a = src(t, k)
                f = lambda e, o=self.ps[b][:, c:c + n], a=a, n=n: e.transpose(o, a, idn[0:n, C_ID:C_ID + n])
                tt = self.T.do(f, *toks)
            tok = self.split(hi[:, k, c0:c1], lo[:, k, c0:c1], self.ps[b][:, c0:c1], tt)
            self.free(b, tok)
        return tok

    def rsqrt(self, y, x, tmp, *toks):
        V = self.V
        V.seq(lambda e: e.tensor_scalar(y.bitcast(I32), x.bitcast(I32), 1, None, ALU.logical_shift_right), *toks)
        V.seq(lambda e: e.tensor_scalar(y.bitcast(I32), y.bitcast(I32), -1.0, 1597463007.0, ALU.mult, ALU.add))
        V.seq(lambda e: e.tensor_scalar(x, x, 0.5, None, ALU.mult))
        for _ in range(4):
            V.seq(lambda e: e.tensor_tensor(tmp, y, y, ALU.mult))
            V.seq(lambda e: e.tensor_tensor(tmp, tmp, x, ALU.mult))
            t = V.seq(lambda e: e.scalar_tensor_tensor(y, tmp, 1.5, y, ALU.subtract, ALU.mult))
        return t

    def layer_norm(self, tiles, src, gi, *toks):
        V, h = self.V, self.h
        i, j = gi
        tg = self.load(self.G, self.lng[:, :], self.d["ln_gain"][i, j:j + 1, :].partition_broadcast(128), self.ln_free)
        tb = self.load(self.G, self.lnb[:, :], self.d["ln_bias"][i, j:j + 1, :].partition_broadcast(128), self.ln_free)
        st, mv, rs, tmp = self.st, self.mv, self.rs, self.rtmp
        V.seq(lambda e: e.memset(mv[:, :, :], 1.0))
        read = None
        for t, n, _ in tiles:
            for q in range(2):
                a = h[0:n, t, q * 512:(q + 1) * 512]
                read = V.do(lambda e, a=a, s=src(t, q): e.scalar_tensor_tensor(a, a, ALPHA, s, ALU.mult, ALU.add), *toks)
        self.ln_read = read
        for t, n, _ in tiles:
            for q in range(2):
                V.seq(lambda e, a=h[0:n, t, q * 512:(q + 1) * 512], o=st[0:n, t, q, :]: e.bn_stats(o, a))
        for t, n, _ in tiles:
            V.seq(lambda e, o=mv[0:n, t, :], a=st[0:n, t, :, :]: e.bn_aggr(o, a))
        V.seq(lambda e: e.tensor_scalar(rs[:, 0, 0:3], mv[:, :, 1], LN_EPS, None, ALU.add))
        self.rsqrt(rs[:, 1, 0:3], rs[:, 0, 0:3], tmp[:, 0:3])
        for t, n, _ in tiles:
            a = h[0:n, t, :]
            V.seq(lambda e, a=a, n=n, t=t: e.tensor_scalar(a, a, mv[0:n, t, 0:1], rs[0:n, 1, t:t + 1],
                                                            ALU.subtract, ALU.mult))
            V.seq(lambda e, a=a, n=n: e.tensor_tensor(a, a, self.lng[0:n, :], ALU.mult), tg)
            self.ln_free = V.seq(lambda e, a=a, n=n: e.tensor_tensor(a, a, self.lnb[0:n, :], ALU.add), tb)
        return self.ln_free

    def plan_ffn(self, key, wg, wu, wd, F):
        for j in range(F // 256):
            for nm, w in (("g", wg), ("u", wu)):
                self.chunk((key, nm, j), 128, CW, lambda s, w=w, j=j: [
                    (s.rearrange("p (k n) -> p k n", k=8),
                     w[:, 256 * j:256 * j + 256].rearrange("(k p) n -> p k n", p=128))])
        for j in range(F // 256):
            self.chunk((key, "d", j), 128, CW, lambda s, j=j: [
                (s.rearrange("p (i n) -> p i n", i=2),
                 wd[256 * j:256 * j + 256, :].rearrange("(i p) n -> p i n", p=128))])

    def moe_order(self, ne, F):
        if F > 512:
            return [(x, e_) for e_ in range(ne) for x in "ud"]
        o = [("u", 0)]
        for e_ in range(ne):
            o += [("u", e_ + 1)] * (e_ + 1 < ne) + [("d", e_)]
        return o

    def plan_moe(self, key, ne, F, f):
        for what, e_ in self.moe_order(ne, F):
            wg, wu, wd = f(e_)
            if what == "u":
                for j in range(F // 512):
                    for nm, w in (("g", wg), ("u", wu)):
                        for kh in range(2):
                            self.chunk((key, e_, nm, j, kh), 128, CW, lambda s, w=w, j=j, kh=kh: [
                                (s.rearrange("p (k n) -> p k n", k=4),
                                 w[512 * kh:512 * kh + 512, 512 * j:512 * j + 512].rearrange("(k p) n -> p k n", p=128))])
            else:
                for j in range(F // 256):
                    self.chunk((key, e_, "d", j), 128, CW, lambda s, j=j, wd=wd: [
                        (s.rearrange("p (i n) -> p i n", i=2),
                         wd[256 * j:256 * j + 256, :].rearrange("(i p) n -> p i n", p=128))])

    def moe_tiles(self, F):
        w = dict(hh=self.ph("hh", [128, 2, 1024], F32R), hl=self.ph("hl", [128, 2, 1024], F32R),
                 ah=self.ph("ah", [128, max(F // 128, 8), 128], F32R), al=self.ph("al", [128, max(F // 128, 8), 128], F32R),
                 sg=self.ph("sg", [128, 2, 512]), xg=self.xh, xgl=self.xl, sel=self.ph("sel", [128, 2, 2, 128], F32R),
                 selT=self.ph("selT", [128, 3, 2, 128], F32R), gs=self.ph("gs", [128, 3]),
                 yh=self.ph("yh", [128, 1024], F32R), yl=self.ph("yl", [128, 1024], F32R),
                 y=self.ph("y", [128, 2, 1024]), rk=self.ph("rk", [128, 2, 16]), one=self.ph("one", [128, 128]),
                 cnt=self.ph("cnt", [128, 2]), flag=self.ph("flag", [128, 1], I32))
        return w

    def moe_ranks(self, w, ne, masks, src, tm, tsrc):
        V, T_, cst = self.V, self.T, self.cst
        for t in range(2):
            ts = self.split(w["hh"][:, t, :], w["hl"][:, t, :], src(t), tsrc)
        t1 = V.do(lambda e: e.memset(w["one"][:, :], 1.0))
        b = self.take()
        p = self.ps[b]
        up = cst[:, C_UP:C_UP + 128]
        self.mm(p[:, 0:ne], up, masks[:, 0, 0:ne], True, True, tm, t1)
        self.mm(p[:, 16:16 + ne], up, masks[:, 1, 0:ne], True, False)
        self.mm(p[:, 16:16 + ne], w["one"][:, :], masks[:, 0, 0:ne], False, True)
        self.mm(p[:, 32:32 + ne], w["one"][:, :], masks[:, 0, 0:ne], True, False)
        tok = self.mm(p[:, 32:32 + ne], w["one"][:, :], masks[:, 1, 0:ne], False, True)
        V.do(lambda e: e.tensor_copy(w["rk"][:, :, 0:ne], p[:, 0:32].rearrange("p (t n) -> p t n", t=2)[:, :, 0:ne]), tok)
        V.do(lambda e: e.tensor_reduce(w["cnt"][:, 0:1], p[:, 32:32 + ne], AX.X, ALU.max))
        tf = V.seq(lambda e: e.tensor_scalar(w["flag"][:, :], w["cnt"][:, 0:1], 128.0, None, ALU.is_gt))
        self.free(b, tf)
        return tf, ts

    def moe_round(self, r, key, ne, F, w, masks, gates, ready):
        V, A, T_, cst, ps = self.V, self.A, self.T, self.cst, self.ps
        Y = {(t, q): self.take() for t in range(2) for q in range(2)}
        nf, nj = F // 128, F // 512
        nb = 2 if F == 512 else 1
        st = dict(act=[None] * nb, sel=[None, None], selT=[None] * 3, xg=[None, None], sg=[None, None], yh=None)
        got, turned, jobs = {}, {}, []
        at = dict(step=0, sg=0, due=0)

        def step(force=False):
            at["step"] += 1
            for i, (due, f) in enumerate(jobs):
                if force or due <= at["step"]:
                    jobs.pop(i)
                    f()
                    return

        def later(f, n=1):
            jobs.append((at["step"] + n, f))

        def gather(e_):
            u, u3 = e_ % 2, e_ % 3
            sel, selT, gs = w["sel"][:, u], w["selT"][:, u3], w["gs"][:, u3:u3 + 1]
            for t in range(2):
                ts = V.do(lambda e, t=t: e.tensor_scalar(sel[:, t, :], cst[:, C_IO + 128 * r:C_IO + 128 * r + 128],
                                                         w["rk"][:, t, e_:e_ + 1], masks[:, t, e_:e_ + 1],
                                                         ALU.is_equal, ALU.mult), st["sel"][u], *ready)

            def turn_sel():
                b = self.take()
                for t in range(2):
                    T_.run(lambda e, t=t: e.transpose(ps[b][:, 128 * t:128 * t + 128], sel[:, t, :].bitcast(F32),
                                                      cst[:, C_ID:C_ID + 128]), ts)
                for t in range(2):
                    tok = self.mm(ps[b][:, 256:257], sel[:, t, :].bitcast(F32), gates[:, t, e_:e_ + 1], t == 0, t == 1)
                A.do(lambda e: e.activation(selT.rearrange("p t n -> p (t n)"), ps[b][:, 0:256], ACT.Copy), tok, st["selT"][u3])
                got[e_] = [A.do(lambda e: e.activation(gs, ps[b][:, 256:257], ACT.Copy))]
                self.free(b, got[e_][0])

            def take_part(q, src, dst, eng):
                b = self.take()
                for k in range(4):
                    for t in range(2):
                        f = lambda e, b=b, k=k, t=t: e.matmul(
                            ps[b][:, 128 * k:128 * k + 128], src[:, t, 128 * (4 * q + k):128 * (4 * q + k) + 128],
                            sel[:, t, :], start=t == 0, stop=t == 1)
                        if k == 3 and t == 1:
                            tok = T_.do(f)
                        else:
                            T_.run(f)
                o = dst[:, 4 * q:4 * q + 4, 128 * u:128 * u + 128]
                x = ps[b][:, :].rearrange("p (k n) -> p k n", k=4)
                if eng is A:
                    z = A.do(lambda e: e.activation(o, x, ACT.Copy), tok, st["xg"][u])
                else:
                    z = V.do(lambda e: e.tensor_copy(o, x), tok, st["xg"][u])
                self.free(b, z)
                got[e_].append(z)
                st["sel"][u] = tok

            n = 1 if nb == 2 else 4
            later(turn_sel, n)
            for q in range(2):
                fs = [lambda q=q: take_part(q, w["hh"], w["xg"], A), lambda q=q: take_part(q, w["hl"], w["xgl"], A if nb == 1 else V)]
                for f in fs if nb == 1 else [lambda fs=fs: [f() for f in fs]]:
                    later(f, n)

        def turn(e_, j, ta_, u):
            b = self.take()
            for i in range(4):
                tok = T_.do(lambda e, i=i: e.transpose(ps[b][:, 128 * i:128 * i + 128], w["sg"][:, u, 128 * i:128 * i + 128],
                                                       cst[:, C_ID:C_ID + 128]), ta_)
            st["sg"][u] = tok
            f = nf * (e_ % nb) + 4 * j
            o = [w[n][:, f:f + 4, :].rearrange("p k n -> p (k n)") for n in ("ah", "al")]
            ts = self.split(o[0], o[1], ps[b][:, :], tok, st["act"][e_ % nb])
            self.free(b, ts)
            turned[e_, j] = ts

        def scatter(e_, D, tok):
            while at["due"]:
                step(True)
            at["due"] = 2
            u = e_ % 3
            gs = w["gs"][:, u:u + 1]
            for q in range(2):
                o = slice(512 * q, 512 * q + 512)
                ta = A.do(lambda e, q=q, o=o: e.activation(w["yh"][:, o], ps[D[q]][:, :], ACT.Copy, scale=gs), tok, st["yh"])
                ty = V.do(lambda e, q=q, o=o: e.scalar_tensor_tensor(w["yl"][:, o], ps[D[q]][:, :], gs, w["yh"][:, o].bitcast(F32),
                                                                     ALU.mult, ALU.subtract), ta, st["yh"])
                self.free(D[q], ty)

            def products(t):
                T_.wait(ty)
                for q in range(2):
                    for n in ("yh", "yl"):
                        f = lambda e, t=t, q=q, n=n: e.matmul(
                            ps[Y[t, q]][:, :], w["selT"][:, u, t, :], w[n][:, 512 * q:512 * q + 512],
                            start=(e_ == 0 and n == "yh"), stop=(e_ == ne - 1 and n == "yl"))
                        if q == 1 and n == "yl":
                            z = T_.do(f)
                        else:
                            T_.run(f)
                if t == 1:
                    st["yh"] = st["selT"][u] = z
                at["z"] = z
                at["due"] -= 1
            later(lambda: products(0), 2)
            later(lambda: products(1), 2)

        def up(e_):
            u = e_ % 2
            while len(got.get(e_, ())) < 5:
                step(True)
            T_.wait(*got[e_])
            if e_ + 1 < ne:
                gather(e_ + 1)
            for j in range(nj):
                for nm in "gu":
                    b = self.take()
                    for kh in range(2):
                        c = self.next((key, e_, nm, j, kh))
                        wh, wl = (c[x].rearrange("p (k n) -> p k n", k=4) for x in ("hi", "lo"))
                        for k in range(4):
                            kk = 4 * kh + k
                            tok = self.mm3(ps[b][:, :], w["xg"][:, kk, 128 * u:128 * u + 128],
                                           w["xgl"][:, kk, 128 * u:128 * u + 128], wh[:, k, :], wl[:, k, :],
                                           kk == 0, kk == 7, mark=(k == 3))
                        if kh == 1 and nm == "g":
                            v = at["sg"] % 2
                            at["sg"] += 1
                            g = w["sg"][:, v, :]
                            t1 = A.do(lambda e, g=g, b=b: e.activation(g, ps[b][:, :], ACT.Silu), tok, st["sg"][v])
                            self.free(b, t1)
                        elif kh == 1:
                            t2 = V.do(lambda e, g=g, b=b: e.tensor_tensor(g, g, ps[b][:, :], ALU.mult), t1, tok)
                            self.free(b, t2)
                            jobs.insert(0, (at["step"] + 2, lambda e_=e_, j=j, t2=t2, v=v: turn(e_, j, t2, v)))
                        self.done(c, tok)
                        step()
            st["xg"][u] = tok

        def down(e_):
            o = nf * (e_ % nb)
            D = [self.take() for _ in range(2)]
            for j in range(F // 256):
                while (e_, j // 2) not in turned:
                    step(True)
                T_.wait(turned[e_, j // 2])
                c = self.next((key, e_, "d", j))
                wh, wl = (c[x].rearrange("p (i n) -> p i n", i=2) for x in ("hi", "lo"))
                for i in range(2):
                    f = 2 * j + i
                    for q in range(2):
                        tok = self.mm3(ps[D[q]][:, :], w["ah"][:, o + f, :], w["al"][:, o + f, :], wh[:, i, 512 * q:512 * q + 512],
                                       wl[:, i, 512 * q:512 * q + 512], f == 0, f == nf - 1, mark=(i == 1 and q == 1))
                if j == F // 256 - 1:
                    st["act"][e_ % nb] = tok
                    scatter(e_, D, tok)
                self.done(c, tok)
                step()

        gather(0)
        for what, e_ in self.moe_order(ne, F):
            (up if what == "u" else down)(e_)
        while jobs:
            step(True)
        for (t, q), b in Y.items():
            o = w["y"][:, t, 512 * q:512 * q + 512]
            if r == 0:
                z = V.do(lambda e, o=o, b=b: e.tensor_copy(o, ps[b][:, :]), at["z"])
            else:
                z = V.do(lambda e, o=o, b=b: e.tensor_tensor(o, o, ps[b][:, :], ALU.add), at["z"])
            self.free(b, z)
        return z

    def moe(self, key, ne, F, w, masks, gates, src, tm, tsrc, again):
        tf, ts = self.moe_ranks(w, ne, masks, src, tm, tsrc)
        z = self.moe_round(0, key, ne, F, w, masks, gates, (tf, ts))
        self.begin_if(key, w["flag"][0:1, 0:1], again, tf)
        self.moe_round(1, key, ne, F, w, masks, gates, ())
        self.end_if()
        return z

    def ffn(self, key, F, tiles, c0, n, xh, xl, ah, al, tx):
        V, A, T_ = self.V, self.A, self.T
        self.T.wait(tx)
        ta = None
        for j in range(F // 256):
            bs = {}
            for nm in "gu":
                c = self.next((key, nm, j))
                wh = c["hi"].rearrange("p (k n) -> p k n", k=8)
                wl = c["lo"].rearrange("p (k n) -> p k n", k=8)
                for i in range(2):
                    b = self.take()
                    for k in range(8):
                        tok = self.mm3(self.ps[b][:, 0:n], wh[:, k, i * 128:i * 128 + 128], wl[:, k, i * 128:i * 128 + 128],
                                       xh[:, k, c0:c0 + n], xl[:, k, c0:c0 + n], k == 0, k == 7)
                    bs[nm, i] = (b, tok)
                self.done(c, tok)
            for i in range(2):
                f = 2 * j + i
                bg, tg = bs["g", i]
                bu, tu = bs["u", i]
                z = self.sg_at
                self.sg_at = (z + 1) % 4
                g = self.sg[:, z, 0:n]
                t1 = A.do(lambda e, g=g, b=bg: e.activation(g, self.ps[b][:, 0:n], ACT.Silu), tg, self.sg_free[z])
                self.free(bg, t1)
                t2 = V.do(lambda e, g=g, b=bu: e.tensor_tensor(g, g, self.ps[b][:, 0:n], ALU.mult), t1, tu)
                self.free(bu, t2)
                ta = self.split(ah[:, f, 0:n], al[:, f, 0:n], g, t2, self.act_free)
                self.sg_free[z] = ta
        acc = {(t, q): self.take() for t, _, _ in tiles for q in range(2)}
        self.T.wait(ta)
        nf = F // 128
        for j in range(F // 256):
            c = self.next((key, "d", j))
            wh = c["hi"].rearrange("p (i n) -> p i n", i=2)
            wl = c["lo"].rearrange("p (i n) -> p i n", i=2)
            for i in range(2):
                f = 2 * j + i
                for t, nt, cc in tiles:
                    for q in range(2):
                        o = self.ps[acc[t, q]][0:nt, :]
                        a = slice(cc - c0, cc - c0 + nt)
                        tok = self.mm3(o, ah[:, f, a], al[:, f, a], wh[:, i, q * 512:q * 512 + 512],
                                       wl[:, i, q * 512:q * 512 + 512], f == 0, f == nf - 1,
                                       mark=(i == 1 and t == tiles[-1][0] and q == 1))
            self.done(c, tok)
        self.act_free = tok
        return acc, tok


def build(nc, d, out, dumps=None):
    P = Program(nc, d, out, dumps)
    T_, V, A, G, S = P.T, P.V, P.A, P.G, P.S
    P.loads = []
    P.banks_init()
    ps = P.ps
    P.cst = cst = P.sb("cst", [128, C_END])
    P.xh = xh = P.sb("xh", [128, 8, T], F32R)
    P.xl = xl = P.sb("xl", [128, 8, T], F32R)
    P.h = h = P.sb("h", [128, 3, 1024])
    lnt = P.sb("lnt", [128, 2048])
    P.lng, P.lnb = lnt[:, 0:1024], lnt[:, 1024:2048]
    P.st = P.sb("st", [128, 8, 2, 6])
    P.mv = P.sb("mv", [128, 3, 2])
    P.rs = P.sb("rs", [128, 2, 32])
    P.rtmp = P.sb("rtmp", [128, 32])
    rwr = P.sb("rwr", [128, 8, 32])
    rwh = P.sb("rwh", [128, 8, 32], F32R)
    rwl = P.sb("rwl", [128, 8, 32], F32R)
    gates = P.sb("gates", [128, 2, 16])
    masks = P.sb("masks", [128, 2, 16])
    gw = P.sb("gw", [128, 2, 64])
    gi = P.sb("gi", [128, 2, 8], U32)
    P.ln_free = None
    P.act_free = None
    P.stream_init()

    w_rg, w_ro = d["rg_w_in"][0], d["rg_w_out"][0]

    def plan_rg(key, off):
        for j in range(6):
            P.chunk((key, j), 128, 8 * 224, lambda s, j=j: [
                (s.rearrange("p (k n) -> p k n", k=8),
                 w_rg[:, off + 224 * j:off + 224 * j + 224].rearrange("(k p) n -> p k n", p=128))])

    plan_rg("xr", 1344)
    wgt = d["rg_w_gates"][0]
    for j in range(4):
        def pieces(s, j=j):
            v = s.rearrange("p (g k n) -> p g k n", g=2, k=3)
            a, b = wgt[:, 2 * j].rearrange("g c n -> c g n"), wgt[:, 2 * j + 1].rearrange("g c n -> c g n")
            return [(v[0:112, :, 0, 0:168], a[0:112]), (v[0:56, :, 1, 0:168], a[112:168]),
                    (v[56:112, :, 1, 168:336], b[0:56]), (v[0:112, :, 2, 168:336], b[56:168])]
        P.chunk(("gt", j), 112, 2 * 3 * 336, pieces, zero=True)
    plan_rg("gb", 0)
    for j in range(6):
        P.chunk(("ro", j), 112, CW, lambda s, j=j: [
            (s.rearrange("p (i n) -> p i n", i=2),
             w_ro[224 * j:224 * j + 224, :].rearrange("(i p) n -> p i n", p=112))])
    P.plan_ffn("ffn", d["ffn_w_in"][0][:, 0:3584], d["ffn_w_in"][0][:, 3584:7168], d["ffn_w_out"][0], 3584)
    w_gl = d["gla_w_in"][0]
    P.chunk("gz", 128, 128, lambda s: [(s.rearrange("p (k n) -> p k n", k=8),
                                        w_gl[:, 3072:3088].rearrange("(k p) n -> p k n", p=128))])

    def plan_cols(key, w, off, m, wd=256):
        for j in range(m):
            P.chunk((key, j), 128, 8 * wd, lambda s, j=j: [
                (s.rearrange("p (k n) -> p k n", k=8),
                 w[:, off + wd * j:off + wd * j + wd].rearrange("(k p) n -> p k n", p=128))])

    def plan_rows(key, w, m):
        for j in range(m):
            P.chunk((key, j), 128, CW, lambda s, j=j: [
                (s.rearrange("p (i n) -> p i n", i=2),
                 w[256 * j:256 * j + 256, :].rearrange("(i p) n -> p i n", p=128))])

    plan_cols("gk", w_gl, 512, 2)
    plan_cols("gq", w_gl, 0, 2)
    plan_cols("gv", w_gl, 1024, 4)
    plan_cols("gr", w_gl, 2048, 4)
    plan_rows("go", d["gla_w_out"][0], 4)
    again = {}

    def plan_experts(key, ne, f, F):
        for twice in range(2):
            before = P.chunks
            if twice:
                P.chunks = again[key] = []
            P.plan_moe(key, ne, F, f)
            P.chunks = before

    plan_experts("m1", 8, lambda e: (d["moe_w_in"][0, e][:, 0:3584], d["moe_w_in"][0, e][:, 3584:7168], d["moe_w_out"][0, e]), 3584)
    fence1 = len(P.chunks)
    w_ada = d["w_ada_2"][0]
    for j in range(24):
        P.chunk(("ada", j), 128, CW, lambda s, j=j: [
            (s.rearrange("p (k n) -> p k n", k=8),
             w_ada[:, 256 * j:256 * j + 256].rearrange("(k p) n -> p k n", p=128))], split=False)
    w_i2 = d["w_in_2"][0]
    plan_cols("wi", w_i2, 0, 8)
    P.chunk(("wi", 8), 128, 8 * 160, lambda s: [(s.rearrange("p (k n) -> p k n", k=8),
                                                 w_i2[:, 2048:2208].rearrange("(k p) n -> p k n", p=128))])
    for j in range(2):
        P.chunk(("uq", j), 128, 3 * 384, lambda s, j=j: [
            (s.rearrange("p (k n) -> p k n", k=3),
             d["w_uq_2"][0][:, 384 * j:384 * j + 384].rearrange("(k p) n -> p k n", p=128))])
    P.chunk("ukv", 128, 2 * 1024, lambda s: [(s.rearrange("p (k n) -> p k n", k=2),
                                              d["w_ukv_2"][0].rearrange("(k p) n -> p k n", p=128))])
    plan_rows("wo", d["w_o_2"][0], 4)
    plan_experts("m2", 16, lambda e: (d["w_gate_2"][0, e], d["w_up_2"][0, e], d["w_down_2"][0, e]), 512)
    P.fence = fence1

    P.phase()
    t_c = P.load(S, cst[:, :], d["consts"])
    t_h = [P.load(S, h[0:16, 2, :], d["meta_tokens"]), P.load(S, h[:, 0, :], d["x"][0, 0:128]),
           P.load(S, h[:, 1, :], d["x"][0, 128:256])]
    vec = lnt[0:8, 0:1344]
    t_v = [P.load(S, vec[0:4, :], d["rg_conv_w"][0]), P.load(S, vec[4:5, :], d["rg_conv_b"]),
           P.load(S, vec[5:7, :], d["rg_b_gates"][0]), P.load(S, vec[7:8, :], d["rg_lambda"])]
    vT = P.ph("vT", [112, 12, 8])
    sp = P.ph("sp", [112, 6, 12])
    X1 = P.ph("X1", [112, 12, 275])
    X2 = P.ph("X2", [112, 12, T])
    xch = P.ph("xch", [112, 12, T], F32R)
    xcl = P.ph("xcl", [112, 12, T], F32R)
    R = P.ph("R", [112, 12, T])
    I = P.ph("I", [112, 12, T])

    P.pump()
    t_x = P.make_T(lambda t, k: h[0:(16 if t == 2 else 128), t, 128 * k:128 * k + 128], TILES, 8, xh, xl, t_c, *t_h)
    b = P.take()
    for c in range(12):
        tok = T_.do(lambda e, c=c, b=b: e.transpose(ps[b][0:112, 8 * c:8 * c + 8], vec[:, 112 * c:112 * c + 112],
                                                    cst[0:8, C_ID:C_ID + 8]), *t_v, t_c)
    tv = V.do(lambda e, b=b: e.tensor_copy(vT[:, :, :], ps[b][0:112, 0:96].rearrange("p (c n) -> p c n", n=8)), tok)
    P.free(b, tv)
    P.ln_free = tv
    lam = vT[:, :, 7]
    ex = A.do(lambda e: e.activation(sp[:, 0, :], lam, ACT.Abs), tv)
    ex = A.seq(lambda e: e.activation(sp[:, 0, :], sp[:, 0, :], ACT.Exp, scale=-1.0))
    V.seq(lambda e: e.tensor_scalar(sp[:, 1, :], sp[:, 0, :], 2.0, None, ALU.add), ex)
    V.seq(lambda e: e.reciprocal(sp[:, 1, :], sp[:, 1, :]))
    V.seq(lambda e: e.tensor_tensor(sp[:, 1, :], sp[:, 1, :], sp[:, 0, :], ALU.mult))
    V.seq(lambda e: e.tensor_tensor(sp[:, 2, :], sp[:, 1, :], sp[:, 1, :], ALU.mult))
    V.seq(lambda e: e.memset(sp[:, 3, :], 1.0 / 17.0))
    for m in (15, 13, 11, 9, 7, 5, 3, 1):
        V.seq(lambda e: e.tensor_tensor(sp[:, 3, :], sp[:, 3, :], sp[:, 2, :], ALU.mult))
        V.seq(lambda e, m=m: e.tensor_scalar(sp[:, 3, :], sp[:, 3, :], 1.0 / m, None, ALU.add))
    V.seq(lambda e: e.tensor_tensor(sp[:, 3, :], sp[:, 3, :], sp[:, 1, :], ALU.mult))
    V.seq(lambda e: e.tensor_scalar(sp[:, 4, :], lam, -1.0, 0.0, ALU.mult, ALU.max))
    V.seq(lambda e: e.scalar_tensor_tensor(sp[:, 5, :], sp[:, 3, :], 2.0, sp[:, 4, :], ALU.mult, ALU.add))
    t_sp = V.seq(lambda e: e.tensor_scalar(sp[:, 5, :], sp[:, 5, :], 4.0, None, ALU.mult))
    V.seq(lambda e: e.memset(X1[:, :, 0:3], 0.0))

    def rg_in(key, j, evac):
        c = P.next((key, j))
        wh = c["hi"].rearrange("p (k n) -> p k n", k=8)
        wl = c["lo"].rearrange("p (k n) -> p k n", k=8)
        for i in range(2):
            b = P.take()
            for k in range(8):
                tok = P.mm3(ps[b][0:112, 0:T], wh[:, k, 112 * i:112 * i + 112], wl[:, k, 112 * i:112 * i + 112],
                            xh[:, k, :], xl[:, k, :], k == 0, k == 7)
            if i == 1:
                P.done(c, tok)
            P.free(b, evac(2 * j + i, ps[b][0:112, 0:T], tok))

    t_xc = {}

    def conv(m, pt, tok):
        te = A.do(lambda e: e.activation(X1[:, m, 3:275], pt, ACT.Copy), tok)
        V.seq(lambda e: e.tensor_scalar(X2[:, m, :], X1[:, m, 0:T], vT[:, m, 0:1], vT[:, m, 4:5], ALU.mult, ALU.add), te)
        for q in range(1, 4):
            t = V.seq(lambda e, q=q: e.scalar_tensor_tensor(X2[:, m, :], X1[:, m, q:q + T], vT[:, m, q:q + 1],
                                                            X2[:, m, :], ALU.mult, ALU.add))
        t_xc[m] = P.split(xch[:, m, :], xcl[:, m, :], X2[:, m, :], t)
        return te

    T_.wait(t_x)
    for j in range(6):
        rg_in("xr", j, conv)
    Qt = X1[:, :, 0:T]
    t_gate = None
    for j in range(4):
        c = P.next(("gt", j))
        wh = c["hi"].rearrange("p (g k n) -> p g k n", g=2, k=3)
        wl = c["lo"].rearrange("p (g k n) -> p g k n", g=2, k=3)
        T_.wait(t_xc[3 * j + 2])
        tt = []
        for mt in range(3):
            for g in range(2):
                b = P.take()
                kts = ([0, 1], [0, 1, 2], [1, 2])[mt]
                for kt in kts:
                    tok = P.mm3(ps[b][0:112, 0:T], wh[:, g, kt, 112 * mt:112 * mt + 112], wl[:, g, kt, 112 * mt:112 * mt + 112],
                                xch[:, 3 * j + kt, :], xcl[:, 3 * j + kt, :], kt == kts[0], kt == kts[-1])
                m = 3 * j + mt
                dst = (R, I)[g][:, m, :]
                t = A.do(lambda e, dst=dst, b=b, g=g, m=m: e.activation(dst, ps[b][0:112, 0:T], ACT.Sigmoid,
                                                                        bias=vT[:, m, 5 + g:6 + g]), tok)
                P.free(b, t)
            tt.append(A.seq(lambda e, m=m: e.activation(R[:, m, :], R[:, m, :], ACT.Tanh, scale=sp[:, 5, m:m + 1]), t_sp))
        P.done(c, tok)
        z = slice(3 * j, 3 * j + 3)
        V.seq(lambda e, z=z: e.tensor_scalar(Qt[:, z, :], R[:, z, :], 1.0, None, ALU.add), *tt)
        V.seq(lambda e, z=z: e.reciprocal(Qt[:, z, :], Qt[:, z, :]))
        V.seq(lambda e, z=z: e.tensor_tensor(I[:, z, :], I[:, z, :], X2[:, z, :], ALU.mult))
        V.seq(lambda e, z=z: e.tensor_scalar(X2[:, z, :], R[:, z, :], -1.0, 1.0, ALU.mult, ALU.add))
        V.seq(lambda e, z=z: e.tensor_tensor(X2[:, z, :], X2[:, z, :], Qt[:, z, :], ALU.mult))
        t_gate = V.seq(lambda e, z=z: e.tensor_tensor(I[:, z, :], I[:, z, :], Qt[:, z, :], ALU.mult))
    ts = A.do(lambda e: e.activation(R[:, :, :], R[:, :, :], ACT.Sqrt), t_gate)
    for m in range(12):
        V.seq(lambda e, m=m: e.scalar_tensor_tensor(I[:, m, :], R[:, m, :], 2.0, I[:, m, :], ALU.mult, ALU.mult), ts)
        t_hs = V.seq(lambda e, m=m: e.tensor_tensor_scan(Qt[:, m, :], X2[:, m, :], I[:, m, :], 0.0, ALU.mult, ALU.add))
    t_y = {}

    def gbr(m, pt, tok):
        te = A.do(lambda e: e.activation(R[:, m, :], pt, ACT.Gelu_apprx_tanh), tok, t_hs)
        t = V.seq(lambda e: e.tensor_tensor(I[:, m, :], R[:, m, :], Qt[:, m, :], ALU.mult), te)
        t_y[m] = P.split(xch[:, m, :], xcl[:, m, :], I[:, m, :], t)
        return te

    for j in range(6):
        rg_in("gb", j, gbr)
    acc = {(t, q): P.take() for t, _, _ in TILES for q in range(2)}
    for j in range(6):
        c = P.next(("ro", j))
        wh = c["hi"].rearrange("p (i n) -> p i n", i=2)
        wl = c["lo"].rearrange("p (i n) -> p i n", i=2)
        for i in range(2):
            m = 2 * j + i
            T_.wait(t_y[m])
            for t, n, cc in TILES:
                for q in range(2):
                    tok = P.mm3(ps[acc[t, q]][0:n, :], xch[:, m, cc:cc + n], xcl[:, m, cc:cc + n],
                                wh[:, i, 512 * q:512 * q + 512], wl[:, i, 512 * q:512 * q + 512], m == 0, m == 11,
                                mark=(i == 1 and t == TILES[-1][0] and q == 1))
        P.done(c, tok)

    def end_block(acc, tiles, gi, tok):
        t = P.layer_norm(tiles, lambda t, q: ps[acc[t, q]][0:(16 if t == 2 else 128), :], gi, tok)
        for b in acc.values():
            P.free(b, P.ln_read)
        return t

    t_ln = end_block(acc, TILES, (0, 0), tok)
    P.dump("h0", h[:, 0:2, :], t_ln)
    src_h = lambda t, k: h[0:(16 if t == 2 else 128), t, 128 * k:128 * k + 128]
    t_x = P.make_T(src_h, TILES, 8, xh, xl, t_ln)

    def ffn_tiles(nf=28):
        P.sg = P.ph(f"sg{P.nsem}", [128, 4, T])
        P.sg_at, P.sg_free = 0, [None] * 4
        ah = P.ph(f"ah{P.nsem}", [128, nf, T], F32R)
        al = P.ph(f"al{P.nsem}", [128, nf, T], F32R)
        return ah, al

    P.phase()
    ah, al = ffn_tiles()
    acc, tok = P.ffn("ffn", 3584, TILES, 0, T, xh, xl, ah, al, t_x)
    t_ln = end_block(acc, TILES, (0, 1), tok)
    P.dump("h1", h[:, 0:2, :], t_ln)
    t_x = P.make_T(src_h, TILES, 8, xh, xl, t_ln)

    P.phase()
    wgu = P.ph("wgu", [16, 512])
    bgr = P.ph("bgr", [4, 128])
    ngb = P.ph("ngb", [128, 1024])
    t_wgu = P.load(G, wgu[:, :], d["gla_w_gate_up"][0], *[q.last for q in (T_, V, A)])
    t_bgr = P.load(G, bgr[:, :], d["gla_b_gate"][0].rearrange("(a n) -> a n", a=4))
    t_ngb = P.load(G, ngb[:, :], d["gla_norm_g"][0].rearrange("(a h) n -> a (h n)", a=1).partition_broadcast(128))
    bgT = P.ph("bgT", [128, 4])
    zT = P.ph("zT", [16, T])
    lg = P.ph("lg", [128, 4, T])
    bb = P.ph("bb", [128, 4, T])
    E1 = P.ph("E1", [128, 4, T])
    E2 = P.ph("E2", [128, 4, T])
    E3 = P.ph("E3", [128, 4, T])
    E4 = P.ph("E4", [128, 4, T])
    kot = P.ph("kot", [128, 3, 512])
    vt = P.ph("vt", [128, 3, 1024])
    rt = P.ph("rt", [128, 2, 1024])
    Sst = P.ph("Sst", [128, 4, 1024])
    sc = P.ph("sc", [128, 2, 512])
    og = rt
    mv8 = P.ph("mv8", [128, 8, 2])

    t_zero = V.do(lambda e: e.memset(sc[:, :, :], 0.0))
    b = P.take()
    tok = T_.do(lambda e, b=b: e.transpose(ps[b][:, 0:4], bgr[:, :], cst[0:4, C_ID:C_ID + 4]), t_bgr)
    t_bg = V.do(lambda e, b=b: e.tensor_copy(bgT[:, :], ps[b][:, 0:4]), tok)
    P.free(b, t_bg)
    T_.wait(t_x)
    c = P.next("gz")
    wh, wl = (c[s].rearrange("p (k n) -> p k n", k=8) for s in ("hi", "lo"))
    b = P.take()
    for k in range(8):
        tok = P.mm3(ps[b][0:16, 0:T], wh[:, k, :], wl[:, k, :], xh[:, k, :], xl[:, k, :], k == 0, k == 7)
    P.done(c, tok)
    t_z = A.do(lambda e, b=b: e.activation(zT[:, :], ps[b][0:16, 0:T], ACT.Copy), tok)
    P.free(b, t_z)
    for hh in range(4):
        b = P.take()
        tok = P.mm(ps[b][:, 0:T], wgu[:, 128 * hh:128 * hh + 128], zT[:, :], True, True, t_z, t_wgu)
        t = V.do(lambda e, b=b, hh=hh: e.tensor_scalar(lg[:, hh, :], ps[b][:, 0:T], bgT[:, hh:hh + 1], None, ALU.add),
                 tok, t_bg)
        P.free(b, t)
    fl = lambda a: a[:, :, :].rearrange("p h n -> p (h n)")
    A.do(lambda e: e.activation(fl(E1), fl(lg), ACT.Abs), t)
    A.seq(lambda e: e.activation(fl(E1), fl(E1), ACT.Exp, scale=-1.0))
    ta = A.seq(lambda e: e.activation(fl(E1), fl(E1), ACT.Ln, bias=1.0))
    V.seq(lambda e: e.scalar_tensor_tensor(fl(lg), fl(lg), 0.0, fl(E1), ALU.min, ALU.subtract), ta)
    for hh in range(4):
        t_b = V.seq(lambda e, hh=hh: e.tensor_tensor_scan(bb[:, hh, :], cst[:, C_SM:C_SM + T], lg[:, hh, :], 0.0,
                                                          ALU.mult, ALU.add))
    dec = lg
    for hh in range(4):
        bx = bb[:, hh, 16:272].rearrange("p (c s) -> p c s", s=64)
        dx = dec[:, hh, 16:272].rearrange("p (c s) -> p c s", s=64)
        V.do(lambda e, bx=bx, dx=dx: e.tensor_tensor(dx, bx, bx[:, :, 31:32].to_broadcast([128, 4, 64]), ALU.subtract), t_b)
        V.do(lambda e, hh=hh: e.tensor_copy(dec[:, hh, 0:16], bb[:, hh, 0:16]))
    t_d = V.last
    A.do(lambda e: e.activation(fl(E1), fl(dec), ACT.Exp, scale=1.0 / 16), t_d)
    te2 = A.do(lambda e: e.activation(fl(E2), fl(dec), ACT.Exp, scale=-1.0 / 16))
    te3 = A.do(lambda e: e.activation(fl(E3), fl(bb), ACT.Exp, scale=1.0 / 16))
    for hh in range(4):
        bx = bb[:, hh, 16:272].rearrange("p (c s) -> p c s", s=64)
        dx = dec[:, hh, 16:272].rearrange("p (c s) -> p c s", s=64)
        V.do(lambda e, bx=bx, dx=dx: e.tensor_tensor(dx, bx[:, :, 63:64].to_broadcast([128, 4, 64]), bx, ALU.subtract), te3)
        t_d = V.do(lambda e, hh=hh: e.tensor_tensor(dec[:, hh, 0:16], bb[:, hh, 15:16].to_broadcast([128, 16]),
                                                    bb[:, hh, 0:16], ALU.subtract))
    te4 = A.do(lambda e: e.activation(fl(E4), fl(dec), ACT.Exp, scale=1.0 / 16), t_d)
    tdc = V.do(lambda e: e.tensor_copy(gw[:, 0, 0:16].rearrange("p (h c) -> p h c", h=4),
                                       E3[:, :, 16:272].rearrange("p h (c s) -> p h c s", s=64)[:, :, :, 63]), te3)
    decs = gw[:, 0, 0:16].rearrange("p (h c) -> p h c", h=4)

    def chan(key, j, evac):
        c = P.next((key, j))
        wh, wl = (c[s].rearrange("p (k n) -> p k n", k=8) for s in ("hi", "lo"))
        for i in range(2):
            b = P.take()
            for k in range(8):
                tok = P.mm3(ps[b][:, 0:T], wh[:, k, 128 * i:128 * i + 128], wl[:, k, 128 * i:128 * i + 128],
                            xh[:, k, :], xl[:, k, :], k == 0, k == 7)
            if i == 1:
                P.done(c, tok)
            P.free(b, evac(2 * j + i, ps[b][:, 0:T], tok))

    def ev_k(m, pt, tok):
        V.do(lambda e: e.tensor_tensor(E2[:, m, :], pt, E2[:, m, :], ALU.mult), tok, te2)
        return V.do(lambda e: e.tensor_tensor(E4[:, m, :], pt, E4[:, m, :], ALU.mult), te4)

    def ev_q(m, pt, tok):
        s = 128.0 ** -0.5
        V.do(lambda e: e.scalar_tensor_tensor(E1[:, m, :], pt, s, E1[:, m, :], ALU.mult, ALU.mult), tok)
        return V.do(lambda e: e.scalar_tensor_tensor(E3[:, m, :], pt, s, E3[:, m, :], ALU.mult, ALU.mult), tdc)

    for j in range(2):
        chan("gk", j, ev_k)
    t_k = V.last
    for j in range(2):
        chan("gq", j, ev_q)
    t_q = V.last
    for t, n, cc in TILES:
        b = P.take()
        for hh in range(4):
            tok = T_.do(lambda e, b=b, n=n, cc=cc, hh=hh: e.transpose(ps[b][0:n, 128 * hh:128 * hh + 128], E4[:, hh, cc:cc + n],
                                                                      cst[:, C_ID:C_ID + 128]), t_k)
        t_ko = A.do(lambda e, b=b, n=n, t=t: e.activation(kot[0:n, t, :], ps[b][0:n, :], ACT.Copy), tok)
        P.free(b, t_ko)
    for t, n, cc in XTILES:
        b = P.take()
        for hh in range(4):
            tok = P.mm(ps[b][:, 128 * hh:128 * hh + 128], E2[:, hh, cc:cc + 128], E1[:, hh, cc:cc + 128], True, True, t_q)
        for hh in range(4):
            t_s = V.do(lambda e, b=b, t=t, hh=hh: e.copy_predicated(sc[:, t, 128 * hh:128 * hh + 128],
                                                                    cst[:, C_CM:C_CM + 128].bitcast(U32),
                                                                    ps[b][:, 128 * hh:128 * hh + 128]), tok, t_zero)
        P.free(b, t_s)

    def tokm(key, j, tiles, evac):
        c = P.next((key, j))
        n = c["n"] // 8
        wh, wl = (c[s].rearrange("p (k n) -> p k n", k=8) for s in ("hi", "lo"))
        for t, nt, cc in tiles:
            b = P.take()
            for k in range(8):
                tok = P.mm3(ps[b][0:nt, 0:n], xh[:, k, cc:cc + nt], xl[:, k, cc:cc + nt], wh[:, k, :], wl[:, k, :],
                            k == 0, k == 7)
            if t == tiles[-1][0]:
                P.done(c, tok)
            P.free(b, evac(t, nt, j, ps[b][0:nt, 0:n], tok))

    for j in range(4):
        tokm("gv", j, TILES, lambda t, n, j, pt, tok: A.do(
            lambda e: e.activation(vt[0:n, t, 256 * j:256 * j + 256], pt, ACT.Copy), tok))
    t_vt = A.last
    for j in range(4):
        tokm("gr", j, XTILES, lambda t, n, j, pt, tok: A.do(
            lambda e: e.activation(rt[0:n, t, 256 * j:256 * j + 256], pt, ACT.Silu), tok))
    t_rt = A.last
    t_S = None
    for ch in range(4):
        t, p0, n = ((2, 0, 16), (0, 0, 64), (0, 64, 64), (1, 0, 64))[ch]
        for pr in range(2):
            b = P.take()
            for hh in (2 * pr, 2 * pr + 1):
                tok = P.mm(ps[b][:, 256 * (hh % 2):256 * (hh % 2) + 256], kot[p0:p0 + n, t, 128 * hh:128 * hh + 128],
                           vt[p0:p0 + n, t, 256 * hh:256 * hh + 256], True, True, t_vt, t_ko)
            for hh in (2 * pr, 2 * pr + 1):
                o, a = Sst[:, ch, 256 * hh:256 * hh + 256], ps[b][:, 256 * (hh % 2):256 * (hh % 2) + 256]
                if ch == 0:
                    t_S = V.do(lambda e, o=o, a=a: e.tensor_copy(o, a), tok)
                else:
                    t_S = V.seq(lambda e, o=o, a=a, hh=hh, ch=ch: e.scalar_tensor_tensor(
                        o, Sst[:, ch - 1, 256 * hh:256 * hh + 256], decs[:, hh, ch - 1:ch], a, ALU.mult, ALU.add), tok, tdc)
            P.free(b, t_S)
    ob = {}
    for t, n, cc in XTILES:
        for pr in range(2):
            b = ob[t, pr] = P.take()
            for hh in (2 * pr, 2 * pr + 1):
                o = slice(256 * (hh % 2), 256 * (hh % 2) + 256)
                P.mm(ps[b][:, o], sc[:, t, 128 * hh:128 * hh + 128], vt[:, t, 256 * hh:256 * hh + 256], True, False, t_s, t_S)
                for u in range(2):
                    tok = P.mm(ps[b][64 * u:64 * u + 64, o], E3[:, hh, cc + 64 * u:cc + 64 * u + 64],
                               Sst[:, 2 * t + u, 256 * hh:256 * hh + 256], False, True)
            for hh in (2 * pr, 2 * pr + 1):
                V.do(lambda e, b=b, t=t, hh=hh: e.bn_stats(P.st[:, 4 * t + hh, 0, :], ps[b][:, 256 * (hh % 2):256 * (hh % 2) + 256]), tok)
                V.seq(lambda e, t=t, hh=hh: e.bn_aggr(mv8[:, 4 * t + hh, :], P.st[:, 4 * t + hh, 0:1, :]))
    V.seq(lambda e: e.tensor_scalar(P.rs[:, 0, 0:8], mv8[:, :, 1], LN_EPS, None, ALU.add))
    P.rsqrt(P.rs[:, 1, 0:8], P.rs[:, 0, 0:8], P.rtmp[:, 0:8])
    V.seq(lambda e: e.tensor_tensor(rt[:, 0, :], rt[:, 0, :], ngb[:, :], ALU.mult), t_rt, t_ngb)
    V.seq(lambda e: e.tensor_tensor(rt[:, 1, :], rt[:, 1, :], ngb[:, :], ALU.mult))
    on = vt
    t_vt2 = T_.last
    for t in range(2):
        for hh in range(4):
            b = ob[t, hh // 2]
            k = 4 * t + hh
            z = V.seq(lambda e, b=b, t=t, hh=hh, k=k: e.tensor_scalar(
                on[:, t, 256 * hh:256 * hh + 256], ps[b][:, 256 * (hh % 2):256 * (hh % 2) + 256],
                mv8[:, k, 0:1], P.rs[:, 1, k:k + 1], ALU.subtract, ALU.mult), t_vt2)
            if hh % 2:
                P.free(b, z)
        t_og = V.seq(lambda e, t=t: e.tensor_tensor(on[:, t, :], on[:, t, :], rt[:, t, :], ALU.mult))
    t_x = P.make_T(lambda t, k: on[:, t, 128 * k:128 * k + 128], XTILES, 8, xh, xl, t_og)

    def rows_out(key, tiles, tx):
        T_.wait(tx)
        acc = {(t, q): P.take() for t, _, _ in tiles for q in range(2)}
        for j in range(4):
            c = P.next((key, j))
            wh, wl = (c[s].rearrange("p (i n) -> p i n", i=2) for s in ("hi", "lo"))
            for i in range(2):
                k = 2 * j + i
                for t, n, cc in tiles:
                    for q in range(2):
                        tok = P.mm3(ps[acc[t, q]][:, :], xh[:, k, cc:cc + n], xl[:, k, cc:cc + n],
                                    wh[:, i, 512 * q:512 * q + 512], wl[:, i, 512 * q:512 * q + 512], k == 0, k == 7,
                                    mark=(i == 1 and t == tiles[-1][0] and q == 1))
            P.done(c, tok)
        return acc, tok

    acc, tok = rows_out("go", XTILES, t_x)
    t_ln = end_block(acc, XTILES, (1, 0), tok)
    P.dump("h2", h[:, 0:2, :], t_ln)
    t_x = P.make_T(src_h, QTILES, 8, xh, xl, t_ln)

    def router(srcs, n):
        tl = []
        o = 0
        for s, m in srcs:
            tl.append(P.load(G, rwr[:, :, o:o + m], s.rearrange("(k p) n -> p k n", p=128)))
            o += m
        tw = P.split(rwh[:, :, 0:n], rwl[:, :, 0:n], rwr[:, :, 0:n], *tl)
        bs = []
        T_.wait(tw, t_x)
        for t, _, cc in QTILES:
            b = P.take()
            for k in range(8):
                tok = P.mm3(ps[b][:, 0:n], xh[:, k, cc:cc + 128], xl[:, k, cc:cc + 128], rwh[:, k, 0:n], rwl[:, k, 0:n],
                            k == 0, k == 7)
            bs.append((b, tok))
        return bs

    def top2(t, lo, n, ready):
        L = gw[:, t, lo:lo + n]
        m8 = gw[:, t, 40:48]
        w = gw[:, t, 48:56]
        V.seq(lambda e: e.max(m8, L), ready)
        t1 = V.seq(lambda e: e.max_index(gi[:, t, :], m8, L))
        V.seq(lambda e: e.tensor_copy(w[:, 0:2], gi[:, t, 0:2]))
        td = V.seq(lambda e: e.tensor_tensor(w[:, 2:3], m8[:, 1:2], m8[:, 0:1], ALU.subtract))
        te = A.do(lambda e: e.activation(w[:, 3:4], w[:, 2:3], ACT.Exp), td)
        V.seq(lambda e: e.tensor_scalar(w[:, 4:5], w[:, 3:4], 1.0, None, ALU.add), te)
        V.seq(lambda e: e.reciprocal(w[:, 4:5], w[:, 4:5]))
        return w

    def top2_gates(t, n, w):
        io = cst[:, C_IO:C_IO + n]
        V.seq(lambda e: e.tensor_tensor(w[:, 5:6], w[:, 3:4], w[:, 4:5], ALU.mult))
        V.seq(lambda e: e.tensor_scalar(gates[:, t, 0:n], io, w[:, 0:1], w[:, 4:5], ALU.is_equal, ALU.mult))
        V.seq(lambda e: e.tensor_scalar(gw[:, t, 0:n], io, w[:, 1:2], w[:, 5:6], ALU.is_equal, ALU.mult))
        V.seq(lambda e: e.tensor_tensor(gates[:, t, 0:n], gates[:, t, 0:n], gw[:, t, 0:n], ALU.add))
        V.seq(lambda e: e.tensor_scalar(masks[:, t, 0:n], io, w[:, 0:1], None, ALU.is_equal))
        V.seq(lambda e: e.tensor_scalar(gw[:, t, 0:n], io, w[:, 1:2], None, ALU.is_equal))
        return V.seq(lambda e: e.tensor_tensor(masks[:, t, 0:n], masks[:, t, 0:n], gw[:, t, 0:n], ALU.add))

    P.phase()
    every = [q.last for q in (T_, V, A)]
    bcast = lambda nm: d[nm].partition_broadcast(128)
    bias = P.rest("bias", [128, 4, 384])
    pf = P.rest("pf", [128, 2])
    mw = P.moe_tiles(3584)
    y = mw["y"]
    for t, (b, tok) in enumerate(router([(d["moe_router"][0], 8)], 8)):
        tc = V.seq(lambda e, t=t, b=b: e.tensor_copy(gw[:, t, 0:8], ps[b][:, 0:8]), tok)
        P.free(b, tc)
        w = top2(t, 0, 8, tc)
        t_g = top2_gates(t, 8, w)

    pi = P.ph("pi", [128, 2], I32)
    t_pi0 = P.load(G, pi[:, 0:1], d["positions_2"][0, 0:128].rearrange("(p a) -> p a", a=1), *every)
    t_pi = P.load(G, pi[:, 1:2], d["positions_2"][0, 128:256].rearrange("(p a) -> p a", a=1))
    pkb = P.ph("pkb", [128, 256], I32)
    t_pk = P.load(G, pkb[:, :], bcast("positions_2"))
    V.wait(t_pi0)
    rel = P.ph("rel", [128, 384])
    stp = P.ph("stp", [128, 384])
    rb = P.ph("rb", [128, 128])
    dl = P.ph("dl", [128, 30, 4])
    i2 = lnt[:, 0:512].bitcast(I32).rearrange("p (a n) -> p a n", a=2)
    j2 = P.ph("j2", [128, 2, 2], I32)
    f2 = lnt[:, 512:1024].rearrange("p (a n) -> p a n", a=2)
    g2f = P.ph("g2f", [128, 2, 2])
    t_rb = P.load(G, rb[:, :], d["rel_bias_2"].rearrange("(a b) h -> a (b h)", a=1).partition_broadcast(128))
    V.seq(lambda e: e.tensor_copy(pf[:, :], pi[:, :]), t_pi)
    for dst, src, tk in ((i2, pkb, t_pk), (j2, pi, t_pi)):
        V.seq(lambda e, dst=dst, src=src: e.tensor_scalar(dst[:, 0, :], src[:, :], 12, None, ALU.arith_shift_right), tk)
        V.seq(lambda e, dst=dst, src=src: e.tensor_scalar(dst[:, 1, :], src[:, :], 4095, None, ALU.bitwise_and))
    V.seq(lambda e: e.tensor_copy(f2[:, :, :], i2[:, :, :]))
    V.seq(lambda e: e.tensor_copy(g2f[:, :, :], j2[:, :, :]))
    for t in range(2):
        n, o = (128, 0) if t == 0 else (256, 128)
        V.seq(lambda e, t=t, n=n: e.tensor_scalar(stp[:, 0:n], f2[:, 0, 0:n], g2f[:, 0, t:t + 1], 4096.0, ALU.subtract, ALU.mult))
        V.seq(lambda e, t=t, n=n, o=o: e.tensor_scalar(rel[:, o:o + n], f2[:, 1, 0:n], g2f[:, 1, t:t + 1], None, ALU.subtract))
        V.seq(lambda e, n=n, o=o: e.tensor_tensor(rel[:, o:o + n], rel[:, o:o + n], stp[:, 0:n], ALU.add))
    prev = 15
    for i, (th, bk) in enumerate(STEPS):
        V.do(lambda e, i=i, bk=bk, prev=prev: e.tensor_tensor(dl[:, i, :], rb[:, 4 * bk:4 * bk + 4], rb[:, 4 * prev:4 * prev + 4],
                                                              ALU.subtract), t_rb)
        prev = bk
    t_dl = P.ln_free = V.last
    for hh in range(4):
        G.seq(lambda e, hh=hh: e.tensor_scalar(bias[:, hh, :], cst[:, C_AM:C_AM + 384], rb[:, 60 + hh:61 + hh], None, ALU.add),
              t_dl, t_rb)
        for i, (th, bk) in enumerate(STEPS):
            G.seq(lambda e, hh=hh, i=i, th=th: e.tensor_scalar(stp[:, :], rel[:, :], float(th), dl[:, i, hh:hh + 1],
                                                               ALU.is_ge, ALU.mult))
            t_bias = G.seq(lambda e, hh=hh: e.tensor_tensor(bias[:, hh, :], bias[:, hh, :], stp[:, :], ALU.add))
    t_y = P.moe("m1", 8, 3584, mw, masks, gates, lambda t: h[:, t, :], t_g, t_ln, again["m1"])
    P.fence = len(P.chunks)
    P.dump("ff1", y[:, :, :], t_y)
    t_ln = P.layer_norm(QTILES, lambda t, q: y[:, t, 512 * q:512 * q + 512], (1, 1), t_y)
    P.dump("h3", h[:, 0:2, :], t_ln)

    P.phase()
    every = [q.last for q in (T_, V, A)]
    mod = P.rest("mod", [128, 4, 1024])
    hn = P.rest("hn", [128, 2, 1024])
    bcast = lambda nm: d[nm].partition_broadcast(128)
    mod2 = P.ph("mod2", [128, 2, 1024])
    t_n1 = P.load(G, P.lng, bcast("norm1_g_2"), *every)
    crow = P.ph("crow", [8, 128])
    bada = P.ph("bada", [1, 6144])
    ccol = P.ph("ccol", [128, 8])
    cbc = P.ph("cbc", [128, 8, 128])
    ones = P.ph("ones", [1, 128])
    t_cr = P.load(G, crow[:, :], d["c_2"][0].rearrange("(k p) -> k p", p=128))
    t_ba = P.load(G, bada[:, :], d["b_ada_2"])
    V.do(lambda e: e.memset(ones[:, :], 1.0))
    t_on = V.do(lambda e: e.memset(cbc[:, :, :], 0.0))
    b = P.take()
    tok = T_.do(lambda e, b=b: e.transpose(ps[b][:, 0:8], crow[:, :], cst[0:8, C_ID:C_ID + 8]), t_cr)
    tcc = A.do(lambda e, b=b: e.activation(ccol[:, :], ps[b][:, 0:8], ACT.Silu), tok)
    P.free(b, tcc)
    t_cb = V.seq(lambda e: e.tensor_tensor(cbc[:, :, :], cbc[:, :, :], ccol[:, :].unsqueeze(2).to_broadcast([128, 8, 128]), ALU.add), tcc)
    T_.wait(t_cb, t_on, t_ba)
    for j in range(24):
        c = P.next(("ada", j))
        w = c["raw"].rearrange("p (k n) -> p k n", k=8)
        b = P.take()
        for k in range(8):
            P.mm(ps[b][:, 0:256], cbc[:, k, :], w[:, k, :], k == 0, False)
        tok = P.mm(ps[b][:, 0:256], ones[:, :], bada[:, 256 * j:256 * j + 256], False, True)
        P.done(c, tok)
        part, q = j // 4, j % 4
        dst = mod2[:, part, 256 * q:256 * q + 256] if part < 2 else mod[:, part - 2, 256 * q:256 * q + 256]
        t_md = A.do(lambda e, b=b, dst=dst, part=part: e.activation(dst, ps[b][:, 0:256], ACT.Copy,
                                                                    bias=1.0 if part in (1, 4) else 0.0), tok)
        P.free(b, t_md)

    def rms_w(dst, src, G_, n, sq, *toks):
        V.seq(lambda e: e.tensor_tensor(sq, src, src, ALU.mult), *toks)
        four = len(src.shape) == 4
        fold = (lambda a: a.rearrange("p (t h) -> p t h", t=2)) if four else (lambda a: a)
        V.seq(lambda e: e.tensor_reduce(fold(P.rs[:, 0, 0:G_]), sq, AX.X, ALU.add))
        V.seq(lambda e: e.tensor_scalar(P.rs[:, 0, 0:G_], P.rs[:, 0, 0:G_], 1.0 / n, RMS_EPS, ALU.mult, ALU.add))
        P.rsqrt(P.rs[:, 1, 0:G_], P.rs[:, 0, 0:G_], P.rtmp[:, 0:G_])
        r = fold(P.rs[:, 1, 0:G_])
        return V.seq(lambda e: e.tensor_tensor(dst, src, r.unsqueeze(len(r.shape)).to_broadcast(list(src.shape)), ALU.mult))

    def modulate(gain, scale, shift, tg, tm):
        rms_w(hn[:, :, :], h[:, 0:2, :], 2, 1024, hn[:, :, :])
        V.seq(lambda e: e.tensor_tensor(gain, gain, scale, ALU.mult), tg, tm)
        for t in range(2):
            V.seq(lambda e, t=t: e.tensor_tensor(hn[:, t, :], hn[:, t, :], gain, ALU.mult))
            z = V.seq(lambda e, t=t: e.tensor_tensor(hn[:, t, :], hn[:, t, :], shift, ALU.add))
        return z

    t_hn = modulate(P.lng, mod2[:, 1, :], mod2[:, 0, :], t_n1, t_md)
    P.dump("hh", hn[:, :, :], t_hn)
    src_n = lambda t, k: hn[:, t, 128 * k:128 * k + 128]
    t_x = P.make_T(src_n, QTILES, 8, xh, xl, t_hn)

    P.phase()
    every = [q.last for q in (T_, V, A)]
    small = lnt[:, 0:1344]
    t_sm = []
    off = {}
    o = 0
    for nm, n in (("mla_cq_g_2", 384), ("mla_ckv_g_2", 256), ("mla_q_g_2", 96), ("mla_k_g_2", 96), ("diff_q_g_2", 64),
                  ("diff_k_g_2", 64), ("diff_subln_g_2", 128), ("lambda_q1_2", 64), ("lambda_k1_2", 64),
                  ("lambda_q2_2", 64), ("lambda_k2_2", 64)):
        off[nm] = (o, n)
        t_sm.append(P.load(G, small[:, o:o + n], bcast(nm)))
        o += n
    sm = lambda nm: small[:, off[nm][0]:off[nm][0] + off[nm][1]]
    pj = P.ph("pj", [128, 2, 2208])
    T_.wait(t_x)
    for j in range(9):
        tokm("wi", j, QTILES, lambda t, n, j, pt, tok: A.do(
            lambda e: e.activation(pj[:, t, 256 * j:256 * j + (256 if j < 8 else 160)], pt, ACT.Copy), tok))
    t_pj = A.last
    P.dump("proj", pj[:, :, :], t_pj)
    ang = P.ph("ang", [128, 4, 2, 16])
    for t in range(2):
        V.seq(lambda e, t=t: e.tensor_scalar(ang[:, 0, t, :], cst[:, C_IF:C_IF + 16], pf[:, t:t + 1], None, ALU.mult))
    a0, a1, a2, a3 = (ang[:, i, :, :] for i in range(4))
    MAGIC = 12582912.0
    V.seq(lambda e: e.tensor_scalar(a1, a0, 1.0 / (2 * math.pi), MAGIC, ALU.mult, ALU.add))
    V.seq(lambda e: e.tensor_scalar(a1, a1, MAGIC, None, ALU.subtract))
    c1 = 6.28125
    c2 = float(np.float32(2 * math.pi - c1).view(np.uint32) & np.uint32(0xFFFFF000))
    c2 = float((np.array(2 * math.pi - c1, np.float32).view(np.uint32) & np.uint32(0xFFFFF000)).view(np.float32))
    c3 = 2 * math.pi - c1 - c2
    for cc in (c1, c2, c3):
        V.seq(lambda e, cc=cc: e.scalar_tensor_tensor(a0, a1, -cc, a0, ALU.mult, ALU.add))
    PI = 3.1415925
    V.seq(lambda e: e.tensor_scalar(a0, a0, PI, -PI, ALU.min, ALU.max))
    V.seq(lambda e: e.tensor_scalar(a1, a0, math.pi / 2, -2 * math.pi, ALU.is_gt, ALU.mult))
    V.seq(lambda e: e.scalar_tensor_tensor(a1, a0, math.pi / 2, a1, ALU.add, ALU.add))
    t_an = V.seq(lambda e: e.tensor_scalar(a1, a1, PI, -PI, ALU.min, ALU.max))
    A.do(lambda e: e.activation(a2, a0, ACT.Sin), t_an)
    t_cs = A.do(lambda e: e.activation(a3, a1, ACT.Sin))
    SIN, COS = a2, a3

    lw = P.ph("lw", [128, 64])
    l2 = P.ph("l2", [128, 4])
    for i in range(2):
        V.seq(lambda e, i=i: e.tensor_tensor(lw[:, :], sm(f"lambda_q{i + 1}_2"), sm(f"lambda_k{i + 1}_2"), ALU.mult), *t_sm)
        tl = V.seq(lambda e, i=i: e.tensor_reduce(l2[:, i:i + 1], lw[:, :], AX.X, ALU.add))
    tl = A.do(lambda e: e.activation(l2[:, 0:2], l2[:, 0:2], ACT.Exp), tl)
    V.seq(lambda e: e.tensor_tensor(l2[:, 2:3], l2[:, 1:2], l2[:, 0:1], ALU.subtract), tl)
    V.seq(lambda e: e.tensor_scalar(l2[:, 2:3], l2[:, 2:3], -LAMBDA_INIT, None, ALU.add))
    nlam = l2[:, 2:3]

    sq = P.ph("sq", [128, 2, 768])
    qq = P.ph("qq", [128, 2, 768])
    kk = P.ph("kk", [128, 2, 768])
    vv = pj[:, :, 0:512]

    def lat(o, n, g):
        a = pj[:, :, o:o + n]
        rms_w(a, a, 2, n, sq[:, :, 0:n], t_pj)
        for t in range(2):
            z = V.seq(lambda e, t=t: e.tensor_tensor(pj[:, t, o:o + n], pj[:, t, o:o + n], sm(g), ALU.mult))
        return z

    t1 = lat(0, 384, "mla_cq_g_2")
    t_x = P.make_T(lambda t, k: pj[:, t, 128 * k:128 * k + 128], QTILES, 3, xh, xl, t1)
    T_.wait(t_x)
    for j in range(2):
        c = P.next(("uq", j))
        wh, wl = (c[s].rearrange("p (k n) -> p k n", k=3) for s in ("hi", "lo"))
        for t, _, cc in QTILES:
            b = P.take()
            for k in range(3):
                tok = P.mm3(ps[b][:, 0:384], xh[:, k, cc:cc + 128], xl[:, k, cc:cc + 128], wh[:, k, :], wl[:, k, :], k == 0, k == 2)
            if t == 1:
                P.done(c, tok)
            t_qq = A.do(lambda e, b=b, t=t, j=j: e.activation(qq[:, t, 384 * j:384 * j + 384], ps[b][:, 0:384], ACT.Copy), tok)
            P.free(b, t_qq)
    t1 = lat(384, 256, "mla_ckv_g_2")
    t_x = P.make_T(lambda t, k: pj[:, t, 384 + 128 * k:512 + 128 * k], QTILES, 2, xh, xl, t1, T_.last)
    c = P.next("ukv")
    wh, wl = (c[s].rearrange("p (k n) -> p k n", k=2) for s in ("hi", "lo"))
    T_.wait(t_x)
    k4 = [kk[:, t, :].rearrange("p (h n) -> p h n", n=96) for t in range(2)]
    v4 = [vv[:, t, :].rearrange("p (h n) -> p h n", n=64) for t in range(2)]
    for t, _, cc in QTILES:
        for q in range(2):
            b = P.take()
            for k in range(2):
                tok = P.mm3(ps[b][:, :], xh[:, k, cc:cc + 128], xl[:, k, cc:cc + 128], wh[:, k, 512 * q:512 * q + 512],
                            wl[:, k, 512 * q:512 * q + 512], k == 0, k == 1)
            if t == 1 and q == 1:
                P.done(c, tok)
            pv = ps[b][:, :].rearrange("p (h n) -> p h n", n=128)
            A.do(lambda e, pv=pv, t=t, q=q: e.activation(k4[t][:, 4 * q:4 * q + 4, 0:64], pv[:, :, 0:64], ACT.Copy), tok)
            t_kv = A.do(lambda e, pv=pv, t=t, q=q: e.activation(v4[t][:, 4 * q:4 * q + 4, :], pv[:, :, 64:128], ACT.Copy))
            P.free(b, t_kv)
        t_kv = A.do(lambda e, t=t: e.activation(k4[t][:, :, 64:96], pj[:, t, 640:672].unsqueeze(1).to_broadcast([128, 8, 32]),
                                                ACT.Copy), t_pj)

    def head_norm(buf, G_, n, g, tok):
        a = buf.rearrange("p t (h n) -> p t h n", n=n)
        s = sq[:, :, 0:G_ * n // 2].rearrange("p t (h n) -> p t h n", n=n)
        rms_w(a, a, G_, n, s, tok)
        return V.seq(lambda e: e.tensor_tensor(a, a, sm(g).unsqueeze(1).unsqueeze(1).to_broadcast(list(a.shape)), ALU.mult))

    def rope(buf):
        v = buf.rearrange("p t (h n) -> p t h n", n=96)
        x1, x2 = v[:, :, :, 64:80], v[:, :, :, 80:96]
        s = sq[:, :, 0:512].rearrange("p t (i h n) -> p t i h n", i=4, n=16)
        for t in range(2):
            cb, sb_ = (a[:, t, :].unsqueeze(1).to_broadcast([128, 8, 16]) for a in (COS, SIN))
            for i, (x, f) in enumerate(((x1, cb), (x2, sb_), (x2, cb), (x1, sb_))):
                V.seq(lambda e, i=i, x=x, f=f, t=t: e.tensor_tensor(s[:, t, i], x[:, t], f, ALU.mult), t_cs)
            V.seq(lambda e, t=t: e.tensor_tensor(x1[:, t], s[:, t, 0], s[:, t, 1], ALU.subtract))
            z = V.seq(lambda e, t=t: e.tensor_tensor(x2[:, t], s[:, t, 2], s[:, t, 3], ALU.add))
        return z

    head_norm(qq[:, :, :], 16, 96, "mla_q_g_2", t_qq)
    t_q = rope(qq[:, :, :])
    head_norm(kk[:, :, :], 16, 96, "mla_k_g_2", t_kv)
    t_k = rope(kk[:, :, :])
    dq, dk, dv = pj[:, :, 672:1184], pj[:, :, 1184:1696], pj[:, :, 1696:2208]
    t_dq = head_norm(dq, 16, 64, "diff_q_g_2", t_pj)
    t_dk = head_norm(dk, 16, 64, "diff_k_g_2", t_pj)

    P.o2 = o2 = hn
    qT = P.ph("qT", [128, 2, 256])
    kT = P.ph("kT", [128, 2, 256])
    Sx = P.ph("Sx", [128, 2, 2, 384])
    Pt = P.ph("Pt", [128, 2, 3, 128])
    ss = P.ph("ss", [128, 2, 16])
    qk_free, S_free, Pt_free = [None, None], [None, None], [None, None]

    def to_heads(i, n, qsrc, ksrc, tq):
        b = P.take()
        for t in range(2):
            T_.do(lambda e, b=b, t=t: e.transpose(ps[b][0:n, 128 * t:128 * t + 128], qsrc(t), cst[:, C_ID:C_ID + 128]), *tq)
            tok = T_.do(lambda e, b=b, t=t: e.transpose(ps[b][0:n, 256 + 128 * t:384 + 128 * t], ksrc(t), cst[:, C_ID:C_ID + 128]))
        A.do(lambda e, b=b: e.activation(qT[0:n, i, :], ps[b][0:n, 0:256], ACT.Copy), tok, qk_free[i])
        z = A.do(lambda e, b=b: e.activation(kT[0:n, i, :], ps[b][0:n, 256:512], ACT.Copy))
        P.free(b, z)
        return z

    def scores(i, u, p0, n, scale, bm, tz, tb):
        b = P.take()
        P.mm(ps[b][:, 0:128], qT[p0:p0 + n, i, 0:128], kT[p0:p0 + n, i, 0:128], True, True, tz)
        tok = P.mm(ps[b][:, 128:384], qT[p0:p0 + n, i, 128:256], kT[p0:p0 + n, i, 0:256], True, True)
        qk_free[i] = tok
        x = Sx[:, i, u, :]
        t1 = V.do(lambda e, b=b: e.scalar_tensor_tensor(x, ps[b][:, 0:384], scale, bm, ALU.mult, ALU.add), tok, tb, S_free[i])
        P.free(b, t1)
        V.seq(lambda e: e.tensor_reduce(ss[:, u, 0:1], x[:, 0:128], AX.X, ALU.max, negate=True))
        t2 = V.seq(lambda e: e.tensor_reduce(ss[:, u, 1:2], x[:, 128:384], AX.X, ALU.max, negate=True))
        A.do(lambda e: e.activation(x[:, 0:128], x[:, 0:128], ACT.Exp, bias=ss[:, u, 0:1], accum_out=ss[:, u, 2:3]), t2)
        t3 = A.do(lambda e: e.activation(x[:, 128:384], x[:, 128:384], ACT.Exp, bias=ss[:, u, 1:2], accum_out=ss[:, u, 3:4]))
        return V.seq(lambda e: e.reciprocal(ss[:, u, 4:6], ss[:, u, 2:4]), t3)

    def probs_T(i, tp):
        b = P.take()
        for m in range(3):
            tok = T_.do(lambda e, b=b, m=m: e.transpose(ps[b][:, 128 * m:128 * m + 128], Sx[:, i, 0, 128 * m:128 * m + 128],
                                                        cst[:, C_ID:C_ID + 128]), tp)
        S_free[i] = tok
        z = A.do(lambda e, b=b: e.activation(Pt[:, i, :, :].rearrange("p m q -> p (m q)"), ps[b][:, 0:384], ACT.Copy), tok, Pt_free[i])
        P.free(b, z)
        return z

    obk = [P.take(), P.take()]

    def values(i, cols, vsrc, tz):
        P.mm(ps[obk[0]][:, cols], Pt[:, i, 0, :], vsrc(0), True, True, tz)
        P.mm(ps[obk[1]][:, cols], Pt[:, i, 1, :], vsrc(0), True, False)
        Pt_free[i] = P.mm(ps[obk[1]][:, cols], Pt[:, i, 2, :], vsrc(1), False, True)
        return Pt_free[i]

    am = cst[:, C_AM:C_AM + 384]
    for hh in range(8):
        i = hh % 2
        tz = to_heads(i, 96, lambda t, hh=hh: qq[:, t, 96 * hh:96 * hh + 96],
                      lambda t, hh=hh: kk[:, t, 96 * hh:96 * hh + 96], (t_q, t_k))
        tr = scores(i, 0, 0, 96, 96.0 ** -0.5, am, tz, None)
        x = Sx[:, i, 0, :]
        V.seq(lambda e, x=x: e.tensor_scalar(x[:, 0:128], x[:, 0:128], ss[:, 0, 4:5], None, ALU.mult))
        tp = V.seq(lambda e, x=x: e.tensor_scalar(x[:, 128:384], x[:, 128:384], ss[:, 0, 5:6], None, ALU.mult))
        tz = probs_T(i, tp)
        tok = values(i, slice(64 * hh, 64 * hh + 64), lambda t, hh=hh: v4[t][:, hh, :], tz)
    for t in range(2):
        z = A.do(lambda e, t=t, b=obk[t]: e.activation(o2[:, t, 0:512], ps[b][:, :], ACT.Copy), tok)
        P.free(obk[t], z)
    P.dump("omla", o2[:, :, 0:512], z)
    obk = [P.take(), P.take()]
    for hh in range(4):
        i = hh % 2
        tz = to_heads(i, 128, lambda t, hh=hh: dq[:, t, 128 * hh:128 * hh + 128], lambda t, hh=hh: dk[:, t, 128 * hh:128 * hh + 128],
                      (t_dq, t_dk))
        scores(i, 0, 0, 64, 0.125, bias[:, hh, :], tz, t_bias)
        scores(i, 1, 64, 64, 0.125, bias[:, hh, :], tz, t_bias)
        V.seq(lambda e: e.tensor_scalar(ss[:, 1, 4:6], ss[:, 1, 4:6], nlam, None, ALU.mult))
        for t, (a, z) in enumerate(((0, 128), (128, 384))):
            V.seq(lambda e, i=i, t=t, a=a, z=z: e.tensor_scalar(Sx[:, i, 1, a:z], Sx[:, i, 1, a:z], ss[:, 1, 4 + t:5 + t], None, ALU.mult))
            tp = V.seq(lambda e, i=i, t=t, a=a, z=z: e.scalar_tensor_tensor(Sx[:, i, 0, a:z], Sx[:, i, 0, a:z], ss[:, 0, 4 + t:5 + t],
                                                                            Sx[:, i, 1, a:z], ALU.mult, ALU.add))
        tz = probs_T(i, tp)
        tok = values(i, slice(128 * hh, 128 * hh + 128), lambda t, hh=hh: dv[:, t, 128 * hh:128 * hh + 128], tz)
    for t in range(2):
        z = A.do(lambda e, t=t, b=obk[t]: e.activation(o2[:, t, 512:1024], ps[b][:, :], ACT.Copy), tok)
        P.free(obk[t], z)
    od = sq[:, :, 0:512].rearrange("p t (h n) -> p t h n", n=128)
    od2 = qq[:, :, 0:512].rearrange("p t (h n) -> p t h n", n=128)
    V.seq(lambda e: e.tensor_copy(sq[:, :, 0:512], o2[:, :, 512:1024]), z)
    rms_w(od, od, 8, 128, od2)
    V.seq(lambda e: e.tensor_tensor(od, od, sm("diff_subln_g_2").unsqueeze(1).unsqueeze(1).to_broadcast(list(od.shape)), ALU.mult))
    t_o = V.seq(lambda e: e.tensor_scalar(o2[:, :, 512:1024], sq[:, :, 0:512], 1.0 - LAMBDA_INIT, None, ALU.mult))
    P.dump("odiff", o2[:, :, 512:1024], t_o)
    t_x = P.make_T(lambda t, k: o2[:, t, 128 * k:128 * k + 128], QTILES, 8, xh, xl, t_o)
    acc, tok = rows_out("wo", QTILES, t_x)
    for (t, q), b in acc.items():
        a = slice(512 * q, 512 * q + 512)
        z = V.do(lambda e, t=t, a=a, b=b: e.tensor_tensor(hn[:, t, a], ps[b][:, :], mod[:, 0, a], ALU.mult), tok)
        P.free(b, z)
        t_h = V.seq(lambda e, t=t, a=a: e.tensor_tensor(h[:, t, a], h[:, t, a], hn[:, t, a], ALU.add))
    P.dump("x1", h[:, 0:2, :], t_h)
    t_n2 = P.load(G, P.lng, bcast("norm2_g_2"), V.last)
    t_hn = modulate(P.lng, mod[:, 2, :], mod[:, 1, :], t_n2, t_md)
    P.dump("hh2", hn[:, :, :], t_hn)
    t_x = P.make_T(src_n, QTILES, 8, xh, xl, t_hn)

    P.phase()
    mw = P.moe_tiles(512)
    y = mw["y"]
    br = P.ph("br", [128, 20])
    big = P.ph("big", [128, 2, 24])
    gm = P.ph("gm", [128, 2, 16], I32)
    t_br = [P.load(G, br[:, 0:4], bcast("b_rg_2"), *[q.last for q in (T_, V, A)]), P.load(G, br[:, 4:20], bcast("b_re_2"))]
    V.seq(lambda e: e.memset(big[:, :, :], -3.0e38))
    for t, (b, tok) in enumerate(router([(d["w_rg_2"][0], 4), (d["w_re_2"][0], 16)], 20)):
        gl, el = gw[:, t, 0:4], gw[:, t, 4:20]
        z = V.seq(lambda e, t=t, b=b: e.tensor_tensor(gw[:, t, 0:20], ps[b][:, 0:20], br[:, :], ALU.add), tok, *t_br)
        P.free(b, z)
        m8, w = gw[:, t, 40:48], gw[:, t, 48:64]
        V.seq(lambda e, t=t, gl=gl: e.tensor_copy(big[:, t, 16:20], gl))
        V.seq(lambda e, t=t, m8=m8: e.max(m8, big[:, t, 16:24]))
        V.seq(lambda e, t=t, m8=m8: e.max_index(gi[:, t, :], m8, big[:, t, 16:24]))
        V.seq(lambda e, t=t, w=w: e.tensor_copy(w[:, 8:9], gi[:, t, 0:1]))
        z = V.seq(lambda e, w=w, m8=m8: e.tensor_scalar(w[:, 9:10], m8[:, 0:1], -1.0, None, ALU.mult))
        z = A.do(lambda e, w=w, gl=gl: e.activation(w[:, 10:14], gl, ACT.Exp, bias=w[:, 9:10], accum_out=w[:, 14:15]), z)
        V.seq(lambda e, w=w: e.reciprocal(w[:, 15:16], w[:, 14:15]), z)
        io = cst[:, C_IO:C_IO + 4].unsqueeze(2).to_broadcast([128, 4, 4])
        V.seq(lambda e, t=t, io=io, w=w: e.tensor_scalar(gm[:, t, :].rearrange("p (g n) -> p g n", n=4), io, w[:, 8:9], None, ALU.is_equal))
        z = V.seq(lambda e, t=t, el=el: e.copy_predicated(big[:, t, 0:16], gm[:, t, :], el))
        z = V.seq(lambda e, t=t: e.tensor_copy(gw[:, t, 20:36], big[:, t, 0:16]))
        w = top2(t, 20, 16, z)
        V.seq(lambda e, t=t, w=w: e.tensor_tensor(w[:, 4:5], w[:, 4:5], gw[:, t, 63:64], ALU.mult))
        t_g = top2_gates(t, 16, w)
    t_y = P.moe("m2", 16, 512, mw, masks, gates, lambda t: hn[:, t, :], t_g, t_hn, again["m2"])
    P.dump("y2", y[:, :, :], t_y)
    for t in range(2):
        V.seq(lambda e, t=t: e.tensor_tensor(y[:, t, :], y[:, t, :], mod[:, 3, :], ALU.mult))
        z = V.seq(lambda e, t=t: e.tensor_tensor(h[:, t, :], h[:, t, :], y[:, t, :], ALU.add))
        P.pending_out.append(P.load(S, out[0, 128 * t:128 * t + 128, :], h[:, t, :], z))
    S.wait(*P.loads)
    P.phase_ctx.close()
    assert P.at == len(P.chunks)

    with P.ctx:
        block = P.ctx.enter_context(nc.Block())

        @block.sync
        def _(eng):
            S.emit(eng)

        @block.tensor
        def _(eng):
            T_.emit(eng)

        @block.vector
        def _(eng):
            V.emit(eng)

        @block.scalar
        def _(eng):
            A.emit(eng)

        @block.gpsimd
        def _(eng):
            G.emit(eng)


NAMES = ["x", "meta_tokens", "ln_gain", "ln_bias", "rg_w_in", "rg_conv_w", "rg_conv_b", "rg_w_gates", "rg_b_gates",
         "rg_lambda", "rg_w_out", "gla_w_in", "gla_w_gate_up", "gla_b_gate", "gla_norm_g", "gla_w_out", "ffn_w_in",
         "ffn_w_out", "moe_router", "moe_w_in", "moe_w_out", "c_2", "positions_2", "rel_bias_2", "w_ada_2", "b_ada_2",
         "norm1_g_2", "w_in_2", "mla_cq_g_2", "w_uq_2", "mla_ckv_g_2", "w_ukv_2", "mla_q_g_2", "mla_k_g_2",
         "diff_q_g_2", "diff_k_g_2", "lambda_q1_2", "lambda_k1_2", "lambda_q2_2", "lambda_k2_2", "diff_subln_g_2",
         "w_o_2", "norm2_g_2", "w_rg_2", "b_rg_2", "w_re_2", "b_re_2", "w_gate_2", "w_up_2", "w_down_2"]


def program(nc, inputs, dumps=None):
    arrays, d = {}, {}
    for name in NAMES:
        arrays["in_" + name] = np.ascontiguousarray(inputs[name])
    arrays["in_consts"] = const_table()
    for name in NAMES + ["consts"]:
        a = arrays["in_" + name]
        d[name] = nc.dram_tensor("in_" + name, a.shape, mybir.dt.from_np(a.dtype), kind="ExternalInput").ap()
    out = nc.dram_tensor("out_0", (1, 256, 1024), F32, kind="ExternalOutput").ap()
    build(nc, d, out, dumps)
    return arrays


def kernel(**inputs):
    import concourse.bacc as bacc
    from concourse.bass_utils import run_bass_kernel_spmd as run

    nc = bacc.Bacc("TRN2", target_bir_lowering=False, num_devices=1)
    arrays = program(nc, inputs)
    r = run(nc, [arrays], core_ids=[0])
    return r.results[0]["out_0"]
```

```python
from contextlib import ExitStack
import math

import numpy as np
import concourse.bass as bass
from concourse import mybir

F32 = mybir.dt.float32
F32R = mybir.dt.float32r
I32 = mybir.dt.int32
U32 = mybir.dt.uint32
ALU = mybir.AluOpType
ACT = mybir.ActivationFunctionType
AX = mybir.AxisListType

ALPHA = (2 * 2) ** 0.25
LN_EPS = 1e-5
RMS_EPS = 1e-6
T = 272
CW = 2048
NRAW, NSPL = 4, 3
LAMBDA_INIT = 0.8 - 0.6 * math.exp(-0.3 * 0)
STEPS = [(-90, 14), (-63, 13), (-45, 12), (-31, 11), (-22, 10), (-15, 9), (-11, 8), (-7, 7), (-6, 6), (-5, 5),
         (-4, 4), (-3, 3), (-2, 2), (-1, 1), (0, 0), (1, 17), (2, 18), (3, 19), (4, 20), (5, 21), (6, 22), (7, 23),
         (8, 24), (12, 25), (16, 26), (23, 27), (32, 28), (46, 29), (64, 30), (91, 31)]
TILES = [(2, 16, 0), (0, 128, 16), (1, 128, 144)]
XTILES = [(0, 128, 16), (1, 128, 144)]
QTILES = [(0, 128, 0), (1, 128, 128)]
C_ID, C_CM, C_SM, C_AM, C_IF, C_UP, C_IO, C_END = 0, 128, 256, 528, 912, 928, 1056, 1312


def const_table():
    c = np.zeros((128, C_END), np.float32)
    c[:, C_ID:C_ID + 128] = np.eye(128, dtype=np.float32)
    s, q = np.arange(128)[:, None], np.arange(128)[None, :]
    c[:, C_CM:C_CM + 128] = (s <= q) & (s // 64 == q // 64)
    m = np.ones(T, np.float32)
    m[[0, 16, 80, 144, 208]] = 0.0
    c[:, C_SM:C_SM + T] = m
    c[:64, C_AM + 64:C_AM + 128] = -1e30
    c[:64, C_AM + 128 + 192:C_AM + 384] = -1e30
    c[:, C_UP:C_UP + 128] = s < q
    c[:, C_IO:C_IO + 256] = np.arange(256, dtype=np.float32)
    c[:, C_IF:C_IF + 16] = np.float32(10000.0) ** (-np.arange(16, dtype=np.float32) / np.float32(16))
    return c


class Queue:

    def __init__(self, sem):
        self.sem, self.n, self.items, self.seen = sem, 0, [], {}

    def wait(self, *toks):
        for tok in toks:
            if tok is None:
                continue
            sem, v = tok
            if self.seen.get(sem.name, 0) < v:
                self.seen[sem.name] = v
                self.items.append((None, sem, v))

    def run(self, f, *toks):
        self.wait(*toks)
        self.items.append((f, None, 0))

    def do(self, f, *toks):
        self.wait(*toks)
        self.n += 1
        self.items.append((f, self.sem, 1))
        return (self.sem, self.n)

    def seq(self, f, *toks):
        return self.do(f, self.last, *toks)

    def dma(self, f, sem, count, *toks):
        self.wait(*toks)
        count[0] += 16
        self.items.append((f, sem, 16))
        return (sem, count[0])

    @property
    def last(self):
        return (self.sem, self.n) if self.n else None

    def begin_if(self, flag, sem):
        self.items.append(("if", flag, 0))
        self.outer = (self.sem, self.n, dict(self.seen))
        self.sem, self.n = sem, 0

    def end_if(self):
        self.items.append(("end", None, 0))
        self.sem, self.n, self.seen = self.outer

    def emit(self, eng):
        guard = None
        for f, sem, v in self.items:
            if f is None:
                eng.wait_ge(sem, v)
            elif f == "if":
                guard = eng.If(eng.value_load(sem, min_val=0, max_val=1) != 0)
                guard.__enter__()
            elif f == "end":
                guard.__exit__(None, None, None)
            elif sem is None:
                f(eng)
            else:
                f(eng).then_inc(sem, v)


class Program:
    def __init__(self, nc, d, out, dumps=None):
        self.nc, self.d, self.out, self.dumps = nc, d, out, dumps
        self.ctx = ExitStack()
        self.T = Queue(self.sem("s_pe"))
        self.V = Queue(self.sem("s_dve"))
        self.A = Queue(self.sem("s_act"))
        self.G = Queue(self.sem("s_pool"))
        self.S = Queue(self.sem("s_sp"))
        self.nsem = 0
        self.n_phase = 0
        self.phase_ctx = None
        self.pending_out = []

    def sem(self, name):
        return self.ctx.enter_context(self.nc.semaphore(name))

    def sb(self, name, shape, dt=F32):
        return self.ctx.enter_context(self.nc.sbuf_tensor(name, shape, dt))

    def ph(self, name, shape, dt=F32):
        return self.phase_ctx.enter_context(self.nc.sbuf_tensor(f"{name}_{self.n_phase}", shape, dt))

    def phase(self):
        if self.phase_ctx is not None:
            self.phase_ctx.close()
            lasts = [q.last for q in (self.T, self.V, self.A, self.G)]
            for q in (self.T, self.V, self.A, self.G):
                q.wait(*lasts, *self.loads)
        self.loads = []
        self.n_phase += 1
        self.phase_ctx = ExitStack()

    def rest(self, name, shape, dt=F32):
        return self.ctx.enter_context(self.nc.sbuf_tensor(name, shape, dt))

    def load(self, q, dst, src, *toks):
        self.nsem += 1
        sem = self.sem(f"s_ld{self.nsem}")
        tok = q.dma(lambda e: e.dma_start(dst, src), sem, [0], *toks)
        self.loads.append(tok)
        return tok

    def dump(self, name, ap, *toks):
        if self.dumps is not None:
            o = self.nc.dram_tensor("dbg_" + name, ap.shape, F32, kind="ExternalOutput").ap()
            self.dumps.append("dbg_" + name)
            t = self.load(self.S, o, ap, *toks)
            for q in (self.T, self.V, self.A, self.G):
                q.wait(t)

    def banks_init(self):
        self.ps = [self.ctx.enter_context(self.nc.psum_tensor(f"ps{i}", [128, 512], F32)) for i in range(8)]
        self.bank_free = [[] for _ in range(8)]
        self.bank_at = 0

    def take(self):
        i = self.bank_at
        while self.bank_free[i] is None:
            i = (i + 1) % 8
        self.bank_at = (i + 1) % 8
        self.T.wait(*self.bank_free[i])
        self.bank_free[i] = None
        return i

    def free(self, i, *toks):
        self.bank_free[i] = list(toks)

    def stream_init(self):
        self.raw = self.sb("raw", [128, NRAW, CW], F32)
        self.whi = self.sb("whi", [128, NSPL, CW], F32R)
        self.wlo = self.sb("wlo", [128, NSPL, CW], F32R)
        self.s_raw = [self.sem(f"s_raw{i}") for i in range(NRAW)]
        self.n_raw = [[0] for _ in range(NRAW)]
        self.chunks = []
        self.at = 0
        self.n_loaded = 0
        self.n_split = 0
        self.spl_next = 0
        self.raw_free = [None] * NRAW
        self.spl_free = [None] * NSPL
        self.raw_busy = [False] * NRAW
        self.spl_busy = [False] * NSPL
        self.fence = 0
        self.hold = False

    def chunk(self, key, rows, n, pieces, split=True, zero=False):
        self.chunks.append(dict(key=key, rows=rows, n=n, pieces=pieces, split=split, zero=zero))

    def pump(self):
        go = True
        while go:
            go = False
            i = self.n_loaded
            if i < self.fence and not self.raw_busy[i % NRAW]:
                c, k = self.chunks[i], i % NRAW
                self.raw_busy[k] = True
                slot = self.raw[0:c["rows"], k, 0:c["n"]]
                before = [self.raw_free[k]]
                if c["zero"]:
                    before = [self.G.do(lambda e, s=slot: e.memset(s, 0.0), *before)]
                for dst, src in c["pieces"](slot):
                    tok = self.S.dma(lambda e, a=dst, b=src: e.dma_start(a, b), self.s_raw[k], self.n_raw[k], *before)
                c["raw"], c["in"], c["k"] = slot, tok, k
                self.n_loaded += 1
                go = True
            i = self.n_split
            if i < self.n_loaded:
                c = self.chunks[i]
                if not c["split"]:
                    self.n_split += 1
                    go = True
                    continue
                s = self.spl_next
                if not self.spl_busy[s] and not self.hold:
                    self.spl_busy[s] = True
                    self.spl_next = (s + 1) % NSPL
                    hi = self.whi[0:c["rows"], s, 0:c["n"]]
                    lo = self.wlo[0:c["rows"], s, 0:c["n"]]
                    t1 = self.A.do(lambda e, h=hi, r=c["raw"]: e.activation(h, r, ACT.Copy), c["in"], self.spl_free[s])
                    t2 = self.V.do(lambda e, l=lo, h=hi, r=c["raw"]:
                                   e.tensor_tensor(l, r, h.bitcast(F32), ALU.subtract), t1, self.spl_free[s])
                    c["hi"], c["lo"], c["s"], c["ready"] = hi, lo, s, t2
                    self.raw_free[c["k"]] = t2
                    self.raw_busy[c["k"]] = False
                    self.n_split += 1
                    go = True

    def next(self, key):
        c = self.chunks[self.at]
        assert c["key"] == key, (c["key"], key)
        self.at += 1
        self.pump()
        self.T.wait(c["ready"] if c["split"] else c["in"])
        return c

    def done(self, c, tok):
        if c["split"]:
            self.spl_free[c["s"]] = tok
            self.spl_busy[c["s"]] = False
        else:
            self.raw_free[c["k"]] = tok
            self.raw_busy[c["k"]] = False
        self.pump()

    def begin_if(self, name, flag, chunks, *toks):
        qs = (self.T, self.V, self.A, self.G, self.S)
        lasts = [q.last for q in qs]
        for q in qs:
            q.wait(*lasts, *toks)
            q.begin_if(flag, self.sem(f"s_{name}_{q.sem.name}"))
        assert not any(self.raw_busy) and not any(self.spl_busy) and None not in self.bank_free
        self.kept = (self.chunks, self.at, self.n_loaded, self.n_split, self.spl_next, self.s_raw, self.n_raw,
                     list(self.raw_free), list(self.spl_free), list(self.bank_free), self.bank_at, self.fence)
        self.chunks, self.at, self.n_loaded, self.n_split, self.fence = chunks, 0, 0, 0, len(chunks)
        self.s_raw = [self.sem(f"s_{name}_raw{i}") for i in range(NRAW)]
        self.n_raw = [[0] for _ in range(NRAW)]
        self.raw_free, self.spl_free, self.bank_free = [None] * NRAW, [None] * NSPL, [[] for _ in range(8)]

    def end_if(self):
        qs = (self.T, self.V, self.A, self.G, self.S)
        assert self.at == len(self.chunks)
        lasts = [q.last for q in qs]
        for q in qs:
            q.wait(*lasts)
            q.end_if()
        (self.chunks, self.at, self.n_loaded, self.n_split, self.spl_next, self.s_raw, self.n_raw,
         self.raw_free, self.spl_free, self.bank_free, self.bank_at, self.fence) = self.kept

    def mm3(self, out, lh, ll, rh, rl, start, stop, mark=False):
        self.T.run(lambda e: e.matmul(out, lh, rh, start=start, stop=False))
        self.T.run(lambda e: e.matmul(out, lh, rl, start=False, stop=False))
        f = lambda e: e.matmul(out, ll, rh, start=False, stop=stop)
        if stop or mark:
            return self.T.do(f)
        self.T.run(f)

    def mm(self, out, l, r, start, stop, *toks):
        f = lambda e: e.matmul(out, l, r, start=start, stop=stop)
        if stop:
            return self.T.do(f, *toks)
        self.T.run(f, *toks)

    def split(self, hi, lo, src, *toks):
        t1 = self.A.do(lambda e: e.activation(hi, src, ACT.Copy), *toks)
        t2 = self.V.do(lambda e: e.tensor_tensor(lo, src, hi.bitcast(F32), ALU.subtract), t1)
        return t2

    def make_T(self, src, tiles, nk, hi, lo, *toks, gain=None, shift=None, tmp=None):
        idn = self.cst
        tok = None
        c0 = min(c for _, _, c in tiles)
        c1 = max(c + n for _, n, c in tiles)
        free = [None, None]
        toks = toks or (None,)
        for k in range(nk):
            b = self.take()
            for t, n, c in tiles:
                a = src(t, k)
                f = lambda e, o=self.ps[b][:, c:c + n], a=a, n=n: e.transpose(o, a, idn[0:n, C_ID:C_ID + n])
                tt = self.T.do(f, *toks)
            p, h, l = self.ps[b][:, c0:c1], hi[:, k, c0:c1], lo[:, k, c0:c1]
            if shift is not None:
                x = tmp[:, k % 2, 0:c1 - c0]
                if k % 2:
                    tx = self.A.do(lambda e, x=x, p=p, g=gain(k), s=shift(k): e.activation(x, p, ACT.Identity, bias=s, scale=g),
                                   tt, free[k % 2])
                    tx = self.A.seq(lambda e, x=x, h=h: e.activation(h, x, ACT.Copy))
                    tok = self.V.do(lambda e, x=x, h=h, l=l: e.tensor_tensor(l, x, h.bitcast(F32), ALU.subtract), tx)
                else:
                    tx = self.V.do(lambda e, x=x, p=p, g=gain(k), s=shift(k): e.tensor_scalar(x, p, g, s, ALU.mult, ALU.add),
                                   tt, free[k % 2])
                    tok = self.split(h, l, x, tx)
                free[k % 2] = tok
            elif gain is not None and gain(k) is not None:
                tx = self.A.do(lambda e, p=p, h=h, g=gain(k): e.activation(h, p, ACT.Copy, scale=g), tt)
                tok = self.V.do(lambda e, p=p, h=h, l=l, g=gain(k): e.scalar_tensor_tensor(
                    l, p, g, h.bitcast(F32), ALU.mult, ALU.subtract), tx)
            else:
                tok = self.split(h, l, p, tt)
            self.free(b, tok)
        return tok

    def rsqrt(self, y, x, tmp, *toks):
        V = self.V
        V.seq(lambda e: e.tensor_scalar(y.bitcast(I32), x.bitcast(I32), 1, None, ALU.logical_shift_right), *toks)
        V.seq(lambda e: e.tensor_scalar(y.bitcast(I32), y.bitcast(I32), -1.0, 1597463007.0, ALU.mult, ALU.add))
        V.seq(lambda e: e.tensor_scalar(x, x, -0.5, None, ALU.mult))
        for _ in range(3):
            V.seq(lambda e: e.tensor_tensor(tmp, y, y, ALU.mult))
            V.seq(lambda e: e.tensor_tensor(tmp, tmp, x, ALU.mult))
            t = V.seq(lambda e: e.scalar_tensor_tensor(y, tmp, 1.5, y, ALU.add, ALU.mult))
        return t

    def layer_norm(self, tiles, src, gi, *toks):
        V, h = self.V, self.h
        i, j = gi
        tg = self.load(self.G, self.lng[:, :], self.d["ln_gain"][i, j:j + 1, :].partition_broadcast(128), self.ln_free)
        tb = self.load(self.G, self.lnb[:, :], self.d["ln_bias"][i, j:j + 1, :].partition_broadcast(128), self.ln_free)
        st, mv, rs, tmp = self.st, self.mv, self.rs, self.rtmp
        V.seq(lambda e: e.memset(mv[:, :, :], 1.0))
        read = None
        for t, n, _ in tiles:
            for q in range(2):
                a = h[0:n, t, q * 512:(q + 1) * 512]
                read = V.do(lambda e, a=a, s=src(t, q): e.scalar_tensor_tensor(a, a, ALPHA, s, ALU.mult, ALU.add), *toks)
        self.ln_read = read
        for t, n, _ in tiles:
            for q in range(2):
                V.seq(lambda e, a=h[0:n, t, q * 512:(q + 1) * 512], o=st[0:n, t, q, :]: e.bn_stats(o, a))
        for t, n, _ in tiles:
            V.seq(lambda e, o=mv[0:n, t, :], a=st[0:n, t, :, :]: e.bn_aggr(o, a))
        V.seq(lambda e: e.tensor_scalar(rs[:, 0, 0:3], mv[:, :, 1], LN_EPS, None, ALU.add))
        self.rsqrt(rs[:, 1, 0:3], rs[:, 0, 0:3], tmp[:, 0:3])
        for t, n, _ in tiles:
            a = h[0:n, t, :]
            V.seq(lambda e, a=a, n=n, t=t: e.tensor_scalar(a, a, mv[0:n, t, 0:1], rs[0:n, 1, t:t + 1],
                                                            ALU.subtract, ALU.mult))
            V.seq(lambda e, a=a, n=n: e.tensor_tensor(a, a, self.lng[0:n, :], ALU.mult), tg)
            self.ln_free = V.seq(lambda e, a=a, n=n: e.tensor_tensor(a, a, self.lnb[0:n, :], ALU.add), tb)
        return self.ln_free

    def plan_ffn(self, key, wg, wu, wd, F):
        for j in range(F // 256):
            for nm, w in (("g", wg), ("u", wu)):
                self.chunk((key, nm, j), 128, CW, lambda s, w=w, j=j: [
                    (s.rearrange("p (k n) -> p k n", k=8),
                     w[:, 256 * j:256 * j + 256].rearrange("(k p) n -> p k n", p=128))])
        for j in range(F // 256):
            self.chunk((key, "d", j), 128, CW, lambda s, j=j: [
                (s.rearrange("p (i n) -> p i n", i=2),
                 wd[256 * j:256 * j + 256, :].rearrange("(i p) n -> p i n", p=128))])

    def moe_order(self, ne, F):
        if F > 512:
            return [(x, e_) for e_ in range(ne) for x in "ud"]
        o = [("u", 0)]
        for e_ in range(ne):
            o += [("u", e_ + 1)] * (e_ + 1 < ne) + [("d", e_)]
        return o

    def plan_moe(self, key, ne, F, f):
        for what, e_ in self.moe_order(ne, F):
            wg, wu, wd = f(e_)
            if what == "u":
                for j in range(F // 512):
                    for nm, w in (("g", wg), ("u", wu)):
                        for kh in range(2):
                            self.chunk((key, e_, nm, j, kh), 128, CW, lambda s, w=w, j=j, kh=kh: [
                                (s.rearrange("p (k n) -> p k n", k=4),
                                 w[512 * kh:512 * kh + 512, 512 * j:512 * j + 512].rearrange("(k p) n -> p k n", p=128))])
            else:
                for j in range(F // 256):
                    self.chunk((key, e_, "d", j), 128, CW, lambda s, j=j, wd=wd: [
                        (s.rearrange("p (i n) -> p i n", i=2),
                         wd[256 * j:256 * j + 256, :].rearrange("(i p) n -> p i n", p=128))])

    def moe_tiles(self, F):
        w = dict(hh=self.ph("hh", [128, 2, 1024], F32R), hl=self.ph("hl", [128, 2, 1024], F32R),
                 ah=self.ph("ah", [128, max(F // 128, 8), 128], F32R), al=self.ph("al", [128, max(F // 128, 8), 128], F32R),
                 sg=self.ph("sg", [128, 2, 512]), xg=self.xh, xgl=self.xl, sel=self.ph("sel", [128, 2, 2, 128], F32R),
                 selT=self.ph("selT", [128, 4 if F == 512 else 3, 2, 128], F32R), gs=self.ph("gs", [128, 4]),
                 yh=self.ph("yh", [128, 1024], F32R), yl=self.ph("yl", [128, 1024], F32R),
                 y=self.ph("y", [128, 2, 1024]), rk=self.ph("rk", [128, 2, 16]), one=self.ph("one", [128, 128]),
                 cnt=self.ph("cnt", [128, 2]), flag=self.flags[:, self.n_moe:self.n_moe + 1])
        self.n_moe += 1
        return w

    def moe_parts(self, w, src, tsrc):
        self.V.do(lambda e: e.memset(w["one"][:, :], 1.0))
        for t in range(2):
            ts = self.split(w["hh"][:, t, :], w["hl"][:, t, :], src(t), tsrc)
        return ts

    def moe_ranks(self, w, ne, masks, tm):
        V, T_, cst = self.V, self.T, self.cst
        b = self.take()
        p = self.ps[b]
        up = cst[:, C_UP:C_UP + 128]
        self.mm(p[:, 0:ne], up, masks[:, 0, 0:ne], True, True, tm)
        self.mm(p[:, 16:16 + ne], up, masks[:, 1, 0:ne], True, False)
        self.mm(p[:, 16:16 + ne], w["one"][:, :], masks[:, 0, 0:ne], False, True)
        self.mm(p[:, 32:32 + ne], w["one"][:, :], masks[:, 0, 0:ne], True, False)
        tok = self.mm(p[:, 32:32 + ne], w["one"][:, :], masks[:, 1, 0:ne], False, True)
        V.do(lambda e: e.tensor_copy(w["rk"][:, :, 0:ne], p[:, 0:32].rearrange("p (t n) -> p t n", t=2)[:, :, 0:ne]), tok)
        V.do(lambda e: e.tensor_reduce(w["cnt"][:, 0:1], p[:, 32:32 + ne], AX.X, ALU.max))
        tf = V.seq(lambda e: e.tensor_scalar(w["flag"][:, :], w["cnt"][:, 0:1], 128.0, None, ALU.is_gt))
        self.free(b, tf)
        return tf

    def moe_round(self, r, key, ne, F, w, masks, gates, ready, extra=()):
        V, A, T_, cst, ps = self.V, self.A, self.T, self.cst, self.ps
        Y = {(t, q): self.take() for t in range(2) for q in range(2)}
        nf, nj = F // 128, F // 512
        nb = 2 if F == 512 else 1
        ns = 4 if F == 512 else 3
        st = dict(act=[None] * nb, sel=[None, None], selT=[None] * ns, xg=[None, None], sg=[None, None], yh=None)
        got, turned, jobs, sel_ts = {}, {}, list(extra), {}
        T_.wait(*ready)
        at = dict(step=0, sg=0, due=0)

        def step(force=False):
            at["step"] += not force
            if force:
                jobs.sort(key=lambda x: x[0])
                jobs.pop(0)[1]()
                return
            for x in [x for x in jobs if x[0] <= at["step"]]:
                jobs.remove(x)
                x[1]()

        def later(f, n=1):
            jobs.append((at["step"] + n, f))

        def choose(e_):
            u = e_ % 2
            for t in range(2):
                sel_ts[e_] = V.do(lambda e, t=t: e.tensor_scalar(
                    w["sel"][:, u, t, :], cst[:, C_IO + 128 * r:C_IO + 128 * r + 128], w["rk"][:, t, e_:e_ + 1],
                    masks[:, t, e_:e_ + 1], ALU.is_equal, ALU.mult), st["sel"][u], *ready)

        def gather(e_):
            u, u3 = e_ % 2, e_ % ns
            sel, selT, gs = w["sel"][:, u], w["selT"][:, u3], w["gs"][:, u3:u3 + 1]
            ts = sel_ts[e_]

            def turn_sel():
                b = self.take()
                for t in range(2):
                    T_.run(lambda e, t=t: e.transpose(ps[b][:, 128 * t:128 * t + 128], sel[:, t, :].bitcast(F32),
                                                      cst[:, C_ID:C_ID + 128]), ts)
                for t in range(2):
                    tok = self.mm(ps[b][:, 256:257], sel[:, t, :].bitcast(F32), gates[:, t, e_:e_ + 1], t == 0, t == 1)
                A.do(lambda e: e.activation(selT.rearrange("p t n -> p (t n)"), ps[b][:, 0:256], ACT.Copy), tok, st["selT"][u3])
                got[e_] = [A.do(lambda e: e.activation(gs, ps[b][:, 256:257], ACT.Copy))]
                self.free(b, got[e_][0])

            def take_part(q, src, dst, eng):
                b = self.take()
                for k in range(4):
                    for t in range(2):
                        f = lambda e, b=b, k=k, t=t: e.matmul(
                            ps[b][:, 128 * k:128 * k + 128], src[:, t, 128 * (4 * q + k):128 * (4 * q + k) + 128],
                            sel[:, t, :], start=t == 0, stop=t == 1)
                        if k == 3 and t == 1:
                            tok = T_.do(f)
                        else:
                            T_.run(f)
                o = dst[:, 4 * q:4 * q + 4, 128 * u:128 * u + 128]
                x = ps[b][:, :].rearrange("p (k n) -> p k n", k=4)
                if eng is A:
                    z = A.do(lambda e: e.activation(o, x, ACT.Copy), tok, st["xg"][u])
                else:
                    z = V.do(lambda e: e.tensor_copy(o, x), tok, st["xg"][u])
                self.free(b, z)
                got[e_].append(z)
                st["sel"][u] = tok

            n = (1, 2, 3, 3, 4) if nb == 2 else (5, 6, 7, 8, 9)
            later(turn_sel, n[0])
            for q in range(2):
                later(lambda q=q: take_part(q, w["hh"], w["xg"], A), n[1 + 2 * q])
                later(lambda q=q: take_part(q, w["hl"], w["xgl"], A if nb == 1 else V), n[2 + 2 * q])

        def turn(e_, j, ta_, u):
            b = self.take()
            for i in range(4):
                tok = T_.do(lambda e, i=i: e.transpose(ps[b][:, 128 * i:128 * i + 128], w["sg"][:, u, 128 * i:128 * i + 128],
                                                       cst[:, C_ID:C_ID + 128]), ta_)
            st["sg"][u] = tok
            f = nf * (e_ % nb) + 4 * j
            o = [w[n][:, f:f + 4, :].rearrange("p k n -> p (k n)") for n in ("ah", "al")]
            ts = self.split(o[0], o[1], ps[b][:, :], tok, st["act"][e_ % nb])
            self.free(b, ts)
            turned[e_, j] = ts

        def scatter(e_, D, tok):
            while at["due"]:
                step(True)
            at["due"] = 2
            u = e_ % ns
            gs = w["gs"][:, u:u + 1]
            for q in range(2):
                o = slice(512 * q, 512 * q + 512)
                ta = A.do(lambda e, q=q, o=o: e.activation(w["yh"][:, o], ps[D[q]][:, :], ACT.Copy, scale=gs), tok, st["yh"])
                ty = V.do(lambda e, q=q, o=o: e.scalar_tensor_tensor(w["yl"][:, o], ps[D[q]][:, :], gs, w["yh"][:, o].bitcast(F32),
                                                                     ALU.mult, ALU.subtract), ta, st["yh"])
                self.free(D[q], ty)

            def products(t):
                T_.wait(ty)
                for q in range(2):
                    for n in ("yh", "yl"):
                        f = lambda e, t=t, q=q, n=n: e.matmul(
                            ps[Y[t, q]][:, :], w["selT"][:, u, t, :], w[n][:, 512 * q:512 * q + 512],
                            start=(e_ == 0 and n == "yh"), stop=(e_ == ne - 1 and n == "yl"))
                        if q == 1 and n == "yl":
                            z = T_.do(f)
                        else:
                            T_.run(f)
                if t == 1:
                    st["yh"] = st["selT"][u] = z
                at["z"] = z
                at["due"] -= 1
            later(lambda: products(0), 3)
            later(lambda: products(1), 4)

        def up(e_):
            u = e_ % 2
            while len(got.get(e_, ())) < 5:
                step(True)
            T_.wait(*got[e_])
            if e_ + 1 < ne:
                gather(e_ + 1)
            for j in range(nj):
                for nm in "gu":
                    b = self.take()
                    for kh in range(2):
                        c = self.next((key, e_, nm, j, kh))
                        wh, wl = (c[x].rearrange("p (k n) -> p k n", k=4) for x in ("hi", "lo"))
                        for k in range(4):
                            kk = 4 * kh + k
                            tok = self.mm3(ps[b][:, :], w["xg"][:, kk, 128 * u:128 * u + 128],
                                           w["xgl"][:, kk, 128 * u:128 * u + 128], wh[:, k, :], wl[:, k, :],
                                           kk == 0, kk == 7, mark=(k == 3))
                        if kh == 1 and nm == "g":
                            v = at["sg"] % 2
                            at["sg"] += 1
                            g = w["sg"][:, v, :]
                            t1 = A.do(lambda e, g=g, b=b: e.activation(g, ps[b][:, :], ACT.Silu), tok, st["sg"][v])
                            self.free(b, t1)
                        elif kh == 1:
                            t2 = V.do(lambda e, g=g, b=b: e.tensor_tensor(g, g, ps[b][:, :], ALU.mult), t1, tok)
                            self.free(b, t2)
                            later(lambda e_=e_, j=j, t2=t2, v=v: turn(e_, j, t2, v), 2)
                        self.done(c, tok)
                        step()
            st["xg"][u] = tok
            if e_ + 2 < ne:
                choose(e_ + 2)

        def down(e_):
            o = nf * (e_ % nb)
            D = [self.take() for _ in range(2)]
            for j in range(F // 256):
                while (e_, j // 2) not in turned:
                    step(True)
                T_.wait(turned[e_, j // 2])
                c = self.next((key, e_, "d", j))
                wh, wl = (c[x].rearrange("p (i n) -> p i n", i=2) for x in ("hi", "lo"))
                for i in range(2):
                    f = 2 * j + i
                    for q in range(2):
                        tok = self.mm3(ps[D[q]][:, :], w["ah"][:, o + f, :], w["al"][:, o + f, :], wh[:, i, 512 * q:512 * q + 512],
                                       wl[:, i, 512 * q:512 * q + 512], f == 0, f == nf - 1, mark=(i == 1 and q == 1))
                if j == F // 256 - 1:
                    st["act"][e_ % nb] = tok
                    scatter(e_, D, tok)
                self.done(c, tok)
                step()

        choose(0)
        choose(1)
        gather(0)
        for what, e_ in self.moe_order(ne, F):
            (up if what == "u" else down)(e_)
        while jobs:
            step(True)
        for (t, q), b in Y.items():
            o = w["y"][:, t, 512 * q:512 * q + 512]
            if r == 0:
                z = V.do(lambda e, o=o, b=b: e.tensor_copy(o, ps[b][:, :]), at["z"], w.get("y_free"))
            else:
                z = V.do(lambda e, o=o, b=b: e.tensor_tensor(o, o, ps[b][:, :], ALU.add), at["z"])
            self.free(b, z)
        return z

    def moe(self, key, ne, F, w, masks, gates, ready, again, extra=()):
        tf = self.moe_ranks(w, ne, masks, ready[0])
        z = self.moe_round(0, key, ne, F, w, masks, gates, (tf, *ready), extra)
        self.begin_if(key, w["flag"][0:1, 0:1], again, tf)
        self.moe_round(1, key, ne, F, w, masks, gates, ())
        self.end_if()
        return z

    def ffn(self, key, F, tiles, c0, n, xh, xl, ah, al, tx):
        V, A, T_ = self.V, self.A, self.T
        self.T.wait(tx)
        ta = None
        for j in range(F // 256):
            bs = {}
            for nm in "gu":
                c = self.next((key, nm, j))
                wh = c["hi"].rearrange("p (k n) -> p k n", k=8)
                wl = c["lo"].rearrange("p (k n) -> p k n", k=8)
                for i in range(2):
                    b = self.take()
                    for k in range(8):
                        tok = self.mm3(self.ps[b][:, 0:n], wh[:, k, i * 128:i * 128 + 128], wl[:, k, i * 128:i * 128 + 128],
                                       xh[:, k, c0:c0 + n], xl[:, k, c0:c0 + n], k == 0, k == 7)
                    bs[nm, i] = (b, tok)
                self.done(c, tok)
            for i in range(2):
                f = 2 * j + i
                bg, tg = bs["g", i]
                bu, tu = bs["u", i]
                z = self.sg_at
                self.sg_at = (z + 1) % 4
                g = self.sg[:, z, 0:n]
                t1 = A.do(lambda e, g=g, b=bg: e.activation(g, self.ps[b][:, 0:n], ACT.Silu), tg, self.sg_free[z])
                self.free(bg, t1)
                t2 = V.do(lambda e, g=g, b=bu: e.tensor_tensor(g, g, self.ps[b][:, 0:n], ALU.mult), t1, tu)
                self.free(bu, t2)
                ta = self.split(ah[:, f, 0:n], al[:, f, 0:n], g, t2, self.act_free)
                self.sg_free[z] = ta
        acc = {(t, q): self.take() for t, _, _ in tiles for q in range(2)}
        self.T.wait(ta)
        nf = F // 128
        for j in range(F // 256):
            c = self.next((key, "d", j))
            wh = c["hi"].rearrange("p (i n) -> p i n", i=2)
            wl = c["lo"].rearrange("p (i n) -> p i n", i=2)
            for i in range(2):
                f = 2 * j + i
                for t, nt, cc in tiles:
                    for q in range(2):
                        o = self.ps[acc[t, q]][0:nt, :]
                        a = slice(cc - c0, cc - c0 + nt)
                        tok = self.mm3(o, ah[:, f, a], al[:, f, a], wh[:, i, q * 512:q * 512 + 512],
                                       wl[:, i, q * 512:q * 512 + 512], f == 0, f == nf - 1,
                                       mark=(i == 1 and t == tiles[-1][0] and q == 1))
            self.done(c, tok)
        self.act_free = tok
        return acc, tok


def build(nc, d, out, dumps=None):
    P = Program(nc, d, out, dumps)
    T_, V, A, G, S = P.T, P.V, P.A, P.G, P.S
    P.loads = []
    P.banks_init()
    ps = P.ps
    P.cst = cst = P.sb("cst", [128, C_END])
    P.xh = xh = P.sb("xh", [128, 8, T], F32R)
    P.xl = xl = P.sb("xl", [128, 8, T], F32R)
    P.h = h = P.sb("h", [128, 3, 1024])
    lnt = P.sb("lnt", [128, 2048])
    P.lng, P.lnb = lnt[:, 0:1024], lnt[:, 1024:2048]
    P.st = P.sb("st", [128, 8, 2, 6])
    P.mv = P.sb("mv", [128, 3, 2])
    P.rs = P.sb("rs", [128, 2, 32])
    P.rtmp = P.sb("rtmp", [128, 32])
    rwr = P.sb("rwr", [128, 8, 32])
    rwh = P.sb("rwh", [128, 8, 32], F32R)
    rwl = P.sb("rwl", [128, 8, 32], F32R)
    gates = P.sb("gates", [128, 2, 16])
    masks = P.sb("masks", [128, 2, 16])
    gw = P.sb("gw", [128, 2, 64])
    gi = P.sb("gi", [128, 2, 8], U32)
    colA = P.sb("colA", [128, 128])
    colB = P.sb("colB", [128, 18])
    modc = P.sb("modc", [128, 48])
    row1 = P.sb("row1", [1, 512])
    P.flags, P.n_moe = P.sb("flags", [128, 2], I32), 0
    P.ln_free = None
    P.act_free = None
    P.stream_init()

    w_rg, w_ro = d["rg_w_in"][0], d["rg_w_out"][0]

    def plan_rg(key, off):
        for j in range(6):
            P.chunk((key, j), 128, 8 * 224, lambda s, j=j: [
                (s.rearrange("p (k n) -> p k n", k=8),
                 w_rg[:, off + 224 * j:off + 224 * j + 224].rearrange("(k p) n -> p k n", p=128))])

    w_ada = d["w_ada_2"][0]
    n_ada = [0]

    def plan_ada(n):
        for j in range(n_ada[0], n_ada[0] + n):
            P.chunk(("ada", j), 128, CW, lambda s, j=j: [
                (s.rearrange("p (k n) -> p k n", k=8),
                 w_ada[:, 256 * j:256 * j + 256].rearrange("(k p) n -> p k n", p=128))], split=False)
        n_ada[0] += n

    plan_rg("xr", 1344)
    wgt = d["rg_w_gates"][0]
    for j in range(4):
        def pieces(s, j=j):
            v = s.rearrange("p (g k n) -> p g k n", g=2, k=3)
            a, b = wgt[:, 2 * j].rearrange("g c n -> c g n"), wgt[:, 2 * j + 1].rearrange("g c n -> c g n")
            return [(v[0:112, :, 0, 0:168], a[0:112]), (v[0:56, :, 1, 0:168], a[112:168]),
                    (v[56:112, :, 1, 168:336], b[0:56]), (v[0:112, :, 2, 168:336], b[56:168])]
        P.chunk(("gt", j), 112, 2 * 3 * 336, pieces, zero=True)
    plan_rg("gb", 0)
    for j in range(6):
        P.chunk(("ro", j), 112, CW, lambda s, j=j: [
            (s.rearrange("p (i n) -> p i n", i=2),
             w_ro[224 * j:224 * j + 224, :].rearrange("(i p) n -> p i n", p=112))])
    plan_ada(8)
    P.plan_ffn("ffn", d["ffn_w_in"][0][:, 0:3584], d["ffn_w_in"][0][:, 3584:7168], d["ffn_w_out"][0], 3584)
    plan_ada(8)
    w_gl = d["gla_w_in"][0]
    P.chunk("gz", 128, 128, lambda s: [(s.rearrange("p (k n) -> p k n", k=8),
                                        w_gl[:, 3072:3088].rearrange("(k p) n -> p k n", p=128))])

    def plan_cols(key, w, off, m, wd=256, first=0):
        for j in range(first, m):
            P.chunk((key, j), 128, 8 * wd, lambda s, j=j: [
                (s.rearrange("p (k n) -> p k n", k=8),
                 w[:, off + wd * j:off + wd * j + wd].rearrange("(k p) n -> p k n", p=128))])

    def plan_rows(key, w, m):
        for j in range(m):
            P.chunk((key, j), 128, CW, lambda s, j=j: [
                (s.rearrange("p (i n) -> p i n", i=2),
                 w[256 * j:256 * j + 256, :].rearrange("(i p) n -> p i n", p=128))])

    plan_cols("gk", w_gl, 512, 2)
    plan_cols("gq", w_gl, 0, 2)
    plan_cols("gv", w_gl, 1024, 4)
    plan_cols("gr", w_gl, 2048, 4)
    plan_rows("go", d["gla_w_out"][0], 4)
    plan_ada(8)
    again = {}

    def plan_experts(key, ne, f, F):
        for twice in range(2):
            before = P.chunks
            if twice:
                P.chunks = again[key] = []
            P.plan_moe(key, ne, F, f)
            P.chunks = before

    plan_experts("m1", 8, lambda e: (d["moe_w_in"][0, e][:, 0:3584], d["moe_w_in"][0, e][:, 3584:7168], d["moe_w_out"][0, e]), 3584)
    fence1 = len(P.chunks)
    w_i2 = d["w_in_2"][0]
    plan_cols("wi", w_i2, 0, 5)
    for j in range(2):
        P.chunk(("uq", j), 128, 3 * 384, lambda s, j=j: [
            (s.rearrange("p (k n) -> p k n", k=3),
             d["w_uq_2"][0][:, 384 * j:384 * j + 384].rearrange("(k p) n -> p k n", p=128))])
    P.chunk("ukv", 128, 2 * 1024, lambda s: [(s.rearrange("p (k n) -> p k n", k=2),
                                              d["w_ukv_2"][0].rearrange("(k p) n -> p k n", p=128))])
    plan_cols("wi", w_i2, 0, 8, first=5)
    P.chunk(("wi", 8), 128, 8 * 160, lambda s: [(s.rearrange("p (k n) -> p k n", k=8),
                                                 w_i2[:, 2048:2208].rearrange("(k p) n -> p k n", p=128))])
    plan_rows("wo", d["w_o_2"][0], 4)
    plan_experts("m2", 16, lambda e: (d["w_gate_2"][0, e], d["w_up_2"][0, e], d["w_down_2"][0, e]), 512)
    P.fence = fence1

    P.phase()
    t_c = P.load(S, cst[:, :], d["consts"])
    t_h = [P.load(S, h[0:16, 2, :], d["meta_tokens"]), P.load(S, h[:, 0, :], d["x"][0, 0:128]),
           P.load(S, h[:, 1, :], d["x"][0, 128:256])]
    vec = lnt[0:8, 0:1344]
    t_v = [P.load(S, vec[0:4, :], d["rg_conv_w"][0]), P.load(S, vec[4:5, :], d["rg_conv_b"]),
           P.load(S, vec[5:7, :], d["rg_b_gates"][0]), P.load(S, vec[7:8, :], d["rg_lambda"])]
    rowA, rowB = lnt[:, 1344:1472], lnt[0:18, 1472:1600]
    s_row, n_row = P.sem("s_row"), [0]
    t_z = V.do(lambda e: e.memset(rowB, 0.0))
    flat8 = lambda a: a.rearrange("a (k p) -> (a k) p", p=128)
    rowsA = [(0, 32, d["ln_gain"].rearrange("i j (k p) -> (i j k) p", p=128)),
             (32, 64, d["ln_bias"].rearrange("i j (k p) -> (i j k) p", p=128)),
             (64, 112, flat8(d["b_ada_2"])), (112, 120, flat8(d["norm1_g_2"])), (120, 128, flat8(d["c_2"]))]
    rowsB = [(0, 8, 0, 128, flat8(d["norm2_g_2"])), (8, 11, 0, 128, flat8(d["mla_cq_g_2"])),
             (11, 13, 0, 128, flat8(d["mla_ckv_g_2"])), (13, 14, 0, 64, d["diff_q_g_2"]), (13, 14, 64, 128, d["diff_q_g_2"]),
             (14, 15, 0, 64, d["diff_k_g_2"]), (14, 15, 64, 128, d["diff_k_g_2"]), (15, 16, 0, 96, d["mla_q_g_2"]),
             (16, 17, 0, 96, d["mla_k_g_2"]), (17, 18, 0, 128, d["diff_subln_g_2"])]
    for a, z, s in rowsA:
        G.dma(lambda e, a=a, z=z, s=s: e.dma_start(rowA[a:z, :], s), s_row, n_row)
    for a, z, o, m, s in rowsB:
        t_row = G.dma(lambda e, a=a, z=z, o=o, m=m, s=s: e.dma_start(rowB[a:z, o:m], s), s_row, n_row, t_z)
    vT = P.ph("vT", [112, 12, 8])
    sp = P.ph("sp", [112, 6, 12])
    X1 = P.ph("X1", [112, 12, 275])
    X2 = P.ph("X2", [112, 12, T])
    xch = P.ph("xch", [112, 12, T], F32R)
    xcl = P.ph("xcl", [112, 12, T], F32R)
    R = P.ph("R", [112, 12, T])
    I = P.ph("I", [112, 12, T])

    P.pump()
    t_x = P.make_T(lambda t, k: h[0:(16 if t == 2 else 128), t, 128 * k:128 * k + 128], TILES, 8, xh, xl, t_c, *t_h)
    b = P.take()
    for c in range(12):
        tok = T_.do(lambda e, c=c, b=b: e.transpose(ps[b][0:112, 8 * c:8 * c + 8], vec[:, 112 * c:112 * c + 112],
                                                    cst[0:8, C_ID:C_ID + 8]), *t_v, t_c)
    tv = V.do(lambda e, b=b: e.tensor_copy(vT[:, :, :], ps[b][0:112, 0:96].rearrange("p (c n) -> p c n", n=8)), tok)
    P.free(b, tv)
    b = P.take()
    T_.do(lambda e, b=b: e.transpose(ps[b][:, 0:128], rowA, cst[:, C_ID:C_ID + 128]), t_row)
    tok = T_.do(lambda e, b=b: e.transpose(ps[b][:, 128:146], rowB, cst[0:18, C_ID:C_ID + 18]))
    V.do(lambda e, b=b: e.tensor_copy(colA[:, :], ps[b][:, 0:128]), tok)
    t_col = V.do(lambda e, b=b: e.tensor_copy(colB[:, :], ps[b][:, 128:146]))
    P.free(b, t_col)
    P.ln_free = t_col
    lam = vT[:, :, 7]
    ex = A.do(lambda e: e.activation(sp[:, 0, :], lam, ACT.Abs), tv)
    ex = A.seq(lambda e: e.activation(sp[:, 0, :], sp[:, 0, :], ACT.Exp, scale=-1.0))
    V.seq(lambda e: e.tensor_scalar(sp[:, 1, :], sp[:, 0, :], 2.0, None, ALU.add), ex)
    V.seq(lambda e: e.reciprocal(sp[:, 1, :], sp[:, 1, :]))
    V.seq(lambda e: e.tensor_tensor(sp[:, 1, :], sp[:, 1, :], sp[:, 0, :], ALU.mult))
    V.seq(lambda e: e.tensor_tensor(sp[:, 2, :], sp[:, 1, :], sp[:, 1, :], ALU.mult))
    V.seq(lambda e: e.memset(sp[:, 3, :], 1.0 / 17.0))
    for m in (15, 13, 11, 9, 7, 5, 3, 1):
        V.seq(lambda e: e.tensor_tensor(sp[:, 3, :], sp[:, 3, :], sp[:, 2, :], ALU.mult))
        V.seq(lambda e, m=m: e.tensor_scalar(sp[:, 3, :], sp[:, 3, :], 1.0 / m, None, ALU.add))
    V.seq(lambda e: e.tensor_tensor(sp[:, 3, :], sp[:, 3, :], sp[:, 1, :], ALU.mult))
    V.seq(lambda e: e.tensor_scalar(sp[:, 4, :], lam, -1.0, 0.0, ALU.mult, ALU.max))
    V.seq(lambda e: e.scalar_tensor_tensor(sp[:, 5, :], sp[:, 3, :], 2.0, sp[:, 4, :], ALU.mult, ALU.add))
    t_sp = V.seq(lambda e: e.tensor_scalar(sp[:, 5, :], sp[:, 5, :], 4.0, None, ALU.mult))
    V.seq(lambda e: e.memset(X1[:, :, 0:3], 0.0))

    def rg_in(key, j, evac):
        c = P.next((key, j))
        wh = c["hi"].rearrange("p (k n) -> p k n", k=8)
        wl = c["lo"].rearrange("p (k n) -> p k n", k=8)
        for i in range(2):
            b = P.take()
            for k in range(8):
                tok = P.mm3(ps[b][0:112, 0:T], wh[:, k, 112 * i:112 * i + 112], wl[:, k, 112 * i:112 * i + 112],
                            xh[:, k, :], xl[:, k, :], k == 0, k == 7)
            if i == 1:
                P.done(c, tok)
            P.free(b, evac(2 * j + i, ps[b][0:112, 0:T], tok))

    t_xc = {}

    def conv(m, pt, tok):
        te = A.do(lambda e: e.activation(X1[:, m, 3:275], pt, ACT.Copy), tok)
        t2 = A.do(lambda e: e.activation(X2[:, m, :], pt, ACT.Identity, bias=vT[:, m, 4:5], scale=vT[:, m, 3:4]))
        V.wait(te, t2)
        for q in range(3):
            t = V.seq(lambda e, q=q: e.scalar_tensor_tensor(X2[:, m, :], X1[:, m, q:q + T], vT[:, m, q:q + 1],
                                                            X2[:, m, :], ALU.mult, ALU.add))
        t_xc[m] = P.split(xch[:, m, :], xcl[:, m, :], X2[:, m, :], t)
        return t2

    T_.wait(t_x)
    for j in range(6):
        rg_in("xr", j, conv)
    Qt = X1[:, :, 0:T]
    t_hs = {}

    def scan(j, t_in):
        z = slice(3 * j, 3 * j + 3)
        ts = A.do(lambda e: e.activation(R[:, z, :], R[:, z, :], ACT.Sqrt), t_in)
        for m in range(3 * j, 3 * j + 3):
            V.do(lambda e, m=m: e.scalar_tensor_tensor(I[:, m, :], R[:, m, :], 2.0, I[:, m, :], ALU.mult, ALU.mult), V.last, ts)
        for m in range(3 * j, 3 * j + 3):
            t_hs[m] = V.do(lambda e, m=m: e.tensor_tensor_scan(Qt[:, m, :], X2[:, m, :], I[:, m, :], 0.0, ALU.mult, ALU.add), V.last)

    for j in range(4):
        c = P.next(("gt", j))
        wh = c["hi"].rearrange("p (g k n) -> p g k n", g=2, k=3)
        wl = c["lo"].rearrange("p (g k n) -> p g k n", g=2, k=3)
        T_.wait(t_xc[3 * j + 2])
        tt = []
        for mt in range(3):
            for g in range(2):
                b = P.take()
                kts = ([0, 1], [0, 1, 2], [1, 2])[mt]
                for kt in kts:
                    tok = P.mm3(ps[b][0:112, 0:T], wh[:, g, kt, 112 * mt:112 * mt + 112], wl[:, g, kt, 112 * mt:112 * mt + 112],
                                xch[:, 3 * j + kt, :], xcl[:, 3 * j + kt, :], kt == kts[0], kt == kts[-1])
                m = 3 * j + mt
                dst = (R, I)[g][:, m, :]
                t = A.do(lambda e, dst=dst, b=b, g=g, m=m: e.activation(dst, ps[b][0:112, 0:T], ACT.Sigmoid,
                                                                        bias=vT[:, m, 5 + g:6 + g]), tok)
                P.free(b, t)
            tt.append(A.seq(lambda e, m=m: e.activation(R[:, m, :], R[:, m, :], ACT.Tanh, scale=sp[:, 5, m:m + 1]), t_sp))
        P.done(c, tok)
        z = slice(3 * j, 3 * j + 3)
        V.seq(lambda e, z=z: e.tensor_scalar(Qt[:, z, :], R[:, z, :], 1.0, None, ALU.add), *tt)
        V.seq(lambda e, z=z: e.reciprocal(Qt[:, z, :], Qt[:, z, :]))
        V.seq(lambda e, z=z: e.tensor_tensor(I[:, z, :], I[:, z, :], X2[:, z, :], ALU.mult))
        V.seq(lambda e, z=z: e.tensor_scalar(X2[:, z, :], R[:, z, :], -1.0, 1.0, ALU.mult, ALU.add))
        V.seq(lambda e, z=z: e.tensor_tensor(X2[:, z, :], X2[:, z, :], Qt[:, z, :], ALU.mult))
        t_gate = V.seq(lambda e, z=z: e.tensor_tensor(I[:, z, :], I[:, z, :], Qt[:, z, :], ALU.mult))
        if j:
            scan(j - 1, before)
        before = t_gate
    scan(3, before)
    t_y = {}

    def gbr(m, pt, tok):
        te = A.do(lambda e: e.activation(R[:, m, :], pt, ACT.Gelu_apprx_tanh), tok, t_hs[m])
        t = V.seq(lambda e: e.tensor_tensor(I[:, m, :], R[:, m, :], Qt[:, m, :], ALU.mult), te)
        t_y[m] = P.split(xch[:, m, :], xcl[:, m, :], I[:, m, :], t)
        return te

    for j in range(6):
        rg_in("gb", j, gbr)
    acc = {(t, q): P.take() for t, _, _ in TILES for q in range(2)}
    for j in range(6):
        c = P.next(("ro", j))
        wh = c["hi"].rearrange("p (i n) -> p i n", i=2)
        wl = c["lo"].rearrange("p (i n) -> p i n", i=2)
        for i in range(2):
            m = 2 * j + i
            T_.wait(t_y[m])
            for t, n, cc in TILES:
                for q in range(2):
                    tok = P.mm3(ps[acc[t, q]][0:n, :], xch[:, m, cc:cc + n], xcl[:, m, cc:cc + n],
                                wh[:, i, 512 * q:512 * q + 512], wl[:, i, 512 * q:512 * q + 512], m == 0, m == 11,
                                mark=(i == 1 and t == TILES[-1][0] and q == 1))
        P.done(c, tok)

    silc = colA[:, 120:128]
    t_silc = A.do(lambda e: e.activation(silc, silc, ACT.Silu), t_col)
    ada_row = [row1[:, 0:256], row1[:, 256:512]]
    ada = dict(at=0, free=[None, None])

    def modulation(n):
        P.hold = True

        def columns(j, tr):
            b = P.take()
            row = ada_row[j % 2]
            for i in range(2):
                tok = T_.do(lambda e, i=i: e.transpose(ps[b][:, i:i + 1], row[:, 128 * i:128 * i + 128],
                                                       cst[0:1, C_ID:C_ID + 1]), tr)
            ada["free"][j % 2] = tok
            for i in range(2):
                z = A.do(lambda e, i=i: e.activation(modc[:, 2 * j + i:2 * j + i + 1], ps[b][:, i:i + 1], ACT.Identity,
                                                     bias=colA[:, 64 + 2 * j + i:65 + 2 * j + i]), tok)
            P.free(b, z)
            ada["done"] = z

        todo = None
        for j in range(ada["at"], ada["at"] + n):
            c = P.next(("ada", j))
            w = c["raw"].rearrange("p (k n) -> p k n", k=8)
            b = P.take()
            for k in range(8):
                tok = P.mm(ps[b][0:1, 0:256], silc[:, k:k + 1], w[:, k, :], k == 0, k == 7, t_silc)
            tr = A.do(lambda e, b=b, j=j: e.activation(ada_row[j % 2], ps[b][0:1, 0:256], ACT.Copy), tok, ada["free"][j % 2])
            P.free(b, tr)
            P.done(c, tok)
            if todo is not None:
                columns(*todo)
            todo = (j, tr)
        columns(*todo)
        ada["at"] += n
        P.hold = False

    def end_block(acc, tiles, gi, tok):
        t = P.layer_norm(tiles, lambda t, q: ps[acc[t, q]][0:(16 if t == 2 else 128), :], gi, tok)
        modulation(8)
        for b in acc.values():
            P.free(b, P.ln_read)
        return t

    t_ln = end_block(acc, TILES, (0, 0), tok)
    P.dump("h0", h[:, 0:2, :], t_ln)
    src_h = lambda t, k: h[0:(16 if t == 2 else 128), t, 128 * k:128 * k + 128]
    t_x = P.make_T(src_h, TILES, 8, xh, xl, t_ln)

    def ffn_tiles(nf=28):
        P.sg = P.ph(f"sg{P.nsem}", [128, 4, T])
        P.sg_at, P.sg_free = 0, [None] * 4
        ah = P.ph(f"ah{P.nsem}", [128, nf, T], F32R)
        al = P.ph(f"al{P.nsem}", [128, nf, T], F32R)
        return ah, al

    P.phase()
    ah, al = ffn_tiles()
    acc, tok = P.ffn("ffn", 3584, TILES, 0, T, xh, xl, ah, al, t_x)
    t_ln = end_block(acc, TILES, (0, 1), tok)
    P.dump("h1", h[:, 0:2, :], t_ln)
    t_x = P.make_T(src_h, TILES, 8, xh, xl, t_ln)

    def router_load(srcs, *toks):
        tl = []
        o = 0
        for s, m in srcs:
            tl.append(P.load(G, rwr[:, :, o:o + m], s.rearrange("(k p) n -> p k n", p=128), *toks))
            o += m
        return lambda: P.split(rwh[:, :, 0:o], rwl[:, :, 0:o], rwr[:, :, 0:o], *tl)

    P.phase()
    split_rw = router_load([(d["moe_router"][0], 8)])
    wgu = h[0:16, 2, 0:512]
    bgr = P.ph("bgr", [4, 128])
    ngb = P.ph("ngb", [128, 1024])
    t_wgu = P.load(G, wgu, d["gla_w_gate_up"][0], *[q.last for q in (T_, V, A)])
    t_bgr = P.load(G, bgr[:, :], d["gla_b_gate"][0].rearrange("(a n) -> a n", a=4))
    t_ngb = P.load(G, ngb[:, :], d["gla_norm_g"][0].rearrange("(a h) n -> a (h n)", a=1).partition_broadcast(128))
    bgT = P.ph("bgT", [128, 4])
    zT = P.ph("zT", [16, T])
    lg = P.ph("lg", [128, 4, T])
    bb = P.ph("bb", [128, 4, T])
    E1 = P.ph("E1", [128, 4, T])
    E2 = P.ph("E2", [128, 4, T])
    E3 = P.ph("E3", [128, 4, T])
    E4 = P.ph("E4", [128, 4, T])
    kot = P.ph("kot", [128, 3, 512])
    vt = P.ph("vt", [128, 3, 1024])
    rt = P.ph("rt", [128, 2, 1024])
    Sst = P.ph("Sst", [128, 4, 1024])
    sc = P.ph("sc", [128, 2, 512])
    og = rt
    mv8 = P.ph("mv8", [128, 8, 2])

    t_zero = V.do(lambda e: e.memset(sc[:, :, :], 0.0))
    b = P.take()
    tok = T_.do(lambda e, b=b: e.transpose(ps[b][:, 0:4], bgr[:, :], cst[0:4, C_ID:C_ID + 4]), t_bgr)
    t_bg = V.do(lambda e, b=b: e.tensor_copy(bgT[:, :], ps[b][:, 0:4]), tok)
    P.free(b, t_bg)
    T_.wait(t_x)
    c = P.next("gz")
    wh, wl = (c[s].rearrange("p (k n) -> p k n", k=8) for s in ("hi", "lo"))
    b = P.take()
    for k in range(8):
        tok = P.mm3(ps[b][0:16, 0:T], wh[:, k, :], wl[:, k, :], xh[:, k, :], xl[:, k, :], k == 0, k == 7)
    P.done(c, tok)
    t_z = A.do(lambda e, b=b: e.activation(zT[:, :], ps[b][0:16, 0:T], ACT.Copy), tok)
    P.free(b, t_z)
    for hh in range(4):
        b = P.take()
        tok = P.mm(ps[b][:, 0:T], wgu[:, 128 * hh:128 * hh + 128], zT[:, :], True, True, t_z, t_wgu)
        t = V.do(lambda e, b=b, hh=hh: e.tensor_scalar(lg[:, hh, :], ps[b][:, 0:T], bgT[:, hh:hh + 1], None, ALU.add),
                 tok, t_bg)
        P.free(b, t)
    fl = lambda a: a[:, :, :].rearrange("p h n -> p (h n)")
    A.do(lambda e: e.activation(fl(E1), fl(lg), ACT.Abs), t)
    A.seq(lambda e: e.activation(fl(E1), fl(E1), ACT.Exp, scale=-1.0))
    ta = A.seq(lambda e: e.activation(fl(E1), fl(E1), ACT.Ln, bias=1.0))
    V.seq(lambda e: e.scalar_tensor_tensor(fl(lg), fl(lg), 0.0, fl(E1), ALU.min, ALU.subtract), ta)
    for hh in range(4):
        t_b = V.seq(lambda e, hh=hh: e.tensor_tensor_scan(bb[:, hh, :], cst[:, C_SM:C_SM + T], lg[:, hh, :], 0.0,
                                                          ALU.mult, ALU.add))
    dec = lg
    for hh in range(4):
        bx = bb[:, hh, 16:272].rearrange("p (c s) -> p c s", s=64)
        dx = dec[:, hh, 16:272].rearrange("p (c s) -> p c s", s=64)
        V.do(lambda e, bx=bx, dx=dx: e.tensor_tensor(dx, bx, bx[:, :, 31:32].to_broadcast([128, 4, 64]), ALU.subtract), t_b)
        V.do(lambda e, hh=hh: e.tensor_copy(dec[:, hh, 0:16], bb[:, hh, 0:16]))
    t_d = V.last
    A.do(lambda e: e.activation(fl(E1), fl(dec), ACT.Exp, scale=1.0 / 16), t_d)
    te2 = A.do(lambda e: e.activation(fl(E2), fl(dec), ACT.Exp, scale=-1.0 / 16))
    te3 = A.do(lambda e: e.activation(fl(E3), fl(bb), ACT.Exp, scale=1.0 / 16))
    for hh in range(4):
        bx = bb[:, hh, 16:272].rearrange("p (c s) -> p c s", s=64)
        dx = dec[:, hh, 16:272].rearrange("p (c s) -> p c s", s=64)
        V.do(lambda e, bx=bx, dx=dx: e.tensor_tensor(dx, bx[:, :, 63:64].to_broadcast([128, 4, 64]), bx, ALU.subtract), te3)
        t_d = V.do(lambda e, hh=hh: e.tensor_tensor(dec[:, hh, 0:16], bb[:, hh, 15:16].to_broadcast([128, 16]),
                                                    bb[:, hh, 0:16], ALU.subtract))
    te4 = A.do(lambda e: e.activation(fl(E4), fl(dec), ACT.Exp, scale=1.0 / 16), t_d)
    tdc = V.do(lambda e: e.tensor_copy(gw[:, 0, 0:16].rearrange("p (h c) -> p h c", h=4),
                                       E3[:, :, 16:272].rearrange("p h (c s) -> p h c s", s=64)[:, :, :, 63]), te3)
    decs = gw[:, 0, 0:16].rearrange("p (h c) -> p h c", h=4)

    def chan(key, j, evac):
        c = P.next((key, j))
        wh, wl = (c[s].rearrange("p (k n) -> p k n", k=8) for s in ("hi", "lo"))
        for i in range(2):
            b = P.take()
            for k in range(8):
                tok = P.mm3(ps[b][:, 0:T], wh[:, k, 128 * i:128 * i + 128], wl[:, k, 128 * i:128 * i + 128],
                            xh[:, k, :], xl[:, k, :], k == 0, k == 7)
            if i == 1:
                P.done(c, tok)
            P.free(b, evac(2 * j + i, ps[b][:, 0:T], tok))

    def ev_k(m, pt, tok):
        V.do(lambda e: e.tensor_tensor(E2[:, m, :], pt, E2[:, m, :], ALU.mult), tok, te2)
        return V.do(lambda e: e.tensor_tensor(E4[:, m, :], pt, E4[:, m, :], ALU.mult), te4)

    def ev_q(m, pt, tok):
        s = 128.0 ** -0.5
        V.do(lambda e: e.scalar_tensor_tensor(E1[:, m, :], pt, s, E1[:, m, :], ALU.mult, ALU.mult), tok)
        return V.do(lambda e: e.scalar_tensor_tensor(E3[:, m, :], pt, s, E3[:, m, :], ALU.mult, ALU.mult), tdc)

    for j in range(2):
        chan("gk", j, ev_k)
    t_k = V.last
    for j in range(2):
        chan("gq", j, ev_q)
    t_q = V.last
    for t, n, cc in TILES:
        b = P.take()
        for hh in range(4):
            tok = T_.do(lambda e, b=b, n=n, cc=cc, hh=hh: e.transpose(ps[b][0:n, 128 * hh:128 * hh + 128], E4[:, hh, cc:cc + n],
                                                                      cst[:, C_ID:C_ID + 128]), t_k)
        t_ko = A.do(lambda e, b=b, n=n, t=t: e.activation(kot[0:n, t, :], ps[b][0:n, :], ACT.Copy), tok)
        P.free(b, t_ko)
    for t, n, cc in XTILES:
        b = P.take()
        for hh in range(4):
            tok = P.mm(ps[b][:, 128 * hh:128 * hh + 128], E2[:, hh, cc:cc + 128], E1[:, hh, cc:cc + 128], True, True, t_q)
        for hh in range(4):
            t_s = V.do(lambda e, b=b, t=t, hh=hh: e.copy_predicated(sc[:, t, 128 * hh:128 * hh + 128],
                                                                    cst[:, C_CM:C_CM + 128].bitcast(U32),
                                                                    ps[b][:, 128 * hh:128 * hh + 128]), tok, t_zero)
        P.free(b, t_s)

    def tokm(key, j, tiles, evac):
        c = P.next((key, j))
        n = c["n"] // 8
        wh, wl = (c[s].rearrange("p (k n) -> p k n", k=8) for s in ("hi", "lo"))
        for t, nt, cc in tiles:
            b = P.take()
            for k in range(8):
                tok = P.mm3(ps[b][0:nt, 0:n], xh[:, k, cc:cc + nt], xl[:, k, cc:cc + nt], wh[:, k, :], wl[:, k, :],
                            k == 0, k == 7)
            if t == tiles[-1][0]:
                P.done(c, tok)
            P.free(b, evac(t, nt, j, ps[b][0:nt, 0:n], tok))

    for j in range(4):
        tokm("gv", j, TILES, lambda t, n, j, pt, tok: A.do(
            lambda e: e.activation(vt[0:n, t, 256 * j:256 * j + 256], pt, ACT.Copy), tok))
    t_vt = A.last
    for j in range(4):
        tokm("gr", j, XTILES, lambda t, n, j, pt, tok: A.do(
            lambda e: e.activation(rt[0:n, t, 256 * j:256 * j + 256], pt, ACT.Silu), tok))
    t_rt = A.last
    t_rw = split_rw()
    t_S = None
    for ch in range(4):
        t, p0, n = ((2, 0, 16), (0, 0, 64), (0, 64, 64), (1, 0, 64))[ch]
        for pr in range(2):
            b = P.take()
            for hh in (2 * pr, 2 * pr + 1):
                tok = P.mm(ps[b][:, 256 * (hh % 2):256 * (hh % 2) + 256], kot[p0:p0 + n, t, 128 * hh:128 * hh + 128],
                           vt[p0:p0 + n, t, 256 * hh:256 * hh + 256], True, True, t_vt, t_ko)
            for hh in (2 * pr, 2 * pr + 1):
                o, a = Sst[:, ch, 256 * hh:256 * hh + 256], ps[b][:, 256 * (hh % 2):256 * (hh % 2) + 256]
                if ch == 0:
                    t_S = V.do(lambda e, o=o, a=a: e.tensor_copy(o, a), tok)
                else:
                    t_S = V.seq(lambda e, o=o, a=a, hh=hh, ch=ch: e.scalar_tensor_tensor(
                        o, Sst[:, ch - 1, 256 * hh:256 * hh + 256], decs[:, hh, ch - 1:ch], a, ALU.mult, ALU.add), tok, tdc)
            P.free(b, t_S)
    ob = {}
    for t, n, cc in XTILES:
        for pr in range(2):
            b = ob[t, pr] = P.take()
            for hh in (2 * pr, 2 * pr + 1):
                o = slice(256 * (hh % 2), 256 * (hh % 2) + 256)
                P.mm(ps[b][:, o], sc[:, t, 128 * hh:128 * hh + 128], vt[:, t, 256 * hh:256 * hh + 256], True, False, t_s, t_S)
                for u in range(2):
                    tok = P.mm(ps[b][64 * u:64 * u + 64, o], E3[:, hh, cc + 64 * u:cc + 64 * u + 64],
                               Sst[:, 2 * t + u, 256 * hh:256 * hh + 256], False, True)
            for hh in (2 * pr, 2 * pr + 1):
                V.do(lambda e, b=b, t=t, hh=hh: e.bn_stats(P.st[:, 4 * t + hh, 0, :], ps[b][:, 256 * (hh % 2):256 * (hh % 2) + 256]), tok)
                V.seq(lambda e, t=t, hh=hh: e.bn_aggr(mv8[:, 4 * t + hh, :], P.st[:, 4 * t + hh, 0:1, :]))
    V.seq(lambda e: e.tensor_scalar(P.rs[:, 0, 0:8], mv8[:, :, 1], LN_EPS, None, ALU.add))
    P.rsqrt(P.rs[:, 1, 0:8], P.rs[:, 0, 0:8], P.rtmp[:, 0:8])
    V.seq(lambda e: e.tensor_tensor(rt[:, 0, :], rt[:, 0, :], ngb[:, :], ALU.mult), t_rt, t_ngb)
    V.seq(lambda e: e.tensor_tensor(rt[:, 1, :], rt[:, 1, :], ngb[:, :], ALU.mult))
    on = vt
    t_vt2 = T_.last
    for t in range(2):
        for hh in range(4):
            b = ob[t, hh // 2]
            k = 4 * t + hh
            z = V.seq(lambda e, b=b, t=t, hh=hh, k=k: e.tensor_scalar(
                on[:, t, 256 * hh:256 * hh + 256], ps[b][:, 256 * (hh % 2):256 * (hh % 2) + 256],
                mv8[:, k, 0:1], P.rs[:, 1, k:k + 1], ALU.subtract, ALU.mult), t_vt2)
            if hh % 2:
                P.free(b, z)
        t_og = V.seq(lambda e, t=t: e.tensor_tensor(on[:, t, :], on[:, t, :], rt[:, t, :], ALU.mult))
    t_x = P.make_T(lambda t, k: on[:, t, 128 * k:128 * k + 128], XTILES, 8, xh, xl, t_og)

    def rows_out(key, tiles, tx, between=(list,) * 4):
        T_.wait(tx)
        acc = {(t, q): P.take() for t, _, _ in tiles for q in range(2)}
        for j in range(4):
            fs = between[j]()
            c = P.next((key, j))
            wh, wl = (c[s].rearrange("p (i n) -> p i n", i=2) for s in ("hi", "lo"))
            for i in range(2):
                k = 2 * j + i
                for t, n, cc in tiles:
                    for q in range(2):
                        tok = P.mm3(ps[acc[t, q]][:, :], xh[:, k, cc:cc + n], xl[:, k, cc:cc + n],
                                    wh[:, i, 512 * q:512 * q + 512], wl[:, i, 512 * q:512 * q + 512], k == 0, k == 7,
                                    mark=(i == 1 and t == tiles[-1][0] and q == 1))
            P.done(c, tok)
            for f in fs:
                f()
        return acc, tok

    acc, tok = rows_out("go", XTILES, t_x)
    t_ln = end_block(acc, XTILES, (1, 0), tok)
    P.dump("h2", h[:, 0:2, :], t_ln)
    t_x = P.make_T(src_h, QTILES, 8, xh, xl, t_ln)

    t_mod = ada["done"]

    def router(n, tw):
        T_.wait(tw, t_x)
        b = P.take()
        for t, _, cc in QTILES:
            for k in range(8):
                tok = P.mm3(ps[b][:, 32 * t:32 * t + n], xh[:, k, cc:cc + 128], xl[:, k, cc:cc + 128], rwh[:, k, 0:n], rwl[:, k, 0:n],
                            k == 0, k == 7)
        return b, ps[b][:, 0:64].rearrange("p (t n) -> p t n", t=2)[:, :, 0:n], tok

    def top2(lo, n, ready):
        w = gw[:, :, 48:56]
        for t in range(2):
            m8, L = gw[:, t, 40:48], gw[:, t, lo:lo + n]
            V.seq(lambda e, m8=m8, L=L: e.max(m8, L), ready)
            V.seq(lambda e, m8=m8, L=L, t=t: e.max_index(gi[:, t, :], m8, L))
        V.seq(lambda e: e.tensor_copy(w[:, :, 0:2], gi[:, :, 0:2]))
        td = V.seq(lambda e: e.tensor_tensor(w[:, :, 2:3], gw[:, :, 41:42], gw[:, :, 40:41], ALU.subtract))
        te = A.do(lambda e: e.activation(w[:, :, 3:4], w[:, :, 2:3], ACT.Exp), td)
        V.seq(lambda e: e.tensor_scalar(w[:, :, 4:5], w[:, :, 3:4], 1.0, None, ALU.add), te)
        V.seq(lambda e: e.reciprocal(w[:, :, 4:5], w[:, :, 4:5]))
        return w

    def top2_gates(n, w):
        io = cst[:, C_IO:C_IO + n]
        V.seq(lambda e: e.tensor_tensor(w[:, :, 5:6], w[:, :, 3:4], w[:, :, 4:5], ALU.mult))
        for t in range(2):
            V.do(lambda e, t=t: e.tensor_scalar(masks[:, t, 0:n], io, w[:, t, 0:1], None, ALU.is_equal), V.last)
            V.do(lambda e, t=t: e.tensor_scalar(gw[:, t, 16:16 + n], io, w[:, t, 1:2], None, ALU.is_equal))
        tm = V.seq(lambda e: e.tensor_tensor(masks[:, :, 0:n], masks[:, :, 0:n], gw[:, :, 16:16 + n], ALU.add))
        for t in range(2):
            V.do(lambda e, t=t: e.tensor_scalar(gates[:, t, 0:n], io, w[:, t, 0:1], w[:, t, 4:5], ALU.is_equal, ALU.mult), V.last)
            V.do(lambda e, t=t: e.tensor_scalar(gw[:, t, 0:n], io, w[:, t, 1:2], w[:, t, 5:6], ALU.is_equal, ALU.mult))
        tg = V.seq(lambda e: e.tensor_tensor(gates[:, :, 0:n], gates[:, :, 0:n], gw[:, :, 0:n], ALU.add))
        return tm, tg

    P.phase()
    every = [q.last for q in (T_, V, A)]
    bcast = lambda nm: d[nm].partition_broadcast(128)
    bias = P.rest("bias", [128, 4, 384])
    pf = P.rest("pf", [128, 2])
    mw = P.moe_tiles(3584)
    y = mw["y"]
    t_h = P.moe_parts(mw, lambda t: h[:, t, :], t_ln)
    b, lg8, tok = router(8, t_rw)
    tc = V.seq(lambda e: e.tensor_copy(gw[:, :, 0:8], lg8), tok)
    P.free(b, tc)
    t_m, t_g = top2_gates(8, top2(0, 8, tc))

    pi = P.ph("pi", [128, 2], I32)
    t_pi0 = P.load(G, pi[:, 0:1], d["positions_2"][0, 0:128].rearrange("(p a) -> p a", a=1), *every)
    t_pi = P.load(G, pi[:, 1:2], d["positions_2"][0, 128:256].rearrange("(p a) -> p a", a=1))
    yf = y.rearrange("p t n -> p (t n)")
    rel, stp, pkb = yf[:, 0:384], yf[:, 384:768], yf[:, 768:1024].bitcast(I32)
    t_pk = P.load(G, pkb, bcast("positions_2"))
    rb = P.ph("rb", [128, 128])
    dl = P.ph("dl", [128, 30, 4])
    i2 = lnt[:, 0:512].bitcast(I32).rearrange("p (a n) -> p a n", a=2)
    j2 = P.ph("j2", [128, 2, 2], I32)
    f2 = lnt[:, 512:1024].rearrange("p (a n) -> p a n", a=2)
    g2f = P.ph("g2f", [128, 2, 2])
    t_rb = P.load(G, rb[:, :], d["rel_bias_2"].rearrange("(a b) h -> a (b h)", a=1).partition_broadcast(128))

    def rel_bias():
        V.wait(t_pi0)
        V.seq(lambda e: e.tensor_copy(pf[:, :], pi[:, :]), t_pi)
        for dst, src, tk in ((i2, pkb, t_pk), (j2, pi, t_pi)):
            V.seq(lambda e, dst=dst, src=src: e.tensor_scalar(dst[:, 0, :], src[:, :], 12, None, ALU.arith_shift_right), tk)
            V.seq(lambda e, dst=dst, src=src: e.tensor_scalar(dst[:, 1, :], src[:, :], 4095, None, ALU.bitwise_and))
        V.seq(lambda e: e.tensor_copy(f2[:, :, :], i2[:, :, :]))
        V.seq(lambda e: e.tensor_copy(g2f[:, :, :], j2[:, :, :]))
        for t in range(2):
            n, o = (128, 0) if t == 0 else (256, 128)
            V.seq(lambda e, t=t, n=n: e.tensor_scalar(stp[:, 0:n], f2[:, 0, 0:n], g2f[:, 0, t:t + 1], 4096.0, ALU.subtract, ALU.mult))
            V.seq(lambda e, t=t, n=n, o=o: e.tensor_scalar(rel[:, o:o + n], f2[:, 1, 0:n], g2f[:, 1, t:t + 1], None, ALU.subtract))
            V.seq(lambda e, n=n, o=o: e.tensor_tensor(rel[:, o:o + n], rel[:, o:o + n], stp[:, 0:n], ALU.add))
        prev = 15
        for i, (th, bk) in enumerate(STEPS):
            V.do(lambda e, i=i, bk=bk, prev=prev: e.tensor_tensor(dl[:, i, :], rb[:, 4 * bk:4 * bk + 4], rb[:, 4 * prev:4 * prev + 4],
                                                                  ALU.subtract), t_rb)
            prev = bk
        t_dl = V.last
        for hh in range(4):
            G.seq(lambda e, hh=hh: e.tensor_scalar(bias[:, hh, :], cst[:, C_AM:C_AM + 384], rb[:, 60 + hh:61 + hh], None, ALU.add),
                  t_dl, t_rb)
            for i, (th, bk) in enumerate(STEPS):
                G.seq(lambda e, hh=hh, i=i, th=th: e.tensor_scalar(stp[:, :], rel[:, :], float(th), dl[:, i, hh:hh + 1],
                                                                   ALU.is_ge, ALU.mult))
                t_bias = G.seq(lambda e, hh=hh: e.tensor_tensor(bias[:, hh, :], bias[:, hh, :], stp[:, :], ALU.add))
        mw["y_free"] = t_bias
        P.ln_free = t_dl
        P.t_bias = t_bias

    t_y = P.moe("m1", 8, 3584, mw, masks, gates, (t_m, t_g, t_h), again["m1"], [(2, rel_bias)])
    t_bias = P.t_bias
    P.fence = len(P.chunks)
    P.dump("ff1", y[:, :, :], t_y)
    t_ln = P.layer_norm(QTILES, lambda t, q: y[:, t, 512 * q:512 * q + 512], (1, 1), t_y)
    P.dump("h3", h[:, 0:2, :], t_ln)

    P.phase()
    hn = P.rest("hn", [128, 2, 1024])
    rs = P.rs
    pj = P.ph("pj", [128, 2, 2208])
    sq = P.ph("sq", [128, 1536])
    qq = P.ph("qq", [128, 2, 768])
    kk = P.ph("kk", [128, 2, 768])
    cq = P.ph("cq", [128, 2, 5, 256], F32R)
    qk0 = P.ph("qk0", [128, 2, 4, 256])
    Sx0 = P.ph("Sx0", [128, 1536])
    ang = P.ph("ang", [128, 4, 2, 16])
    rot = P.ph("rot", [128, 8, 2, 16])
    gbr2 = P.ph("gbr2", [128, 320])
    lw = P.ph("lw", [128, 64])
    l2 = P.ph("l2", [128, 4])
    ones = P.ph("ones", [128, 128])
    dgs = [kk.rearrange("p t n -> p (t n)")[:, 512 * q:512 * q + 512].rearrange("p (a n) -> p a n", a=4) for q in range(2)]
    gc = P.ph("gc", [128, 2, 8])
    gqk = P.ph("gqk", [128, 4])
    r4 = P.ph("r4", [128, 4])
    rq = P.ph("rq", [128, 2, 2, 8])
    rk16 = P.ph("rk16", [128, 2, 8])
    pe2 = P.ph("pe2", [128, 2])
    ssum = P.ph("ssum", [128, 2, 2, 2, 4])
    every = [q.last for q in (T_, V, A)]
    t_sm = []
    for o, n, s in ((0, 32, d["mla_q_g_2"][:, 64:96]), (32, 32, d["mla_k_g_2"][:, 64:96]), (64, 64, d["lambda_q1_2"]),
                    (128, 64, d["lambda_k1_2"]), (192, 64, d["lambda_q2_2"]), (256, 64, d["lambda_k2_2"])):
        t_sm.append(P.load(G, gbr2[:, o:o + n], s.partition_broadcast(128), *every))

    def mean_sq(t_in):
        for t in range(2):
            z = A.do(lambda e, t=t: e.activation(hn[:, t, :], h[:, t, :], ACT.Square, scale=1.0 / 32,
                                                 accum_out=rs[:, 0, t:t + 1]), t_in)
        V.seq(lambda e: e.tensor_scalar(rs[:, 0, 0:2], rs[:, 0, 0:2], RMS_EPS, None, ALU.add), z)
        z = P.rsqrt(rs[:, 1, 0:2], rs[:, 0, 0:2], P.rtmp[:, 0:2])
        ta = A.do(lambda e: e.activation(hn[:, 0, :], h[:, 0, :], ACT.Copy, scale=rs[:, 1, 0:1]), z)
        tv = V.seq(lambda e: e.tensor_scalar(hn[:, 1, :], h[:, 1, :], rs[:, 1, 1:2], None, ALU.mult))
        return ta, tv

    split_rw = router_load([(d["w_rg_2"][0], 4), (d["w_re_2"][0], 16)], *every)
    V.seq(lambda e: e.scalar_tensor_tensor(gc[:, 0, :], modc[:, 8:16], 1.0, colA[:, 112:120], ALU.add, ALU.mult), t_mod)
    t_gc = V.seq(lambda e: e.scalar_tensor_tensor(gc[:, 1, :], modc[:, 32:40], 1.0, colB[:, 0:8], ALU.add, ALU.mult))
    t_hn = mean_sq(t_ln)
    src_n = lambda t, k: hn[:, t, 128 * k:128 * k + 128]
    tmpT = sq.rearrange("p (a n) -> p a n", a=2)
    t_x = P.make_T(src_n, QTILES, 8, xh, xl, *t_hn, gain=lambda k: gc[:, 0, k:k + 1], shift=lambda k: modc[:, k:k + 1], tmp=tmpT)

    T_.wait(t_x)

    def ev_pj(t, n, j, pt, tok):
        return A.do(lambda e: e.activation(pj[:, t, 256 * j:256 * j + (256 if j < 8 else 160)], pt, ACT.Copy), tok)

    for j in range(4):
        tokm("wi", j, QTILES, ev_pj)
        if j == 2:
            t_lat = A.last
    for i, (o, n) in enumerate(((0, 384), (384, 256))):
        for t in range(2):
            z = A.do(lambda e, o=o, n=n, t=t, i=i: e.activation(Sx0[:, 0:n], pj[:, t, o:o + n], ACT.Square, scale=n ** -0.5,
                                                                 accum_out=r4[:, 2 * i + t:2 * i + t + 1]), z if t or i else t_lat)
    for t in range(2):
        z = A.do(lambda e, t=t: e.activation(Sx0[:, 0:32], pj[:, t, 640:672], ACT.Square, accum_out=pe2[:, t:t + 1]), z)
    V.seq(lambda e: e.tensor_scalar(rs[:, 0, 0:4], r4[:, :], RMS_EPS, None, ALU.add), z)
    t_r4 = P.rsqrt(r4[:, :], rs[:, 0, 0:4], P.rtmp[:, 0:4])
    t_cq = P.make_T(lambda t, k: pj[:, t, 128 * k:128 * k + 128], QTILES, 5, cq[:, 0], cq[:, 1], t_lat,
                    gain=lambda k: colB[:, 8 + k:9 + k])
    for t in range(2):
        V.seq(lambda e, t=t: e.tensor_scalar(ang[:, 0, t, :], cst[:, C_IF:C_IF + 16], pf[:, t:t + 1], None, ALU.mult))
    a0, a1, a2, a3 = (ang[:, i, :, :] for i in range(4))
    MAGIC = 12582912.0
    V.seq(lambda e: e.tensor_scalar(a1, a0, 1.0 / (2 * math.pi), MAGIC, ALU.mult, ALU.add))
    V.seq(lambda e: e.tensor_scalar(a1, a1, MAGIC, None, ALU.subtract))
    c1 = 6.28125
    c2 = float((np.array(2 * math.pi - c1, np.float32).view(np.uint32) & np.uint32(0xFFFFF000)).view(np.float32))
    c3 = 2 * math.pi - c1 - c2
    for cc in (c1, c2, c3):
        V.seq(lambda e, cc=cc: e.scalar_tensor_tensor(a0, a1, -cc, a0, ALU.mult, ALU.add))
    PI = 3.1415925
    V.seq(lambda e: e.tensor_scalar(a0, a0, PI, -PI, ALU.min, ALU.max))
    V.seq(lambda e: e.tensor_scalar(a1, a0, math.pi / 2, -2 * math.pi, ALU.is_gt, ALU.mult))
    V.seq(lambda e: e.scalar_tensor_tensor(a1, a0, math.pi / 2, a1, ALU.add, ALU.add))
    t_an = V.seq(lambda e: e.tensor_scalar(a1, a1, PI, -PI, ALU.min, ALU.max))
    A.do(lambda e: e.activation(a2, a0, ACT.Sin), t_an)
    t_cs = A.do(lambda e: e.activation(a3, a1, ACT.Sin))
    V.wait(t_cs, *t_sm)
    for m in range(2):
        g1_, g2_ = (gbr2[:, 32 * m + 16 * i:32 * m + 16 * i + 16].unsqueeze(1).to_broadcast([128, 2, 16]) for i in range(2))
        for i, (x, f) in enumerate(((g1_, a3), (g2_, a2), (g2_, a3), (g1_, a2))):
            V.do(lambda e, m=m, i=i, x=x, f=f: e.tensor_tensor(rot[:, 4 * m + i, :, :], x, f, ALU.mult))

    for i in range(2):
        V.seq(lambda e, i=i: e.tensor_tensor(lw[:, :], gbr2[:, 64 + 128 * i:128 + 128 * i], gbr2[:, 128 + 128 * i:192 + 128 * i], ALU.mult))
        tl = V.seq(lambda e, i=i: e.tensor_reduce(l2[:, i:i + 1], lw[:, :], AX.X, ALU.add))
    tl = A.do(lambda e: e.activation(l2[:, 0:2], l2[:, 0:2], ACT.Exp), tl)
    V.seq(lambda e: e.memset(gqk[:, 0:1], 1.0))
    V.seq(lambda e: e.tensor_tensor(gqk[0:64, 0:1], colB[0:64, 15:16], colB[0:64, 16:17], ALU.mult))
    V.seq(lambda e: e.tensor_tensor(gqk[:, 1:2], colB[:, 13:14], colB[:, 14:15], ALU.mult))
    V.seq(lambda e: e.tensor_scalar(gqk[:, 2:3], colB[:, 17:18], 1.0 - LAMBDA_INIT, None, ALU.mult))
    V.seq(lambda e: e.memset(ones[:, :], 1.0))
    V.seq(lambda e: e.tensor_tensor(l2[:, 2:3], l2[:, 1:2], l2[:, 0:1], ALU.subtract), tl)
    t_misc = V.seq(lambda e: e.tensor_scalar(l2[:, 2:3], l2[:, 2:3], -LAMBDA_INIT, None, ALU.add))
    nlam = l2[:, 2:3]

    tokm("wi", 4, QTILES, ev_pj)
    T_.wait(t_cq)
    vv = pj[:, :, 0:512]
    k4 = [kk[:, t, :].rearrange("p (h n) -> p h n", n=96) for t in range(2)]
    v4 = [vv[:, t, :].rearrange("p (h n) -> p h n", n=64) for t in range(2)]
    for j in range(2):
        c = P.next(("uq", j))
        wh, wl = (c[s].rearrange("p (k n) -> p k n", k=3) for s in ("hi", "lo"))
        for t, _, cc in QTILES:
            b = P.take()
            for k in range(3):
                tok = P.mm3(ps[b][:, 0:384], cq[:, 0, k, cc:cc + 128], cq[:, 1, k, cc:cc + 128], wh[:, k, :], wl[:, k, :], k == 0, k == 2)
            t_qq = A.do(lambda e, b=b, t=t, j=j: e.activation(qq[:, t, 384 * j:384 * j + 384], ps[b][:, 0:384], ACT.Copy,
                                                              scale=r4[:, t:t + 1]), tok, t_r4)
            P.free(b, t_qq)
        P.done(c, tok)
    c = P.next("ukv")
    wh, wl = (c[s].rearrange("p (k n) -> p k n", k=2) for s in ("hi", "lo"))
    for t, _, cc in QTILES:
        for q in range(2):
            b = P.take()
            for k in range(2):
                tok = P.mm3(ps[b][:, :], cq[:, 0, 3 + k, cc:cc + 128], cq[:, 1, 3 + k, cc:cc + 128],
                            wh[:, k, 512 * q:512 * q + 512], wl[:, k, 512 * q:512 * q + 512], k == 0, k == 1)
            pv = ps[b][:, :].rearrange("p (h n) -> p h n", n=128)
            t_kv = A.do(lambda e, pv=pv, t=t, q=q: e.activation(k4[t][:, 4 * q:4 * q + 4, 0:64], pv[:, :, 0:64], ACT.Copy,
                                                                scale=r4[:, 2 + t:3 + t]), tok)
            t_vv = V.do(lambda e, pv=pv, t=t, q=q: e.tensor_scalar(v4[t][:, 4 * q:4 * q + 4, :], pv[:, :, 64:128],
                                                                   r4[:, 2 + t:3 + t], None, ALU.mult), t_kv)
            P.free(b, t_vv)
    t_ukv = tok
    P.done(c, tok)

    def head_rms(src, n, m, extra, dst, *toks):
        s = sq[:, 0:16 * m].rearrange("p (t g n) -> p t g n", t=2, g=8)
        z = A.do(lambda e: e.activation(s, src, ACT.Square), V.last, *toks)
        r0 = rs[:, 0, 0:16].rearrange("p (t g) -> p t g", t=2)
        V.seq(lambda e: e.tensor_reduce(r0, s, AX.X, ALU.add), z)
        if extra is not None:
            V.seq(lambda e: e.tensor_tensor(r0, r0, extra.unsqueeze(2).to_broadcast([128, 2, 8]), ALU.add))
        V.seq(lambda e: e.tensor_scalar(rs[:, 0, 0:16], rs[:, 0, 0:16], 1.0 / n, RMS_EPS, ALU.mult, ALU.add))
        return P.rsqrt(dst.rearrange("p t g -> p (t g)"), rs[:, 0, 0:16], P.rtmp[:, 0:16])

    q5 = qq.rearrange("p t (h n) -> p t h n", n=96)
    k5 = kk.rearrange("p t (h n) -> p t h n", n=96)

    def rotate(x1, x2, o1, o2_, m, shape, s):
        f = [rot[:, 4 * m + i, :, :] for i in range(4)]
        if len(shape) == 4:
            f = [a.unsqueeze(2).to_broadcast(shape) for a in f]
        V.do(lambda e: e.tensor_tensor(s[0], x1, f[0], ALU.mult), V.last)
        V.do(lambda e: e.tensor_tensor(s[1], x2, f[1], ALU.mult))
        V.do(lambda e: e.tensor_tensor(s[2], x2, f[2], ALU.mult))
        V.do(lambda e: e.tensor_tensor(s[3], x1, f[3], ALU.mult))
        z = V.seq(lambda e: e.tensor_tensor(o1, s[0], s[1], ALU.subtract))
        return V.do(lambda e: e.tensor_tensor(o2_, s[2], s[3], ALU.add))

    s4 = [sq[:, 256 * i:256 * i + 256].rearrange("p (t h n) -> p t h n", t=2, h=8) for i in range(4)]
    kpe = Sx0[:, 0:64].rearrange("p (t n) -> p t n", t=2)
    head_rms(q5, 96, 96, None, rq[:, 0], t_qq)
    V.seq(lambda e: e.tensor_scalar(rq[:, 0], rq[:, 0], 96.0 ** -0.5, None, ALU.mult))
    t_q = rotate(q5[:, :, :, 64:80], q5[:, :, :, 80:96], q5[:, :, :, 64:80], q5[:, :, :, 80:96], 0, [128, 2, 8, 16], s4)
    pr = pj[:, :, 640:672]
    sk = [Sx0[:, 64 + 32 * i:96 + 32 * i].rearrange("p (t n) -> p t n", t=2) for i in range(4)]
    rotate(pr[:, :, 0:16], pr[:, :, 16:32], kpe[:, :, 0:16], kpe[:, :, 16:32], 1, [128, 2, 16], sk)
    z = head_rms(k5[:, :, :, 0:64], 96, 64, pe2[:, :], rk16, t_kv)
    V.seq(lambda e: e.tensor_tensor(k5[:, :, :, 0:64], k5[:, :, :, 0:64], rk16[:, :, :].unsqueeze(3).to_broadcast([128, 2, 8, 64]), ALU.mult))
    for t in range(2):
        t_k = V.seq(lambda e, t=t: e.tensor_tensor(
            k4[t][:, :, 64:96], kpe[:, t, :].unsqueeze(1).to_broadcast([128, 8, 32]),
            rk16[:, t, :].unsqueeze(2).to_broadcast([128, 8, 32]), ALU.mult))

    for j in range(5, 9):
        tokm("wi", j, QTILES, ev_pj)
        if j == 6:
            t_dqk = A.last
    t_pj = A.last
    P.dump("proj", pj[:, :, :], t_pj)

    o2 = hn
    dq, dk, dv = pj[:, :, 672:1184], pj[:, :, 1184:1696], pj[:, :, 1696:2208]
    d5 = [a.rearrange("p t (h n) -> p t h n", n=64) for a in (dq, dk)]
    QK = [qk0, lnt[:, :].rearrange("p (a u n) -> p a u n", a=2, u=4)]
    SX = [a.rearrange("p (u n) -> p u n", u=4) for a in (Sx0[:, :], qq.rearrange("p t n -> p (t n)"))]
    PT = [a.rearrange("p (u m n) -> p u m n", u=4, m=3) for a in (sq[:, :], kk.rearrange("p t n -> p (t n)"))]
    am = cst[:, C_AM:C_AM + 384]
    st_k, st_s, st_p, st_e = {}, {}, {}, {}
    flip = [0]

    def copy(dst, src, *toks):
        flip[0] += 1
        if flip[0] % 2:
            return A.do(lambda e: e.activation(dst, src, ACT.Copy), *toks)
        return V.do(lambda e: e.tensor_copy(dst, src), *toks)

    def heads(B, ready):
        i = B % 2
        toks = []
        n, w = (96, 96) if B < 2 else (128, 128)
        for u in range(4 if B < 2 else 2):
            hh = 4 * B + u if B < 2 else 2 * (B - 2) + u
            qs, ks = (qq, kk) if B < 2 else (dq, dk)
            b = P.take()
            for t in range(2):
                T_.do(lambda e, b=b, t=t, hh=hh: e.transpose(ps[b][0:n, 128 * t:128 * t + 128], qs[:, t, w * hh:w * hh + w],
                                                            cst[:, C_ID:C_ID + 128]), *ready)
                tok = T_.do(lambda e, b=b, t=t, hh=hh: e.transpose(ps[b][0:n, 256 + 128 * t:384 + 128 * t],
                                                                  ks[:, t, w * hh:w * hh + w], cst[:, C_ID:C_ID + 128]))
            g = gqk[0:n, 0:1] if B < 2 else gqk[0:n, 1:2]
            ta = A.do(lambda e, b=b, u=u: e.activation(QK[i][0:n, 0, u, :], ps[b][0:n, 0:256], ACT.Copy, scale=g), tok, t_misc,
                      st_s.get(B - 2))
            tv = V.do(lambda e, b=b, u=u: e.tensor_copy(QK[i][0:n, 1, u, :], ps[b][0:n, 256:512]), ta, st_s.get(B - 2))
            P.free(b, tv)
            toks += [ta, tv]
        st_k[B] = toks

    def scores(B):
        i = B % 2
        x = SX[i]
        T_.wait(*st_k[B])
        for u in range(4):
            b = P.take()
            p0, n, v = (0, 96, u) if B < 2 else (64 * (u % 2), 64, u // 2)
            hh = 4 * B + u if B < 2 else 4 * (B - 2) + u
            qT, kT = (QK[i][p0:p0 + n, a, v, :] for a in range(2))
            P.mm(ps[b][:, 0:128], qT[:, 0:128], kT[:, 0:128], True, True)
            tok = P.mm(ps[b][:, 128:384], qT[:, 128:256], kT, True, True)
            bm = am if B < 2 else bias[:, hh // 2, :]
            for t, (a, z) in enumerate(((0, 128), (128, 384))):
                ts = V.do(lambda e, b=b, u=u, a=a, z=z, t=t, bm=bm, hh=hh: e.scalar_tensor_tensor(
                    x[:, u, a:z], ps[b][:, a:z], rq[:, B // 2, t, hh:hh + 1], bm[:, a:z], ALU.mult, ALU.add),
                    tok, t_bias, st_p.get(B - 2))
            P.free(b, ts)
        st_s[B] = tok
        S4 = ssum[:, i]
        for t, (a, z) in enumerate(((0, 128), (128, 384))):
            tm = V.do(lambda e, t=t, a=a, z=z: e.tensor_reduce(S4[:, t, 0, :], x[:, :, a:z], AX.X, ALU.max, negate=True), V.last,
                      st_e.get(B - 2))
        te = None
        for u in range(4):
            for t, (a, z) in enumerate(((0, 128), (128, 384))):
                te = A.do(lambda e, u=u, t=t, a=a, z=z: e.activation(x[:, u, a:z], x[:, u, a:z], ACT.Exp, bias=S4[:, t, 0, u:u + 1],
                                                                     accum_out=S4[:, t, 1, u:u + 1]), tm)
            st_e[B, u] = te

    def probs(B):
        i = B % 2
        st_p[B, "z"] = []
        for u in range(4):
            b = P.take()
            for m in range(3):
                tok = T_.do(lambda e, b=b, m=m, u=u: e.transpose(ps[b][:, 128 * m:128 * m + 128], SX[i][:, u, 128 * m:128 * m + 128],
                                                                 cst[:, C_ID:C_ID + 128]), st_e[B, u])
            z = copy(PT[i][:, u].rearrange("p m q -> p (m q)"), ps[b][:, 0:384], tok, st_p.get((B - 2, "v")), t_norm)
            P.free(b, z)
            st_p[B, "z"].append(z)
        st_p[B] = tok

    def values(B):
        i = B % 2
        S4 = ssum[:, i]
        bk = [P.take(), P.take()]
        e_ = 64 if B < 2 else 128
        T_.wait(*st_p[B, "z"])
        for u in range(4):
            o = slice(e_ * u, e_ * u + e_)
            if B < 2:
                vs = [v4[t][:, 4 * B + u, :] for t in range(2)]
            else:
                hh = 2 * (B - 2) + u // 2
                vs = [dv[:, t, 128 * hh:128 * hh + 128] for t in range(2)]
            P.mm(ps[bk[0]][:, o], PT[i][:, u, 0, :], vs[0], True, True, t_vv, t_pj)
            P.mm(ps[bk[1]][:, o], PT[i][:, u, 1, :], vs[0], True, False)
            tok = P.mm(ps[bk[1]][:, o], PT[i][:, u, 2, :], vs[1], False, True)
        st_p[B, "v"] = tok
        V.seq(lambda e: e.reciprocal(S4[:, :, 1, :], S4[:, :, 1, :]), st_e[B, 3])
        if B >= 2:
            for t in range(2):
                w = S4[:, t, 1, :].rearrange("p (h m) -> p h m", m=2)[:, :, 1]
                V.seq(lambda e, w=w: e.tensor_scalar(w, w, nlam, None, ALU.mult))
        for t in range(2):
            p = ps[bk[t]][:, 0:4 * e_].rearrange("p (u n) -> p u n", u=4)
            r = S4[:, t, 1, :].unsqueeze(2).to_broadcast([128, 4, e_])
            if B < 2:
                z = V.seq(lambda e, t=t, p=p, r=r: e.tensor_tensor(
                    o2[:, t, 256 * B:256 * B + 256].rearrange("p (u n) -> p u n", u=4), p, r, ALU.mult), tok)
            else:
                f = dq[:, t, :].rearrange("p (u n) -> p u n", u=4)
                z = V.seq(lambda e, p=p, r=r, f=f: e.tensor_tensor(f, p, r, ALU.mult), tok)
                f = dq[:, t, :].rearrange("p (h m n) -> p h m n", m=2, n=128)
                o = o2[:, t, 256 * B:256 * B + 256].rearrange("p (h n) -> p h n", n=128)
                z2 = V.seq(lambda e, f=f, o=o: e.tensor_tensor(o, f[:, :, 0, :], f[:, :, 1, :], ALU.add))
            P.free(bk[t], z)
            st_e[B] = V.last
        return V.last

    def spread_half(q, dst, cols, one, dg, *toks):
        for i in range(4):
            z = V.do(lambda e, i=i: e.tensor_scalar(dg[:, i, :], cst[:, C_ID:C_ID + 128], cols[:, 4 * q + i:4 * q + i + 1],
                                                    None, ALU.mult), *toks)

        def rest():
            b = P.take()
            for i in range(4):
                tok = P.mm(ps[b][:, 128 * i:128 * i + 128], one[:, :], dg[:, i, :], True, True, z)
            t = A.do(lambda e, b=b: e.activation(dst[:, 512 * q:512 * q + 512], ps[b][:, :], ACT.Copy), tok)
            P.free(b, t)
            return t
        return rest

    g1t, gain2, shift2 = h[:, 2, :], lnt[:, 0:1024], lnt[:, 1024:2048]
    heads(0, (t_q, t_k))
    t_rw2 = split_rw()
    t_norm = None
    scores(0)
    heads(1, (t_q, t_k))
    head_rms(d5[0], 64, 64, None, rq[:, 1], t_dqk)
    V.seq(lambda e: e.tensor_scalar(rq[:, 1], rq[:, 1], 0.125, None, ALU.mult))
    head_rms(d5[1], 64, 64, None, rk16, t_dqk)
    t_dk = t_norm = V.seq(lambda e: e.tensor_tensor(d5[1], d5[1], rk16[:, :, :].unsqueeze(3).to_broadcast([128, 2, 8, 64]), ALU.mult))
    scores(1)
    probs(0)
    values(0)
    heads(2, (t_dk, t_dqk))
    scores(2)
    probs(1)
    t_omla = values(1)
    heads(3, (t_dk, t_dqk))
    scores(3)
    probs(2)
    values(2)
    probs(3)
    values(3)
    P.dump("omla", o2[:, :, 0:512], t_omla)
    od = o2[:, :, 512:1024].rearrange("p t (h n) -> p t h n", n=128)
    od2 = dk.rearrange("p t (h n) -> p t h n", n=128)
    z = A.do(lambda e: e.activation(od2, od, ACT.Square), V.last)
    r0 = rs[:, 0, 0:8].rearrange("p (t g) -> p t g", t=2)
    V.seq(lambda e: e.tensor_reduce(r0, od2, AX.X, ALU.add), z)
    V.seq(lambda e: e.tensor_scalar(rs[:, 0, 0:8], rs[:, 0, 0:8], 1.0 / 128, RMS_EPS, ALU.mult, ALU.add))
    P.rsqrt(rs[:, 1, 0:8], rs[:, 0, 0:8], P.rtmp[:, 0:8])
    r1 = rs[:, 1, 0:8].rearrange("p (t g) -> p t g", t=2)
    t_o = V.seq(lambda e: e.tensor_tensor(od, od, r1.unsqueeze(3).to_broadcast([128, 2, 4, 128]), ALU.mult))
    t_x = P.make_T(lambda t, k: o2[:, t, 128 * k:128 * k + 128], QTILES, 8, xh, xl, t_o,
                   gain=lambda k: gqk[:, 2:3] if k >= 4 else None)
    between = [lambda x=x, t=t: [spread_half(q, x[0], x[1], ones, dgs[q], t, T_.last) for q in range(2)]
               for x, t in (((g1t, modc[:, 16:24]), t_ln), ((gain2, gc[:, 1, :]), None), ((shift2, modc[:, 24:32]), None))]
    acc, tok = rows_out("wo", QTILES, t_x, between + [list])
    t_g1 = t_sp2 = A.last
    for (t, q), b in acc.items():
        a = slice(512 * q, 512 * q + 512)
        z = V.do(lambda e, t=t, a=a, b=b: e.tensor_tensor(pj[:, t, a], ps[b][:, :], g1t[:, a], ALU.mult), tok, t_g1)
        P.free(b, z)
        t_h = V.seq(lambda e, t=t, a=a: e.tensor_tensor(h[:, t, a], h[:, t, a], pj[:, t, a], ALU.add))
    P.dump("x1", h[:, 0:2, :], t_h)
    t_hn = mean_sq(t_h)
    t_x = P.make_T(src_n, QTILES, 8, xh, xl, *t_hn, gain=lambda k: gc[:, 1, k:k + 1], shift=lambda k: modc[:, 24 + k:25 + k], tmp=tmpT)
    for t in range(2):
        V.seq(lambda e, t=t: e.tensor_tensor(hn[:, t, :], hn[:, t, :], gain2, ALU.mult), T_.last, t_sp2)
        t_hn = V.seq(lambda e, t=t: e.tensor_tensor(hn[:, t, :], hn[:, t, :], shift2, ALU.add))
    P.dump("hh2", hn[:, :, :], t_hn)

    P.phase()
    mw = P.moe_tiles(512)
    y = mw["y"]
    br = P.ph("br", [128, 20])
    g2t = P.ph("g2t", [128, 1024])
    big = P.ph("big", [128, 2, 24])
    gm = P.ph("gm", [128, 2, 16], I32)
    t_br = [P.load(G, br[:, 0:4], bcast("b_rg_2"), *[q.last for q in (T_, V, A)]), P.load(G, br[:, 4:20], bcast("b_re_2"))]
    V.seq(lambda e: e.memset(big[:, :, :], -3.0e38))
    t_h = P.moe_parts(mw, lambda t: hn[:, t, :], t_hn)
    b, lg20, tok = router(20, t_rw2)
    gl, w = gw[:, :, 0:4], gw[:, :, 48:64]
    z = V.seq(lambda e: e.tensor_tensor(gw[:, :, 0:20], lg20, br[:, :].unsqueeze(1).to_broadcast([128, 2, 20]), ALU.add), tok, *t_br)
    P.free(b, z)
    V.seq(lambda e: e.tensor_copy(big[:, :, 16:20], gl))
    for t in range(2):
        V.seq(lambda e, t=t: e.max(gw[:, t, 40:48], big[:, t, 16:24]))
        V.seq(lambda e, t=t: e.max_index(gi[:, t, :], gw[:, t, 40:48], big[:, t, 16:24]))
    V.seq(lambda e: e.tensor_scalar(w[:, :, 9:10], gw[:, :, 40:41], -1.0, None, ALU.mult))
    z = V.seq(lambda e: e.tensor_copy(w[:, :, 8:9], gi[:, :, 0:1]))
    for t in range(2):
        ta = A.do(lambda e, t=t: e.activation(w[:, t, 10:14], gl[:, t], ACT.Exp, bias=w[:, t, 9:10], accum_out=w[:, t, 14:15]), z)
    io = cst[:, C_IO:C_IO + 4].unsqueeze(2).to_broadcast([128, 4, 4])
    for t in range(2):
        V.seq(lambda e, t=t: e.tensor_scalar(gm[:, t, :].rearrange("p (g n) -> p g n", n=4), io, w[:, t, 8:9], None, ALU.is_equal))
        V.seq(lambda e, t=t: e.copy_predicated(big[:, t, 0:16], gm[:, t, :], gw[:, t, 4:20]))
    z = V.seq(lambda e: e.tensor_copy(gw[:, :, 20:36], big[:, :, 0:16]))
    V.seq(lambda e: e.reciprocal(w[:, :, 15:16], w[:, :, 14:15]), ta)
    top2(20, 16, z)
    V.seq(lambda e: e.tensor_tensor(w[:, :, 4:5], w[:, :, 4:5], w[:, :, 15:16], ALU.mult))
    t_m, t_g = top2_gates(16, w)

    def last_gate():
        fs = [spread_half(q, g2t, modc[:, 40:48], mw["one"], y[:, 0, 512 * q:512 * q + 512].rearrange("p (a n) -> p a n", a=4))
              for q in range(2)]
        P.t_g2 = [f() for f in fs][-1]
        mw["y_free"] = P.t_g2

    t_y = P.moe("m2", 16, 512, mw, masks, gates, (t_m, t_g, t_h), again["m2"], [(20, last_gate)])
    P.dump("y2", y[:, :, :], t_y)
    for t in range(2):
        V.seq(lambda e, t=t: e.tensor_tensor(y[:, t, :], y[:, t, :], g2t[:, :], ALU.mult), P.t_g2)
        z = V.seq(lambda e, t=t: e.tensor_tensor(h[:, t, :], h[:, t, :], y[:, t, :], ALU.add))
        P.pending_out.append(P.load(S, out[0, 128 * t:128 * t + 128, :], h[:, t, :], z))
    S.wait(*P.loads)
    P.phase_ctx.close()
    assert P.at == len(P.chunks)

    with P.ctx:
        block = P.ctx.enter_context(nc.Block())

        @block.sync
        def _(eng):
            S.emit(eng)

        @block.tensor
        def _(eng):
            T_.emit(eng)

        @block.vector
        def _(eng):
            V.emit(eng)

        @block.scalar
        def _(eng):
            A.emit(eng)

        @block.gpsimd
        def _(eng):
            G.emit(eng)


NAMES = ["x", "meta_tokens", "ln_gain", "ln_bias", "rg_w_in", "rg_conv_w", "rg_conv_b", "rg_w_gates", "rg_b_gates",
         "rg_lambda", "rg_w_out", "gla_w_in", "gla_w_gate_up", "gla_b_gate", "gla_norm_g", "gla_w_out", "ffn_w_in",
         "ffn_w_out", "moe_router", "moe_w_in", "moe_w_out", "c_2", "positions_2", "rel_bias_2", "w_ada_2", "b_ada_2",
         "norm1_g_2", "w_in_2", "mla_cq_g_2", "w_uq_2", "mla_ckv_g_2", "w_ukv_2", "mla_q_g_2", "mla_k_g_2",
         "diff_q_g_2", "diff_k_g_2", "lambda_q1_2", "lambda_k1_2", "lambda_q2_2", "lambda_k2_2", "diff_subln_g_2",
         "w_o_2", "norm2_g_2", "w_rg_2", "b_rg_2", "w_re_2", "b_re_2", "w_gate_2", "w_up_2", "w_down_2"]


def program(nc, inputs, dumps=None):
    arrays, d = {}, {}
    for name in NAMES:
        arrays["in_" + name] = np.ascontiguousarray(inputs[name])
    arrays["in_consts"] = const_table()
    for name in NAMES + ["consts"]:
        a = arrays["in_" + name]
        d[name] = nc.dram_tensor("in_" + name, a.shape, mybir.dt.from_np(a.dtype), kind="ExternalInput").ap()
    out = nc.dram_tensor("out_0", (1, 256, 1024), F32, kind="ExternalOutput").ap()
    build(nc, d, out, dumps)
    return arrays


def kernel(**inputs):
    import concourse.bacc as bacc
    from concourse.bass_utils import run_bass_kernel_spmd as run

    nc = bacc.Bacc("TRN2", target_bir_lowering=False, num_devices=1)
    arrays = program(nc, inputs)
    r = run(nc, [arrays], core_ids=[0])
    return r.results[0]["out_0"]
```
